# Optimizing a Trainium2 kernel written in Bass

```python
import math
import jax, jax.numpy as jnp
from jax import lax
import numpy as np

D_MODEL = 1024
BATCH = 1
SEQ = 1024
DEPTH = 1
DEC_BATCH = 8
DEC_SEQ = 4
PAST_LEN = 4096
PAGE_SIZE = 128

HEAD_DIM = 64
A_HEADS = 4
A_QK = 2 * HEAD_DIM
A_VDIM = 2 * HEAD_DIM
A_WIDTH = A_HEADS * A_VDIM
B_HEADS = 8
B_WIDTH = B_HEADS * HEAD_DIM
MIX_WIDTH = A_WIDTH + B_WIDTH
DILATIONS = ((128, 1), (512, 4), (2048, 16))
B_WINDOW = 2048
COL_SPLITS = (A_HEADS * A_QK, A_HEADS * A_QK, A_WIDTH, B_WIDTH, B_WIDTH, B_WIDTH)
IN_COLS = 2 * A_HEADS * A_QK + A_WIDTH + 3 * B_WIDTH
Q_BLOCK = 128
PEER_HEADS = 8
N_KEYS = 128
N_EXPERTS = N_KEYS * N_KEYS
PEER_TOPK = 16
D_KEY = 128
PEER_BLOCK = 128
RMS_EPS = 1e-6
NEG_INF = -1e30

kernel_name = 'hymba_diffattn_dilated_peer_step'

def rms_norm(x, g):
    xf = x.astype(jnp.float32)
    xf = xf * lax.rsqrt(jnp.mean(jnp.square(xf), axis=-1, keepdims=True) + RMS_EPS)
    return (xf * g.astype(jnp.float32)).astype(x.dtype)

def alibi_slopes(n):
    return jnp.asarray(2.0 ** (-8.0 * np.arange(1, n + 1) / n), dtype=jnp.float32)

def softmax_stats(s):
    m = jnp.max(s, axis=-1, keepdims=True)
    e = jnp.exp(s - m)
    den = jnp.sum(e, axis=-1, keepdims=True)
    return e / den, (m + jnp.log(den))[..., 0]

def project(x, norm_g, w_in, qn_a, kn_a, qn_b, kn_b):
    B, T, _ = x.shape
    h = jnp.einsum('btd,dc->btc', rms_norm(x, norm_g), w_in)
    offs = [sum(COL_SPLITS[:i + 1]) for i in range(len(COL_SPLITS) - 1)]
    qa, ka, va, qb, kb, vb = jnp.split(h, offs, axis=-1)
    qa = rms_norm(qa.reshape(B, T, A_HEADS, 2, HEAD_DIM), qn_a)
    ka = rms_norm(ka.reshape(B, T, A_HEADS, 2, HEAD_DIM), kn_a).reshape(B, T, A_HEADS, A_QK)
    va = va.reshape(B, T, A_HEADS, A_VDIM)
    qb = rms_norm(qb.reshape(B, T, B_HEADS, HEAD_DIM), qn_b)
    kb = rms_norm(kb.reshape(B, T, B_HEADS, HEAD_DIM), kn_b)
    vb = vb.reshape(B, T, B_HEADS, HEAD_DIM)
    return qa, ka, va, qb, kb, vb

def diff_scores(q, k, dist, mask):
    s = jnp.einsum('bqhmd,bkhmd->bmhqk', q, k, preferred_element_type=jnp.float32) * (HEAD_DIM ** -0.5)
    s = s - alibi_slopes(A_HEADS)[:, None, None] * dist
    if mask is not None:
        s = jnp.where(mask, s, NEG_INF)
    return s

def diff_weights(s, lam):
    p = jax.nn.softmax(s, axis=-1)
    return p[:, 0] - lam * p[:, 1]

def diff_attn_prompt(qa, ka, va, lam):
    B, T = qa.shape[:2]
    nb = T // Q_BLOCK
    k = ka.reshape(B, T, A_HEADS, 2, HEAD_DIM)
    qblk = jnp.moveaxis(qa.reshape(B, nb, Q_BLOCK, A_HEADS, 2, HEAD_DIM), 1, 0)
    kpos = jnp.arange(T)

    def block(args):
        qi, i = args
        d = (i * Q_BLOCK + jnp.arange(Q_BLOCK))[:, None] - kpos[None, :]
        w = diff_weights(diff_scores(qi, k, d.astype(jnp.float32), d >= 0), lam)
        return jnp.einsum('bhqk,bkhe->bqhe', w.astype(va.dtype), va)

    o = lax.map(block, (qblk, jnp.arange(nb)))
    return jnp.moveaxis(o, 0, 1).reshape(B, T, A_HEADS, A_VDIM)

def diff_attn_sample(qa, ka, va, cache_k, cache_v, page_table, lam):
    DB, Tq = qa.shape[:2]
    kp = cache_k[page_table]
    P = kp.shape[1] * kp.shape[2]
    kp = kp.reshape(DB, P, A_HEADS, 2, HEAD_DIM)
    vp = cache_v[page_table].reshape(DB, P, A_HEADS, A_VDIM)
    qpos = P + jnp.arange(Tq)
    d_past = (qpos[:, None] - jnp.arange(P)[None, :]).astype(jnp.float32)
    d_new = jnp.arange(Tq)[:, None] - jnp.arange(Tq)[None, :]
    s = jnp.concatenate([
        diff_scores(qa, kp, d_past, None),
        diff_scores(qa, ka.reshape(DB, Tq, A_HEADS, 2, HEAD_DIM), d_new.astype(jnp.float32), d_new >= 0)],
        axis=-1)
    w = diff_weights(s, lam).astype(va.dtype)
    return (jnp.einsum('bhqk,bkhe->bqhe', w[..., :P], vp)
            + jnp.einsum('bhqk,bkhe->bqhe', w[..., P:], va))

def dilated_branch_prompt(q, k, v, window, dil):
    B, T, H, Dh = q.shape
    n = window // dil
    L = T // dil
    nb = -(-L // Q_BLOCK)
    Lp = nb * Q_BLOCK

    def streams(a):
        return a.reshape(B, L, dil, H, Dh).transpose(0, 2, 1, 3, 4).reshape(B * dil, L, H, Dh)

    qs = jnp.pad(streams(q), ((0, 0), (0, Lp - L), (0, 0), (0, 0)))
    ks = jnp.pad(streams(k), ((0, 0), (n, Lp - L), (0, 0), (0, 0)))
    vs = jnp.pad(streams(v), ((0, 0), (n, Lp - L), (0, 0), (0, 0)))
    qblk = jnp.moveaxis(qs.reshape(B * dil, nb, Q_BLOCK, H, Dh), 1, 0)
    cidx = jnp.arange(Q_BLOCK + n)
    sd = jnp.arange(Q_BLOCK)[:, None] + n - cidx[None, :]
    bias = alibi_slopes(H)[:, None, None] * (sd * dil).astype(jnp.float32)

    def block(args):
        qi, i = args
        i0 = i * Q_BLOCK
        kb = lax.dynamic_slice_in_dim(ks, i0, Q_BLOCK + n, axis=1)
        vb = lax.dynamic_slice_in_dim(vs, i0, Q_BLOCK + n, axis=1)
        ok = (sd >= 0) & (sd <= n) & ((i0 - n + cidx) >= 0)[None, :]
        s = jnp.einsum('bqhd,bkhd->bhqk', qi, kb, preferred_element_type=jnp.float32) * (Dh ** -0.5) - bias
        p, lse = softmax_stats(jnp.where(ok, s, NEG_INF))
        o = jnp.einsum('bhqk,bkhd->bqhd', p.astype(vb.dtype), vb, preferred_element_type=jnp.float32)
        return o, jnp.moveaxis(lse, 1, 2)

    o, lse = lax.map(block, (qblk, jnp.arange(nb)))

    def unstream(a):
        tail = a.shape[3:]
        a = jnp.moveaxis(a, 0, 1).reshape((B * dil, Lp) + tail)[:, :L]
        a = a.reshape((B, dil, L) + tail)
        return jnp.swapaxes(a, 1, 2).reshape((B, T) + tail)

    return unstream(o), unstream(lse)

def dilated_branch_sample(q, k_ext, v_ext, n_buf, window, dil):
    DB, Tq, H, Dh = q.shape
    n = window // dil
    dist = jnp.arange(n + 1) * dil
    idx = n_buf + jnp.arange(Tq)[:, None] - dist[None, :]
    ok = idx >= 0
    idx = jnp.maximum(idx, 0)
    kg = jnp.take(k_ext, idx, axis=1)
    vg = jnp.take(v_ext, idx, axis=1)
    s = (jnp.einsum('bqhd,bqkhd->bhqk', q, kg, preferred_element_type=jnp.float32) * (Dh ** -0.5)
         - alibi_slopes(H)[:, None, None] * dist.astype(jnp.float32)[None, None, :])
    p, lse = softmax_stats(jnp.where(ok, s, NEG_INF))
    o = jnp.einsum('bhqk,bqkhd->bqhd', p.astype(vg.dtype), vg, preferred_element_type=jnp.float32)
    return o, jnp.moveaxis(lse, 1, 2)

def combine_branches(outs, lses, dtype):
    w = jax.nn.softmax(jnp.stack(lses, axis=0), axis=0)
    return jnp.sum(w[..., None] * jnp.stack(outs, axis=0), axis=0).astype(dtype)

def dilated_prompt(qb, kb, vb):
    res = [dilated_branch_prompt(qb, kb, vb, w, d) for (w, d) in DILATIONS]
    return combine_branches([r[0] for r in res], [r[1] for r in res], vb.dtype)

def dilated_sample(qb, k_ext, v_ext, n_buf):
    res = [dilated_branch_sample(qb, k_ext, v_ext, n_buf, w, d) for (w, d) in DILATIONS]
    return combine_branches([r[0] for r in res], [r[1] for r in res], qb.dtype)

def mix_out(x, oa, ob, subln_g, lam_init, w_out):
    B, T = x.shape[:2]
    oa = (rms_norm(oa, subln_g) * (1.0 - lam_init)).reshape(B, T, A_WIDTH)
    o = jnp.concatenate([oa, ob.reshape(B, T, B_WIDTH)], axis=-1)
    return x + jnp.einsum('btc,cd->btd', o, w_out)

def peer(x, w_q, sub_keys, u_tab, v_tab):
    n = x.shape[0]
    npad = -(-n // PEER_BLOCK) * PEER_BLOCK
    xb_all = jnp.pad(x, ((0, npad - n), (0, 0))).reshape(npad // PEER_BLOCK, PEER_BLOCK, D_MODEL)

    def block(xb):
        q = jnp.einsum('td,dc->tc', xb, w_q).reshape(PEER_BLOCK, PEER_HEADS, 2, D_KEY // 2)
        s = jnp.einsum('thcd,hcnd->thcn', q, sub_keys, preferred_element_type=jnp.float32)
        v1, i1 = lax.top_k(s[:, :, 0], PEER_TOPK)
        v2, i2 = lax.top_k(s[:, :, 1], PEER_TOPK)
        cand = (v1[..., :, None] + v2[..., None, :]).reshape(PEER_BLOCK, PEER_HEADS, PEER_TOPK * PEER_TOPK)
        cid = (i1[..., :, None] * N_KEYS + i2[..., None, :]).reshape(PEER_BLOCK, PEER_HEADS, PEER_TOPK * PEER_TOPK)
        sc, sel = lax.top_k(cand, PEER_TOPK)
        expert = jnp.take_along_axis(cid, sel, axis=-1)
        g = jax.nn.softmax(sc, axis=-1)
        a = jnp.einsum('td,thkd->thk', xb, u_tab[expert], preferred_element_type=jnp.float32)
        coef = (g * jax.nn.gelu(a, approximate=False)).astype(xb.dtype)
        return jnp.einsum('thk,thkd->td', coef, v_tab[expert])

    return lax.map(block, xb_all).reshape(npad, D_MODEL)[:n]

def channel(h, norm_g, w_q, sub_keys, u_tab, v_tab):
    B, T, D = h.shape
    y = peer(rms_norm(h, norm_g).reshape(B * T, D), w_q, sub_keys, u_tab, v_tab)
    return h + y.reshape(B, T, D)

def setup_inputs(seed: int = 0) -> dict:
    key = jax.random.key(seed)
    ks = jax.random.split(key, 24)
    f32 = jnp.float32
    n_pages = PAST_LEN // PAGE_SIZE
    n_used = DEC_BATCH * n_pages
    n_phys = n_used + max(1, n_used // 4)
    buf = min(B_WINDOW, PAST_LEN)

    def nrm(k, shape, scale):
        return jax.random.normal(k, shape, f32) * scale

    def gain(k, n):
        return 1.0 + nrm(k, (DEPTH, n), 0.05)

    page_table = jax.random.permutation(ks[4], n_phys)[:n_used].reshape(DEC_BATCH, n_pages).astype(jnp.int32)
    return {
        'x_prompt': nrm(ks[0], (BATCH, SEQ, D_MODEL), 1.0),
        'x_sample': nrm(ks[1], (DEC_BATCH, DEC_SEQ, D_MODEL), 1.0),
        'cache_a_k': nrm(ks[2], (DEPTH, n_phys, PAGE_SIZE, A_HEADS, A_QK), 1.0),
        'cache_a_v': nrm(ks[3], (DEPTH, n_phys, PAGE_SIZE, A_HEADS, A_VDIM), 1.0),
        'page_table': page_table,
        'state_b_k': nrm(ks[5], (DEPTH, DEC_BATCH, buf, B_HEADS, HEAD_DIM), 1.0),
        'state_b_v': nrm(ks[6], (DEPTH, DEC_BATCH, buf, B_HEADS, HEAD_DIM), 1.0),
        'norm1_g': gain(ks[7], D_MODEL),
        'w_in': nrm(ks[8], (DEPTH, D_MODEL, IN_COLS), D_MODEL ** -0.5),
        'qnorm_a': gain(ks[9], HEAD_DIM),
        'knorm_a': gain(ks[10], HEAD_DIM),
        'lambda_q1': nrm(ks[11], (DEPTH, HEAD_DIM), 0.1),
        'lambda_k1': nrm(ks[12], (DEPTH, HEAD_DIM), 0.1),
        'lambda_q2': nrm(ks[13], (DEPTH, HEAD_DIM), 0.1),
        'lambda_k2': nrm(ks[14], (DEPTH, HEAD_DIM), 0.1),
        'subln_g': gain(ks[15], A_VDIM),
        'qnorm_b': gain(ks[16], HEAD_DIM),
        'knorm_b': gain(ks[17], HEAD_DIM),
        'w_out': nrm(ks[18], (DEPTH, MIX_WIDTH, D_MODEL), MIX_WIDTH ** -0.5),
        'norm2_g': gain(ks[19], D_MODEL),
        'peer_wq': nrm(ks[20], (DEPTH, D_MODEL, PEER_HEADS * D_KEY), D_MODEL ** -0.5),
        'peer_subkeys': nrm(ks[21], (DEPTH, PEER_HEADS, 2, N_KEYS, D_KEY // 2), (D_KEY // 2) ** -0.5),
        'peer_u': nrm(ks[22], (DEPTH, N_EXPERTS, D_MODEL), D_MODEL ** -0.5),
        'peer_v': nrm(ks[23], (DEPTH, N_EXPERTS, D_MODEL), 0.25),
    }

def reference(x_prompt, x_sample, cache_a_k, cache_a_v, page_table, state_b_k, state_b_v,
              norm1_g, w_in, qnorm_a, knorm_a, lambda_q1, lambda_k1, lambda_q2, lambda_k2,
              subln_g, qnorm_b, knorm_b, w_out, norm2_g, peer_wq, peer_subkeys, peer_u, peer_v):
    hp, hs = x_prompt, x_sample
    akp, avp, aks, avs, bkp, bvp, bks, bvs = [], [], [], [], [], [], [], []
    for l in range(DEPTH):
        lam_init = 0.8 - 0.6 * math.exp(-0.3 * l)
        lam = (jnp.exp(jnp.sum(lambda_q1[l].astype(jnp.float32) * lambda_k1[l].astype(jnp.float32)))
               - jnp.exp(jnp.sum(lambda_q2[l].astype(jnp.float32) * lambda_k2[l].astype(jnp.float32)))
               + lam_init)
        qa, ka, va, qb, kb, vb = project(hp, norm1_g[l], w_in[l], qnorm_a[l], knorm_a[l], qnorm_b[l], knorm_b[l])
        oa = diff_attn_prompt(qa, ka, va, lam)
        ob = dilated_prompt(qb, kb, vb)
        hp = mix_out(hp, oa, ob, subln_g[l], lam_init, w_out[l])
        hp = channel(hp, norm2_g[l], peer_wq[l], peer_subkeys[l], peer_u[l], peer_v[l])
        keep = max(hp.shape[1] - B_WINDOW, 0)
        akp.append(ka)
        avp.append(va)
        bkp.append(kb[:, keep:])
        bvp.append(vb[:, keep:])
        qa, ka, va, qb, kb, vb = project(hs, norm1_g[l], w_in[l], qnorm_a[l], knorm_a[l], qnorm_b[l], knorm_b[l])
        oa = diff_attn_sample(qa, ka, va, cache_a_k[l], cache_a_v[l], page_table, lam)
        n_buf = state_b_k.shape[2]
        k_ext = jnp.concatenate([state_b_k[l], kb], axis=1)
        v_ext = jnp.concatenate([state_b_v[l], vb], axis=1)
        ob = dilated_sample(qb, k_ext, v_ext, n_buf)
        hs = mix_out(hs, oa, ob, subln_g[l], lam_init, w_out[l])
        hs = channel(hs, norm2_g[l], peer_wq[l], peer_subkeys[l], peer_u[l], peer_v[l])
        aks.append(ka)
        avs.append(va)
        bks.append(k_ext[:, -n_buf:])
        bvs.append(v_ext[:, -n_buf:])
    return (hp, hs, jnp.stack(akp), jnp.stack(avp), jnp.stack(aks), jnp.stack(avs),
            jnp.stack(bkp), jnp.stack(bvp), jnp.stack(bks), jnp.stack(bvs))


_drawn_inputs = setup_inputs


def setup_inputs(seed=0):
    import zlib

    import numpy as np

    out = dict(_drawn_inputs(seed))
    spreads = {}
    factors = {'qnorm_b': 4.096}
    for name, (base, spread) in spreads.items():
        noise = np.random.default_rng([zlib.crc32(name.encode()), seed]).standard_normal(out[name].shape)
        drawn = base * np.exp(spread * noise) if base else spread * noise
        out[name] = __import__('jax').numpy.asarray(drawn.astype(out[name].dtype))
    for name, factor in factors.items():
        out[name] = (out[name] * factor).astype(out[name].dtype)
    return out
```

```python
from contextlib import ExitStack

import numpy as np
import concourse.bass as bass
from concourse import mybir

F32 = mybir.dt.float32
BF16 = mybir.dt.bfloat16
I32 = mybir.dt.int32
U32 = mybir.dt.uint32
ALU = mybir.AluOpType
ACT = mybir.ActivationFunctionType
AX_X = mybir.AxisListType.X

P = 128
D = 1024
KD = D // P
SEQ = 1024
DB, DQ = 8, 4
NS = DB * DQ
NT = SEQ + NS
TILES = -(-NT // P)
TP = TILES * P
COLS = 3072
SEG = 512
NSEG = COLS // SEG
HD = 64
EPS = 1e-6
NEG = -1e30
PAST, PAGE, STATE = 4096, 128, 2048
PAGES = PAST // PAGE
LAM_INIT = 0.8 - 0.6
DILATIONS = ((128, 1), (512, 4), (2048, 16))
ds = bass.ds


def since(eng, sem, value):
    if not isinstance(value, int) or value > 0:
        eng.wait_ge(sem, value)


def turns(eng, n, body):
    body(0)
    with eng.Fori(1, n) as i:
        body(i)


class Steps:

    def __init__(self, base=0):
        self.base, self.n = base, 0

    def up(self):
        self.n += 1
        return 1

    @property
    def now(self):
        return self.base + self.n


def load_constants(nc, io, sems, ident):
    ident_loaded = sems("ident_loaded")
    pad_zeroed = sems("pad_zeroed")
    with nc.Block() as block:
        @block.sync
        def _(sp):
            sp.dma_start(ident, io["ident"]).then_inc(ident_loaded, 16)
            sp.dma_start(io["mix"][NT:TP, :], io["x"][NT:TP, :]).then_inc(pad_zeroed, 16)
            sp.wait_ge(ident_loaded, 16)
            sp.wait_ge(pad_zeroed, 16)


def project(nc, io, sems, ident, bank):
    with ExitStack() as ctx:
        def sb(name, shape, dt=F32):
            return ctx.enter_context(nc.sbuf_tensor(name, shape, dt))

        w = sb("w_in_sb", [P, KD, COLS])
        x_rows = sb("x_rows", [P, TILES, D])
        xs = sb("x_scaled", [P, D])
        xnT = sb("xn_T", [P, KD, P])
        h = sb("h_rows", [P, COLS])
        hn = sb("h_normed", [P, 4 * SEG])
        sq = sb("squares", [P, 4 * SEG])
        qkT = sb("qk_T", [P, 16, P])
        g1T = sb("g1_T", [P, KD])
        gain = sb("qk_gain", [P, 4, HD])
        ss = sb("x_sumsq", [P, TILES])
        std = sb("x_std", [P, TILES])
        rstd = sb("x_rstd", [P, TILES])
        hss = sb("h_sumsq", [P, 32])
        hstd = sb("h_std", [P, 32])
        hrstd = sb("h_rstd", [P, 32])

        w_loaded = [sems(f"w_loaded{k}") for k in range(KD)]
        gains_loaded = sems("p_gains_loaded")
        x_loaded = sems("x_loaded")
        step = sems("p_dve_step")
        x_squared = sems("x_squared")
        x_var_ready = sems("x_var_ready")
        x_std_ready = sems("x_std_ready")
        xs_ready = sems("xs_ready")
        xT_in_psum = sems("xT_in_psum")
        xnT_ready = sems("xnT_ready")
        xnT_used = sems("xnT_used")
        h_var_ready = sems("h_var_ready")
        h_std_ready = sems("h_std_ready")
        h_dve = sems("h_evac_dve")
        h_act = sems("h_evac_act")
        hn_ready = sems("hn_ready")
        qkT_in_psum = sems("qkT_in_psum")
        qkT_ready = sems("qkT_ready")
        rows_stored = sems("rows_stored")
        qkT_stored = sems("qkT_stored")

        h2 = h[:, :].rearrange("p (a c) -> p a c", a=2)[:, :, 0:2 * SEG]
        hn2 = hn[:, :].rearrange("p (a c) -> p a c", a=2)
        sq2 = sq[:, :].rearrange("p (a c) -> p a c", a=2)
        DVE_STEPS = 5

        block = ctx.enter_context(nc.Block())

        @block.sync
        def _(sp):
            sp.dma_start(x_rows[:, :, :], io["x"].rearrange("(t p) d -> p t d", p=P)).then_inc(x_loaded, 16)
            sp.dma_start(g1T[:, :], io["g1"]).then_inc(gains_loaded, 16)
            sp.dma_start(gain[:, :, :], io["qk_gain"].partition_broadcast(P)).then_inc(gains_loaded, 16)
            for k in range(KD):
                sp.dma_start(w[:, k, :], io["w_in"][k * P:(k + 1) * P, :]).then_inc(w_loaded[k], 16)
            def turn_of(t):
                r = ds(t * P, P)
                sp.wait_ge(hn_ready, t + 1)
                sp.wait_ge(qkT_ready, t * 4 + 4)
                sp.wait_ge(h_act, t * 3 + 3)
                sp.dma_start(io["ka"][r, :], hn[:, SEG:2 * SEG]).then_inc(rows_stored, 16)
                sp.dma_start(io["va"][r, :], h[:, 2 * SEG:3 * SEG]).then_inc(rows_stored, 16)
                sp.dma_start(io["kb"][r, :], hn[:, 3 * SEG:4 * SEG]).then_inc(rows_stored, 16)
                sp.dma_start(io["vb"][r, :], h[:, 5 * SEG:6 * SEG]).then_inc(rows_stored, 16)
                sp.dma_start(io["qkT"][:, :, ds(t * P, P)].rearrange("b p t -> p b t"), qkT[:, :, :]).then_inc(qkT_stored, 16)

            turns(sp, TILES, turn_of)
            sp.wait_ge(rows_stored, 64 * TILES)
            sp.wait_ge(qkT_stored, 16 * TILES)

        @block.vector
        def _(dve):
            dve.wait_ge(gains_loaded, 32)
            for seg in (0, 2):
                nc.vector.tensor_scalar(gain[:, seg, :], gain[:, seg, :], HD ** -0.5, None, ALU.mult).then_inc(step, 1)
            dve.wait_ge(x_squared, TILES)
            nc.vector.tensor_scalar(ss[:, :], ss[:, :], 1.0 / D, EPS, ALU.mult, ALU.add).then_inc(x_var_ready, 1)
            dve.wait_ge(x_std_ready, 1)
            nc.vector.reciprocal(rstd[:, :], std[:, :]).then_inc(step, 1)
            dve.wait_ge(step, 3)

            def scale_rows(t):
                nc.vector.tensor_scalar(xs[:, :], x_rows[:, ds(t, 1), :].rearrange("p a d -> p (a d)"),
                                        rstd[:, ds(t, 1)], None, ALU.mult).then_inc(xs_ready, 1)

            def gain_xT(t):
                since(dve, xnT_used, t * 2)
                for b in range(2):
                    dve.wait_ge(xT_in_psum, t * 2 + b + 1)
                    nc.vector.tensor_tensor(
                        xnT[:, 4 * b:4 * b + 4, :], bank[:, 6 + b, :].rearrange("p (k t) -> p k t", k=4),
                        g1T[:, 4 * b:4 * b + 4].unsqueeze(2).broadcast_to([P, 4, P]), ALU.mult).then_inc(xnT_ready, 1)

            def norm_qk(t):
                s = Steps(t * DVE_STEPS + 3)
                dve.wait_ge(xnT_used, t * 2 + 2)
                since(dve, hn_ready, t)
                for c in (0, 1, 3):
                    nc.vector.tensor_copy(h[:, c * SEG:(c + 1) * SEG], bank[:, c, :]).then_inc(h_dve, 1)
                dve.wait_ge(h_dve, t * 3 + 3)
                dve.wait_ge(h_act, t * 3 + 1)
                nc.vector.tensor_tensor(sq2, h2, h2, ALU.mult).then_inc(step, s.up())
                dve.wait_ge(step, s.now)
                nc.vector.tensor_reduce(hss[:, :], sq[:, :].rearrange("p (g d) -> p g d", d=HD), AX_X,
                                        ALU.add).then_inc(step, s.up())
                dve.wait_ge(step, s.now)
                nc.vector.tensor_scalar(hss[:, :], hss[:, :], 1.0 / HD, EPS, ALU.mult, ALU.add).then_inc(h_var_ready, 1)
                dve.wait_ge(h_std_ready, t + 1)
                nc.vector.reciprocal(hrstd[:, :], hstd[:, :]).then_inc(step, s.up())
                dve.wait_ge(step, s.now)
                since(dve, rows_stored, t * 64)
                since(dve, qkT_in_psum, t * 4)
                for a in range(2):
                    nc.vector.tensor_tensor(
                        hn2[:, a, :].rearrange("p (g d) -> p g d", d=HD), h2[:, a, :].rearrange("p (g d) -> p g d", d=HD),
                        hrstd[:, 16 * a:16 * a + 16].unsqueeze(2).broadcast_to([P, 16, HD]),
                        ALU.mult).then_inc(step, s.up())
                dve.wait_ge(step, s.now)
                assert s.n == DVE_STEPS
                for seg in range(4):
                    hs = hn[:, seg * SEG:(seg + 1) * SEG].rearrange("p (g d) -> p g d", d=HD)
                    ins = nc.vector.tensor_tensor(hs, hs, gain[:, seg, :].unsqueeze(1).broadcast_to([P, 8, HD]), ALU.mult)
                ins.then_inc(hn_ready, 1)

            scale_rows(0)
            gain_xT(0)
            def turn_of(t):
                scale_rows(t + 1)
                gain_xT(t + 1)
                norm_qk(t)

            turns(dve, TILES - 1, turn_of)
            norm_qk(TILES - 1)

        @block.scalar
        def _(act):
            act.wait_ge(x_loaded, 16)
            for t in range(TILES):
                if t:
                    since(act, x_squared, t)
                nc.scalar.activation(sq[:, 0:D], x_rows[:, t, :], ACT.Square,
                                     accum_out=ss[:, t:t + 1]).then_inc(x_squared, 1)
            act.wait_ge(x_var_ready, 1)
            nc.scalar.activation(std[:, :], ss[:, :], ACT.Sqrt).then_inc(x_std_ready, 1)
            def turn_of(t):
                act.wait_ge(xnT_used, t * 2 + 2)
                since(act, rows_stored, t * 64)
                since(act, hn_ready, t)
                for c in (4, 2, 5):
                    nc.scalar.copy(h[:, c * SEG:(c + 1) * SEG], bank[:, c, :]).then_inc(h_act, 1)
                act.wait_ge(h_var_ready, t + 1)
                nc.scalar.activation(hstd[:, :], hss[:, :], ACT.Sqrt).then_inc(h_std_ready, 1)
                since(act, qkT_stored, t * 16)
                for g in range(4):
                    act.wait_ge(qkT_in_psum, t * 4 + g + 1)
                    nc.scalar.copy(qkT[:, 4 * g:4 * g + 4, :].rearrange("p k t -> p (k t)"),
                                   bank[:, 6 + g % 2, :]).then_inc(qkT_ready, 1)

            turns(act, TILES, turn_of)

        @block.tensor
        def _(pe):
            def transpose_x(t):
                pe.wait_ge(xs_ready, t + 1)
                if not (isinstance(t, int) and t == 0):
                    pe.wait_ge(qkT_ready, t * 4 - 4)
                for b in range(2):
                    for j in range(4):
                        k = 4 * b + j
                        ins = nc.tensor.transpose(bank[:, 6 + b, j * P:(j + 1) * P], xs[:, k * P:(k + 1) * P], ident)
                    ins.then_inc(xT_in_psum, 1)

            def products(t, ks):
                for k in ks:
                    if k == 0:
                        since(pe, h_dve, t * 3)
                        since(pe, h_act, t * 3)
                    if k % 4 == 0:
                        pe.wait_ge(xnT_ready, t * 2 + k // 4 + 1)
                    pe.wait_ge(w_loaded[k], 16)
                    for c in range(NSEG):
                        ins = nc.tensor.matmul(bank[:, c, :], xnT[:, k, :], w[:, k, c * SEG:(c + 1) * SEG],
                                               start=(k == 0), stop=(k == KD - 1))
                    if k % 4 == 3:
                        ins.then_inc(xnT_used, 1)

            def transpose_qk(t):
                pe.wait_ge(hn_ready, t + 1)
                for g in range(4):
                    if g >= 2:
                        pe.wait_ge(qkT_ready, t * 4 + g - 1)
                    for j in range(4):
                        c = 4 * g + j
                        ins = nc.tensor.transpose(bank[:, 6 + g % 2, j * P:(j + 1) * P], hn[:, c * P:(c + 1) * P], ident)
                    ins.then_inc(qkT_in_psum, 1)

            transpose_x(0)
            products(0, range(7))
            transpose_x(1)
            products(0, [7])
            with pe.Fori(1, TILES - 1) as t:
                products(t, range(4))
                pe.wait_ge(xnT_ready, t * 2 + 2)
                transpose_qk(t - 1)
                products(t, range(4, 7))
                transpose_x(t + 1)
                products(t, [7])
            products(TILES - 1, range(4))
            pe.wait_ge(xnT_ready, 2 * TILES)
            transpose_qk(TILES - 2)
            products(TILES - 1, range(4, 8))
            transpose_qk(TILES - 1)


UNITS = 4
QT = SEQ // P
NB = 2


def lambda_column(nc, io, sems, out):
    with ExitStack() as ctx:
        def sb(name, shape):
            return ctx.enter_context(nc.sbuf_tensor(name, shape, F32))

        lams = sb("lams", [P, 2, 2, HD])
        prod = sb("lam_prod", [P, 2, HD])
        dots = sb("lam_dots", [P, 2])
        exps = sb("lam_exps", [P, 2])
        diff = sb("lam_diff", [P, 1])
        lams_loaded = sems("lams_loaded")
        step = sems("lam_step")
        dots_ready = sems("lam_dots_ready")
        exps_ready = sems("lam_exps_ready")
        with nc.Block() as block:
            @block.sync
            def _(sp):
                sp.dma_start(lams[:, :, :, :].rearrange("p a b d -> p (a b) d"),
                             io["lams"].partition_broadcast(P)).then_inc(lams_loaded, 16)

            @block.vector
            def _(dve):
                dve.wait_ge(lams_loaded, 16)
                nc.vector.tensor_tensor(prod[:, :, :], lams[:, :, 0, :], lams[:, :, 1, :], ALU.mult).then_inc(step, 1)
                dve.wait_ge(step, 1)
                nc.vector.tensor_reduce(dots[:, :], prod[:, :, :], AX_X, ALU.add).then_inc(dots_ready, 1)
                dve.wait_ge(exps_ready, 1)
                nc.vector.tensor_tensor(diff[:, :], exps[:, 1:2], exps[:, 0:1], ALU.subtract).then_inc(step, 1)
                dve.wait_ge(step, 2)
                nc.vector.tensor_scalar(out, diff[:, :], -LAM_INIT, None, ALU.add).then_inc(step, 1)
                dve.wait_ge(step, 3)

            @block.scalar
            def _(act):
                act.wait_ge(dots_ready, 1)
                nc.scalar.activation(exps[:, :], dots[:, :], ACT.Exp).then_inc(exps_ready, 1)


def attend_prompt(nc, io, sems, ident, bank, neg_lam, mixer):
    a = mixer == "a"
    with ExitStack() as ctx:
        def sb(name, shape, dt=F32):
            return ctx.enter_context(nc.sbuf_tensor(f"{name}_{mixer}", shape, dt))

        def sem(name):
            return sems(f"{name}_{mixer}")

        MW = 1 if a else 2
        q = [sb(f"q{u}", [HD, 2, SEQ]) for u in range(NB)]
        k = [sb(f"k{u}", [HD, 2, SEQ]) for u in range(NB)]
        v = [sb(f"v{u}", [P, QT, P]) for u in range(NB)]
        strip = [sb(f"strip{u}", [P, MW, SEQ]) for u in range(NB)]
        neg_s = sb("neg_scores", [P, 2, SEQ])
        e = sb("exps", [P, 2, 2, SEQ])
        w = sb("weights", [P, 2, 1, SEQ]) if a else e
        wT = sb("weights_T", [P, 2, MW, QT, P])
        neg_max = sb("neg_max", [P, 2, 2])
        den = sb("den", [P, 2, 2])
        rden = sb("rden", [P, 2, 2])
        r2 = sb("r2", [P, 2])
        o = sb("o", [P, 2, P])
        gate = sb("gate", [P, 2 * NB * QT])

        loaded = [sem(f"pr_loaded{u}") for u in range(NB)]
        s_in_psum = sem("s_in_psum")
        s_biased = sem("s_biased")
        exp_done = sem("exp_done")
        step = sem("pr_step")
        w_ready = sem("w_ready")
        wT_in_psum = sem("wT_in_psum")
        wT_ready = sem("wT_ready")
        o_in_psum = sem("o_in_psum")
        o_ready = sem("o_ready")
        o_stored = [sem(f"o_stored{par}") for par in range(2)]

        TURNS = UNITS // NB
        TURN_TILES = NB * QT
        GROUPS = [-(-(i + 1) // 4) for i in range(QT)]
        TURN_GROUPS = NB * MW * sum(GROUPS)
        first_q, first_k = (0, 4) if a else (8, 12)
        v_rows = io["va"] if a else io["vb"]

        def group_at(n):
            return MW * (n // QT * sum(GROUPS) + sum(GROUPS[:n % QT]))

        block = ctx.enter_context(nc.Block())

        @block.sync
        def _(sp):
            def turn_of(turn):
                for u in range(NB):
                    since(sp, o_ready, turn * TURN_TILES)
                    qt = io["qkT"][ds(turn * NB + (first_q + u), 1), :, 0:SEQ]
                    sp.dma_start(q[u][:, :, :], qt.rearrange("a (m d) t -> d (a m) t", m=2)).then_inc(loaded[u], 16)
                    kt = io["qkT"][ds(turn * NB + (first_k + u), 1), :, 0:SEQ]
                    sp.dma_start(k[u][:, :, :], kt.rearrange("a (m d) t -> d (a m) t", m=2)).then_inc(loaded[u], 16)
                    vt = v_rows[0:SEQ, ds(turn * (NB * P) + u * P, P)]
                    sp.dma_start(v[u][:, :, :], vt.rearrange("(j p) e -> p j e", p=P)).then_inc(loaded[u], 16)
                    st = io["strips"][ds(turn * (NB * MW) + (u * MW + (0 if a else 4)), MW), :, :]
                    sp.dma_start(strip[u][:, :, :], st.rearrange("m p c -> p m c")).then_inc(loaded[u], 16)
                for n in range(TURN_TILES):
                    u, i = n // QT, n % QT
                    sp.wait_ge(o_ready, turn * TURN_TILES + (n + 1))
                    sp.dma_start(io["mix"][i * P:(i + 1) * P, ds(turn * (NB * P) + ((0 if a else SEG) + u * P), P)],
                                 o[:, n % 2, :]).then_inc(o_stored[n % 2], 16)

            turns(sp, TURNS, turn_of)
            for par in range(2):
                sp.wait_ge(o_stored[par], 8 * UNITS * QT)

        @block.tensor
        def _(pe):
            def scores(turn, n):
                u, i = n // QT, n % QT
                for m in range(2):
                    since(pe, s_biased, turn * (2 * TURN_TILES) + max(0, 2 * n + m - 1))
                    for c in range(0, (i + 1) * P, 512):
                        width = min(512, (i + 1) * P - c)
                        ins = nc.tensor.matmul(bank[:, 2 * m + c // 512, 0:width], q[u][:, m, i * P:(i + 1) * P],
                                               k[u][:, m, c:c + width], start=True, stop=True)
                    ins.then_inc(s_in_psum, 1)

            def transpose_weights(turn, n):
                i = n % QT
                g = group_at(n)
                if a:
                    pe.wait_ge(w_ready, turn * TURN_TILES + (n + 1))
                for mw in range(MW):
                    if not a:
                        pe.wait_ge(exp_done, turn * (2 * TURN_TILES) + (2 * n + mw + 1))
                    for j0 in range(0, i + 1, 4):
                        since(pe, wT_ready, turn * TURN_GROUPS + max(0, g - 1))
                        for j in range(j0, min(j0 + 4, i + 1)):
                            ins = nc.tensor.transpose(bank[:, 4 + g % 2, (j - j0) * P:(j - j0 + 1) * P],
                                                      w[:, n % 2, mw, j * P:(j + 1) * P], ident)
                        ins.then_inc(wT_in_psum, 1)
                        g += 1

            def weigh_values(turn, n):
                u, i = n // QT, n % QT
                since(pe, o_ready, turn * TURN_TILES + max(0, n - 1))
                width = P // MW
                for mw in range(MW):
                    pe.wait_ge(wT_ready, turn * TURN_GROUPS + (group_at(n) + (mw + 1) * GROUPS[i]))
                    for j in range(i + 1):
                        ins = nc.tensor.matmul(bank[:, 6 + n % 2, mw * width:(mw + 1) * width], wT[:, n % 2, mw, j, :],
                                               v[u][:, j, mw * width:(mw + 1) * width], start=(j == 0), stop=(j == i))
                ins.then_inc(o_in_psum, 1)

            def turn_of(turn):
                pe.wait_ge(loaded[0], turn * 64 + 64)
                scores(turn, 0)
                for n in range(TURN_TILES):
                    if n + 1 == QT:
                        pe.wait_ge(loaded[1], turn * 64 + 64)
                    if n + 1 < TURN_TILES:
                        scores(turn, n + 1)
                    transpose_weights(turn, n)
                    weigh_values(turn, n)

            turns(pe, TURNS, turn_of)

        @block.vector
        def _(dve):
            def bias(turn, n):
                u, i = n // QT, n % QT
                L = (i + 1) * P
                for m in range(2):
                    dve.wait_ge(s_in_psum, turn * (2 * TURN_TILES) + (2 * n + m + 1))
                    since(dve, exp_done, turn * (2 * TURN_TILES) + max(0, 2 * n + m - 1))
                    nc.vector.memset(gate[:, 2 * n + m:2 * n + m + 1], 0.0)
                    nc.vector.tensor_tensor_reduce(
                        neg_s[:, m, 0:L], bank[:, 2 * m:2 * m + 2, :].rearrange("p b c -> p (b c)")[:, 0:L],
                        strip[u][:, m % MW, SEQ - L:SEQ], -1.0, 3e38, ALU.add, ALU.min,
                        neg_max[:, n % 2, m:m + 1]).then_inc(s_biased, 1)

            STEPS = 3 if a else 1

            def combine(turn, n):
                i, par = n % QT, n % 2
                L = (i + 1) * P
                s = Steps(n * STEPS)
                dve.wait_ge(exp_done, turn * (2 * TURN_TILES) + (2 * n + 2))
                nc.vector.reciprocal(rden[:, par, :], den[:, par, :]).then_inc(step, s.up())
                dve.wait_ge(step, turn * (TURN_TILES * STEPS) + s.now)
                if a:
                    nc.vector.tensor_tensor(r2[:, par:par + 1], rden[:, par, 1:2], neg_lam, ALU.mult).then_inc(step, s.up())
                    dve.wait_ge(step, turn * (TURN_TILES * STEPS) + s.now)
                    nc.vector.tensor_scalar(e[:, par, 1, 0:L], e[:, par, 1, 0:L], r2[:, par:par + 1], None,
                                            ALU.mult).then_inc(step, s.up())
                    since(dve, wT_in_psum, turn * TURN_GROUPS + (group_at(n - 1) if n else 0))
                    dve.wait_ge(step, turn * (TURN_TILES * STEPS) + s.now)
                    nc.vector.scalar_tensor_tensor(w[:, par, 0, 0:L], e[:, par, 0, 0:L], rden[:, par, 0:1],
                                                   e[:, par, 1, 0:L], ALU.mult, ALU.add).then_inc(w_ready, 1)

            def output(turn, n):
                par = n % 2
                dve.wait_ge(o_in_psum, turn * TURN_TILES + (n + 1))
                since(dve, o_stored[par], turn * (8 * TURN_TILES) + 16 * (n // 2))
                if a:
                    nc.vector.tensor_copy(o[:, par, :], bank[:, 6 + par, 0:P]).then_inc(o_ready, 1)
                else:
                    for m in range(2):
                        ins = nc.vector.tensor_scalar(o[:, par, m * HD:(m + 1) * HD], bank[:, 6 + par, m * HD:(m + 1) * HD],
                                                      rden[:, par, m:m + 1], None, ALU.mult)
                    ins.then_inc(o_ready, 1)

            def turn_of(turn):
                dve.wait_ge(loaded[0], turn * 64 + 64)
                bias(turn, 0)
                for n in range(TURN_TILES):
                    combine(turn, n)
                    if n + 1 == QT:
                        dve.wait_ge(loaded[1], turn * 64 + 64)
                    if n + 1 < TURN_TILES:
                        bias(turn, n + 1)
                    output(turn, n)

            turns(dve, TURNS, turn_of)

        @block.scalar
        def _(act):
            def exps(turn, n):
                L = (n % QT + 1) * P
                if a:
                    since(act, w_ready, turn * TURN_TILES + max(0, n - 1))
                else:
                    since(act, wT_in_psum, turn * TURN_GROUPS + (group_at(n - 1) if n else 0))
                    since(act, o_ready, turn * TURN_TILES + max(0, n - 1))
                for m in range(2):
                    act.wait_ge(s_biased, turn * (2 * TURN_TILES) + (2 * n + m + 1))
                    nc.scalar.activation(e[:, n % 2, m, 0:L], neg_s[:, m, 0:L], ACT.Exp, bias=neg_max[:, n % 2, m:m + 1],
                                         scale=-1.0, accum_out=den[:, n % 2, m:m + 1]).then_inc(exp_done, 1)

            def take_weights_T(turn, n):
                i = n % QT
                g = group_at(n)
                since(act, o_in_psum, turn * TURN_TILES + max(0, n - 1))
                for mw in range(MW):
                    for j0 in range(0, i + 1, 4):
                        j1 = min(j0 + 4, i + 1)
                        act.wait_ge(wT_in_psum, turn * TURN_GROUPS + (g + 1))
                        nc.scalar.copy(wT[:, n % 2, mw, j0:j1, :].rearrange("p j t -> p (j t)"),
                                       bank[:, 4 + g % 2, 0:(j1 - j0) * P]).then_inc(wT_ready, 1)
                        g += 1

            def turn_of(turn):
                exps(turn, 0)
                for n in range(TURN_TILES):
                    take_weights_T(turn, n)
                    if n + 1 < TURN_TILES:
                        exps(turn, n + 1)

            turns(act, TURNS, turn_of)


ROWS = 32


def attend_sample(nc, io, sems, ident, bank, neg_lam, mixer):
    a = mixer == "a"
    with ExitStack() as ctx:
        def sb(name, shape, dt=F32):
            return ctx.enter_context(nc.sbuf_tensor(f"{name}_s{mixer}", shape, dt))

        def sem(name):
            return sems(f"{name}_s{mixer}")

        TILES_OF = [4] * (PAGES // 4) if a else [4, 3]
        C = len(TILES_OF)
        R = min(4, C)
        KEYS = P * sum(TILES_OF)
        LAG = 2
        FILL = 64 if a else 16
        heads = 4 if a else 8
        width = SEG // heads

        kbuf = [sb(f"keys{r}", [P, 4, 4, P]) for r in range(R)]
        vbuf = [sb(f"values{r}", [P, 4, SEG]) for r in range(R)]
        bias = sb("bias", [ROWS, KEYS + DQ])
        neg_s = sb("neg_scores", [ROWS, KEYS + DQ])
        e = sb("exps", [ROWS, KEYS + DQ])
        eT = sb("exps_T", [P, sum(TILES_OF), ROWS])
        eT_new = sb("exps_T_new", [DQ, ROWS])
        v_new = sb("v_new", [DQ, SEG])
        qs = sb("q_new", [P, 4, NS])
        kn = sb("k_new", [P, 4, NS])
        q_all = sb("q_blocks_all", [P, DB, 4, ROWS])
        qd = sb("q_blocks", [P, 4, ROWS])
        pages = sb("pages", [1, DB * PAGES], I32)
        mins = sb("mins", [ROWS, C + 1])
        neg_max = sb("neg_max", [ROWS, 1])
        den = sb("den", [ROWS, 1])
        rden = sb("rden", [ROWS, 1])
        rvec = sb("rvec", [ROWS, 1])
        second = sb("second_map", [ROWS, 1])
        coef = sb("coef", [ROWS, 1])
        sel = sb("sel", [P, heads, DQ])
        o_rows = sb("o_rows", [P, SEG])
        o = sb("o", [DQ, SEG])
        gate = sb("gate", [ROWS, C + 1])

        consts_loaded = sem("consts_loaded")
        cleared = sem("cleared")
        k_loaded = [sem(f"k_loaded{r}") for r in range(R)]
        v_loaded = [sem(f"v_loaded{r}") for r in range(R)]
        v_new_loaded = sem("v_new_loaded")
        setup = sem("setup")
        qd_ready = sem("qd_ready")
        scored = sem("scored")
        s_biased = sem("s_biased")
        max_ready = sem("max_ready")
        exp_done = sem("exp_done")
        e_transposed = sem("e_transposed")
        eT_ready = sem("eT_ready")
        values_done = sem("values_done")
        step = sem("step")
        o_scaled = sem("o_scaled")
        o_folded = sem("o_folded")
        o_ready = sem("o_ready")
        o_stored = sem("o_stored")
        first_q, first_k = (0, 4) if a else (8, 12)
        new_scores = bank[0:ROWS, 4, 0:DQ]

        block = ctx.enter_context(nc.Block())

        @block.sync
        def _(sp):
            def load_k(b, c):
                r = c % R
                if not (isinstance(b, int) and b * C + c < R):
                    sp.wait_ge(scored, b * (C + 1) + (c - R + 1 if c >= R else c - R))
                if a:
                    for j in range(4):
                        page = sp.value_load(pages[0:1, ds(b * PAGES + (4 * c + j), 1)], min_val=0,
                                             max_val=io["cache_k"].shape[0] - 1)
                        sp.dma_start(kbuf[r][:, j, :, :].rearrange("p h t -> p (h t)"),
                                     io["cache_k"][ds(page, 1), :, :].rearrange("a p c -> (a p) c")).then_inc(k_loaded[r], 16)
                else:
                    n, at = TILES_OF[c], sum(TILES_OF[:c])
                    sp.dma_start(kbuf[r][:, 0:n, :, :].rearrange("p j h t -> p (j h t)"),
                                 io["win_k"][ds(b, 1), :, at * SEG:(at + n) * SEG].rearrange("a p c -> (a p) c")).then_inc(k_loaded[r], 16)

            def load_v(b, c):
                r = c % R
                if not (isinstance(b, int) and b * C + c < R):
                    sp.wait_ge(values_done, b * C + (c - R + 1))
                if a:
                    for j in range(4):
                        page = sp.value_load(pages[0:1, ds(b * PAGES + (4 * c + j), 1)], min_val=0,
                                             max_val=io["cache_v"].shape[0] - 1)
                        sp.dma_start(vbuf[r][:, j, :],
                                     io["cache_v"][ds(page, 1), :, :].rearrange("a p c -> (a p) c")).then_inc(v_loaded[r], 16)
                else:
                    n, at = TILES_OF[c], sum(TILES_OF[:c])
                    sp.dma_start(vbuf[r][:, 0:n, :].rearrange("p j c -> p (j c)"),
                                 io["win_v"][ds(b, 1), :, at * SEG:(at + n) * SEG].rearrange("a p c -> (a p) c")).then_inc(v_loaded[r], 16)
                if c == C - 1:
                    since(sp, values_done, b * C)
                    v_rows = io["va"] if a else io["vb"]
                    sp.dma_start(v_new[:, :], v_rows[ds(b * DQ + SEQ, DQ), :]).then_inc(v_new_loaded, 16)

            def store(b):
                sp.wait_ge(o_ready, b + 1)
                sp.dma_start(io["mix"][ds(b * DQ + SEQ, DQ), (0 if a else SEG):(SEG if a else D)], o[:, :]).then_inc(o_stored, 16)

            sp.dma_start(qs[:, :, :], io["qkT"][first_q:first_q + 4, :, SEQ:NT].rearrange("h p t -> p h t")).then_inc(consts_loaded, 16)
            sp.dma_start(kn[:, :, :], io["qkT"][first_k:first_k + 4, :, SEQ:NT].rearrange("h p t -> p h t")).then_inc(consts_loaded, 16)
            sp.dma_start(bias[:, :], io[f"bias_{mixer}"]).then_inc(consts_loaded, 16)
            sp.dma_start(second[:, :], io["second_map"]).then_inc(consts_loaded, 16)
            sp.dma_start(pages[:, :], io["page_table"]).then_inc(consts_loaded, 16)
            sp.wait_ge(cleared, 2)
            sp.dma_start(sel[0:ROWS, :, :], io[f"sel_{mixer}"]).then_inc(consts_loaded, 16)
            sp.wait_ge(consts_loaded, 96)
            for c in range(C):
                load_k(0, c)
            for c in range(C):
                load_k(1, c)
                load_v(0, c)
            with sp.Fori(1, DB - 1) as b:
                store(b - 1)
                for c in range(C):
                    load_k(b + 1, c)
                    load_v(b, c)
            store(DB - 2)
            for c in range(C):
                load_v(DB - 1, c)
            store(DB - 1)
            sp.wait_ge(o_stored, 16 * DB)

        @block.gpsimd
        def _(pool):
            nc.gpsimd.memset(sel[:, :, :], 0.0).then_inc(cleared, 1)
            nc.gpsimd.memset(o_rows[:, :], 0.0).then_inc(cleared, 1)

        @block.tensor
        def _(pe):
            def scores(b, c):
                n = TILES_OF[c]
                pe.wait_ge(k_loaded[c % R], b * (FILL * (C // R)) + FILL * (c // R + 1))
                if c == 0:
                    pe.wait_ge(qd_ready, b + 1)
                if not (isinstance(b, int) and b == 0 and c < R):
                    pe.wait_ge(s_biased, b * (C + 1) + (c - R + 1 if c >= R else c - R))
                if c == C - 1:
                    since(pe, s_biased, b * (C + 1))
                    if not isinstance(b, int):
                        pe.wait_ge(o_ready, b - 1)
                for h in range(4):
                    ins = nc.tensor.matmul(bank[0:ROWS, c % R, 0:n * P], qd[:, h, :], kbuf[c % R][:, 0:n, h, :],
                                           start=(h == 0), stop=(h == 3))
                ins.then_inc(scored, 1)
                if c == C - 1:
                    for h in range(4):
                        ins = nc.tensor.matmul(new_scores, qd[:, h, :], kn[:, h, ds(b * DQ, DQ)],
                                               start=(h == 0), stop=(h == 3))
                    ins.then_inc(scored, 1)

            def transpose_exps(b):
                pe.wait_ge(exp_done, b + 1)
                for c in range(C):
                    n, at = TILES_OF[c], sum(TILES_OF[:c])
                    since(pe, eT_ready, b * C + max(0, c - 1))
                    nc.tensor.transpose(bank[:, 5 + c % 2, 3 * P:4 * P], ident, ident)
                    for j in range(n):
                        ins = nc.tensor.transpose(bank[:, 5 + c % 2, j * ROWS:(j + 1) * ROWS],
                                                  e[:, (at + j) * P:(at + j + 1) * P], ident[0:ROWS, 0:ROWS])
                    if c == C - 1:
                        ins = nc.tensor.transpose(bank[0:DQ, 5 + c % 2, 4 * ROWS:5 * ROWS], e[:, KEYS:KEYS + DQ],
                                                  ident[0:ROWS, 0:ROWS])
                    ins.then_inc(e_transposed, 1)

            def values(b, c):
                n, at = TILES_OF[c], sum(TILES_OF[:c])
                pe.wait_ge(v_loaded[c % R], b * (FILL * (C // R)) + FILL * (c // R + 1))
                pe.wait_ge(eT_ready, b * C + (c + 1))
                if c == 0:
                    since(pe, o_scaled, b)
                if c == C - 1:
                    pe.wait_ge(v_new_loaded, b * 16 + 16)
                for j in range(n):
                    ins = nc.tensor.matmul(bank[0:ROWS, 7, :], eT[:, at + j, :], vbuf[c % R][:, j, :],
                                           start=(c == 0 and j == 0), stop=False)
                if c == C - 1:
                    ins = nc.tensor.matmul(bank[0:ROWS, 7, :], eT_new[:, :], v_new[:, :], start=False, stop=True)
                ins.then_inc(values_done, 1)

            def fold(b):
                pe.wait_ge(o_scaled, b + 1)
                since(pe, o_ready, b)
                pe.wait_ge(s_biased, min(b + 2, DB) * (C + 1) if isinstance(b, int) else b * (C + 1) + 2 * (C + 1))
                for h in range(heads):
                    ins = nc.tensor.matmul(bank[0:DQ, 4, h * width:(h + 1) * width], sel[:, h, :],
                                           o_rows[:, h * width:(h + 1) * width], start=True, stop=True)
                ins.then_inc(o_folded, 1)

            pe.wait_ge(consts_loaded, 96)
            pe.wait_ge(cleared, 2)
            for c in range(C):
                scores(0, c)
            def turn_of(b):
                for c in range(C):
                    scores(b + 1, c)
                    if c == LAG - 1:
                        transpose_exps(b)
                    if c >= LAG:
                        values(b, c - LAG)
                for c in range(C - LAG, C):
                    values(b, c)
                fold(b)

            turns(pe, DB - 1, turn_of)
            transpose_exps(DB - 1)
            for c in range(C):
                values(DB - 1, c)
            fold(DB - 1)

        @block.vector
        def _(dve):
            dve.wait_ge(cleared, 2)
            nc.vector.memset(q_all[:, :, :, :], 0.0).then_inc(setup, 1)
            dve.wait_ge(consts_loaded, 96)
            dve.wait_ge(setup, 1)
            for h in range(4):
                for m in range(2):
                    half = slice(m * HD, (m + 1) * HD)
                    col = h * 2 * DQ + m * DQ
                    nc.vector.tensor_copy(q_all[half, :, h, col:col + DQ],
                                          qs[half, h, :].rearrange("p (b q) -> p b q", q=DQ)).then_inc(setup, 1)
            nc.vector.tensor_scalar(coef[:, :], second[:, :], -1.0 if a else 0.0, 1.0, ALU.mult, ALU.add).then_inc(setup, 1)
            dve.wait_ge(setup, 10)
            if a:
                nc.vector.scalar_tensor_tensor(coef[:, :], second[:, :], neg_lam[0:ROWS, :], coef[:, :],
                                               ALU.mult, ALU.add).then_inc(setup, 1)
                dve.wait_ge(setup, 11)

            def blocks(b):
                since(dve, scored, b * (C + 1))
                nc.vector.tensor_copy(qd[:, :, :], q_all[:, ds(b, 1), :, :].rearrange("p a h r -> p (a h) r")).then_inc(qd_ready, 1)

            def bias_scores(b, c):
                n = KEYS if c == C else sum(TILES_OF[:c]) * P
                w = DQ if c == C else TILES_OF[c] * P
                src = new_scores if c == C else bank[0:ROWS, c % R, 0:w]
                dve.wait_ge(scored, b * (C + 1) + (c + 1))
                since(dve, exp_done, b)
                nc.vector.memset(gate[:, c:c + 1], 0.0)
                nc.vector.tensor_tensor_reduce(neg_s[:, n:n + w], src, bias[:, n:n + w], -1.0, 3e38, ALU.add, ALU.min,
                                               mins[:, c:c + 1]).then_inc(s_biased, 1)
                if c == C:
                    dve.wait_ge(s_biased, b * (C + 1) + (C + 1))
                    nc.vector.tensor_reduce(neg_max[:, :], mins[:, :], AX_X, ALU.min).then_inc(max_ready, 1)

            def scale_output(b):
                dve.wait_ge(exp_done, b + 1)
                nc.vector.reciprocal(rden[:, :], den[:, :]).then_inc(step, 1)
                dve.wait_ge(step, b * 2 + 1)
                nc.vector.tensor_tensor(rvec[:, :], rden[:, :], coef[:, :], ALU.mult).then_inc(step, 1)
                dve.wait_ge(step, b * 2 + 2)

            def take_output(b):
                dve.wait_ge(values_done, b * C + C)
                since(dve, o_folded, b)
                nc.vector.tensor_scalar(o_rows[0:ROWS, :], bank[0:ROWS, 7, :], rvec[:, :], None, ALU.mult).then_inc(o_scaled, 1)
                dve.wait_ge(o_folded, b + 1)
                since(dve, o_stored, b * 16)
                nc.vector.tensor_copy(o[:, :], bank[0:DQ, 4, :]).then_inc(o_ready, 1)

            blocks(0)
            for c in range(C + 1):
                bias_scores(0, c)
            def turn_of(b):
                scale_output(b)
                blocks(b + 1)
                for c in range(C + 1):
                    bias_scores(b + 1, c)
                take_output(b)

            turns(dve, DB - 1, turn_of)
            scale_output(DB - 1)
            take_output(DB - 1)

        @block.scalar
        def _(act):
            def exps(b):
                act.wait_ge(max_ready, b + 1)
                since(act, e_transposed, b * C)
                since(act, step, b * 2)
                nc.scalar.activation(e[:, :], neg_s[:, :], ACT.Exp, bias=neg_max[:, :], scale=-1.0,
                                     accum_out=den[:, :]).then_inc(exp_done, 1)

            def take_exps_T(b):
                since(act, values_done, b * C)
                for c in range(C):
                    n, at = TILES_OF[c], sum(TILES_OF[:c])
                    act.wait_ge(e_transposed, b * C + (c + 1))
                    if c == C - 1:
                        nc.scalar.copy(eT_new[:, :], bank[0:DQ, 5 + c % 2, 4 * ROWS:5 * ROWS])
                    nc.scalar.copy(eT[:, at:at + n, :].rearrange("p j r -> p (j r)"),
                                   bank[:, 5 + c % 2, 0:n * ROWS]).then_inc(eT_ready, 1)

            exps(0)
            def turn_of(b):
                take_exps_T(b)
                exps(b + 1)

            turns(act, DB - 1, turn_of)
            take_exps_T(DB - 1)


PH = 8
TOPK = 16
PICKS = PH * TOPK


def mix_and_route(nc, io, sems, ident, bank, x2T, picksT):
    with ExitStack() as ctx:
        def sb(name, shape, dt=F32):
            return ctx.enter_context(nc.sbuf_tensor(name, shape, dt))

        w_out = sb("w_out_sb", [P, KD, D])
        w_q = sb("w_q_sb", [P, KD, D])
        sub_keys = sb("sub_keys_sb", [P, PH, P])
        iota = sb("iota_sb", [P, P])
        g2T = sb("g2_T", [P, KD])
        subln = sb("subln_sb", [P, 1])
        m_rows = sb("mixed_rows", [P, D])
        x_rows = sb("x_rows4", [P, D])
        sq = sb("squares4", [P, D])
        oss = sb("o_sumsq", [P, 4])
        ostd = sb("o_std", [P, 4])
        orstd = sb("o_rstd", [P, 4])
        mT = sb("mixed_T", [P, KD, P])
        h = sb("h_rows4", [P, D])
        hss = sb("h_sumsq4", [P, 1])
        hstd = sb("h_std4", [P, 1])
        hrstd = sb("h_rstd4", [P, 1])
        hT = sb("h_T", [P, KD, P])
        xr = sb("h_scaled", [P, D])
        qT = sb("peer_q_T", [P, PH, P])
        s1 = sb("key_scores", [P, 2 * PH, P])
        s2 = sb("key_scores_rest", [P, 2 * PH, P])
        best = sb("best_scores", [P, 2 * PH, TOPK])
        at = sb("best_at", [P, 2 * PH, TOPK], U32)
        at_f = sb("best_at_f", [P, 2 * PH, TOPK])
        cand = sb("cand", [P, PH, TOPK * TOPK])
        cand2 = sb("cand_rest", [P, PH, TOPK * TOPK])
        top = sb("top_scores", [P, PH, TOPK])
        top_at = sb("top_at", [P, PH, TOPK], U32)
        side = sb("top_side", [P, 2, PH, TOPK], U32)
        side_f = sb("top_side_f", [P, 2, PH, TOPK])
        onehot = sb("onehot", [P, PH, TOPK, TOPK])
        sq_o = sb("squares_o", [P, SEG])
        top_e = sb("top_exps", [P, PH, TOPK])
        gsum = sb("gate_sum", [P, PH])
        picks = sb("picks", [P, 3, PH, TOPK])
        gate = sb("gate4", [P, 24])

        weights_loaded = sems("w4_loaded")
        consts_loaded = sems("c4_loaded")
        m_loaded = sems("m_loaded")
        x_loaded = sems("x4_loaded")
        f_step = sems("front_step")
        s_step = sems("selection_step")
        subln_ready = sems("subln_ready")
        oss_ready = sems("oss_ready")
        ostd_ready = sems("ostd_ready")
        m_ready = sems("m_ready")
        mT_in_psum = sems("mT_in_psum")
        mT_ready = sems("mT_ready")
        h_in_psum = sems("h_in_psum")
        h_ready = sems("h4_ready")
        hss_ready = sems("hss_ready")
        hvar_ready = sems("hvar4_ready")
        hstd_ready = sems("hstd_ready")
        xr_ready = sems("xr_ready")
        hT_in_psum = sems("hT_in_psum")
        hT_ready = sems("hT_ready")
        hT_stored = sems("hT_stored")
        x2T_in_psum = sems("x2T_in_psum")
        x2T_ready = sems("x2T_ready")
        q_in_psum = sems("q_in_psum")
        qT_ready = sems("qT_ready")
        s_in_psum = sems("ks_in_psum")
        s_ready = sems("ks_ready")
        s_used = sems("ks_used")
        shifted = sems("top_shifted")
        exp_done = sems("top_exp_done")
        picks_ready = sems("picks_ready")
        picks_in_psum = sems("picks_in_psum")
        picksT_ready = sems("picksT_ready")

        block = ctx.enter_context(nc.Block())

        @block.sync
        def _(sp):
            sp.dma_start(g2T[:, :], io["g2"]).then_inc(consts_loaded, 16)
            sp.dma_start(subln[:, :], io["subln"]).then_inc(consts_loaded, 16)
            sp.dma_start(sub_keys[:, :, :], io["sub_keys"]).then_inc(consts_loaded, 16)
            sp.dma_start(iota[:, :], io["iota"]).then_inc(consts_loaded, 16)
            sp.dma_start(m_rows[:, :], io["mix"][0:P, :]).then_inc(m_loaded, 16)
            sp.dma_start(x_rows[:, :], io["x"][0:P, :]).then_inc(x_loaded, 16)
            sp.dma_start(w_out[:, :, :], io["w_out"].rearrange("(k p) c -> p k c", p=P)).then_inc(weights_loaded, 16)
            sp.dma_start(w_q[:, :, :], io["w_q"].rearrange("(k p) c -> p k c", p=P)).then_inc(weights_loaded, 16)
            def turn_of(t):
                sp.wait_ge(mT_in_psum, t * 2 + 2)
                sp.dma_start(m_rows[:, :], io["mix"][ds(t * P + P, P), :]).then_inc(m_loaded, 16)
                sp.wait_ge(h_ready, t + 1)
                sp.wait_ge(hT_ready, t * 2 + 2)
                sp.dma_start(x_rows[:, :], io["x"][ds(t * P + P, P), :]).then_inc(x_loaded, 16)
                sp.dma_start(io["hT"][:, :, ds(t * P, P)].rearrange("k p t -> p k t"), hT[:, :, :]).then_inc(hT_stored, 16)

            turns(sp, TILES - 1, turn_of)
            sp.wait_ge(hT_ready, 2 * TILES)
            sp.dma_start(io["hT"][:, :, (TILES - 1) * P:TP].rearrange("k p t -> p k t"), hT[:, :, :]).then_inc(hT_stored, 16)
            sp.wait_ge(hT_stored, 16 * TILES)

        @block.tensor
        def _(pe):
            def front(t):
                pe.wait_ge(m_ready, t + 1)
                since(pe, x2T_ready, t * 2)
                since(pe, hT_ready, t * 2)
                for b in range(2):
                    for j in range(4):
                        ins = nc.tensor.transpose(bank[:, b, j * P:(j + 1) * P], m_rows[:, (4 * b + j) * P:(4 * b + j + 1) * P], ident)
                    ins.then_inc(mT_in_psum, 1)
                since(pe, s_ready, t * 4)
                for k in range(KD):
                    if k % 4 == 0:
                        pe.wait_ge(mT_ready, t * 2 + k // 4 + 1)
                    for c in range(2):
                        ins = nc.tensor.matmul(bank[:, 2 + c, :], mT[:, k, :], w_out[:, k, c * 512:(c + 1) * 512],
                                               start=(k == 0), stop=(k == KD - 1))
                ins.then_inc(h_in_psum, 1)
                pe.wait_ge(h_ready, t + 1)
                for b in range(2):
                    for j in range(4):
                        ins = nc.tensor.transpose(bank[:, b, j * P:(j + 1) * P], h[:, (4 * b + j) * P:(4 * b + j + 1) * P], ident)
                    ins.then_inc(hT_in_psum, 1)
                pe.wait_ge(xr_ready, t + 1)
                for b in range(2):
                    for j in range(4):
                        ins = nc.tensor.transpose(bank[:, 4 + b, j * P:(j + 1) * P], xr[:, (4 * b + j) * P:(4 * b + j + 1) * P], ident)
                    ins.then_inc(x2T_in_psum, 1)
                since(pe, picksT_ready, t - 1)
                since(pe, qT_ready, t * 2)
                pe.wait_ge(x2T_ready, t * 2 + 2)
                for hd in range(PH):
                    for k in range(KD):
                        ins = nc.tensor.matmul(bank[:, 6 + hd // 4, (hd % 4) * P:(hd % 4 + 1) * P],
                                               w_q[:, k, hd * P:(hd + 1) * P], x2T[:, k, ds(t * P, P)],
                                               start=(k == 0), stop=(k == KD - 1))
                    if hd % 4 == 3:
                        ins.then_inc(q_in_psum, 1)
                pe.wait_ge(qT_ready, t * 2 + 2)
                for c in range(2):
                    half = slice(c * HD, (c + 1) * HD)
                    for hd in range(PH):
                        ins = nc.tensor.matmul(bank[:, 2 + 2 * c + hd // 4, (hd % 4) * P:(hd % 4 + 1) * P],
                                               qT[half, hd, :], sub_keys[half, hd, :], start=True, stop=True)
                        if hd % 4 == 3:
                            ins.then_inc(s_in_psum, 1)

            def transpose_picks(t):
                pe.wait_ge(picks_ready, t + 1)
                for j in range(3):
                    ins = nc.tensor.transpose(bank[:, 6, j * P:(j + 1) * P], picks[:, j, :, :].rearrange("p h s -> p (h s)"), ident)
                ins.then_inc(picks_in_psum, 1)

            pe.wait_ge(weights_loaded, 32)
            pe.wait_ge(consts_loaded, 64)
            front(0)
            front(1)
            transpose_picks(0)
            with pe.Fori(2, TILES) as t:
                front(t)
                transpose_picks(t - 1)
            transpose_picks(TILES - 1)

        @block.scalar
        def _(act):
            def front(t):
                act.wait_ge(oss_ready, t + 1)
                nc.scalar.activation(ostd[:, :], oss[:, :], ACT.Sqrt).then_inc(ostd_ready, 1)
                for b in range(2):
                    act.wait_ge(mT_in_psum, t * 2 + b + 1)
                    dst = mT[:, 4 * b:4 * b + 4, :].rearrange("p k t -> p (k t)")
                    if b == 0:
                        nc.scalar.activation(dst, bank[:, b, :], ACT.Copy, scale=subln[:, 0:1]).then_inc(mT_ready, 1)
                    else:
                        nc.scalar.copy(dst, bank[:, b, :]).then_inc(mT_ready, 1)
                act.wait_ge(h_ready, t + 1)
                nc.scalar.activation(sq[:, :], h[:, :], ACT.Square, accum_out=hss[:, :]).then_inc(hss_ready, 1)
                act.wait_ge(hvar_ready, t + 1)
                nc.scalar.activation(hstd[:, :], hss[:, :], ACT.Sqrt).then_inc(hstd_ready, 1)
                since(act, hT_stored, t * 16)
                for b in range(2):
                    act.wait_ge(hT_in_psum, t * 2 + b + 1)
                    nc.scalar.copy(hT[:, 4 * b:4 * b + 4, :].rearrange("p k t -> p (k t)"), bank[:, b, :]).then_inc(hT_ready, 1)
                for b in range(2):
                    act.wait_ge(q_in_psum, t * 2 + b + 1)
                    nc.scalar.copy(qT[:, 4 * b:4 * b + 4, :].rearrange("p k t -> p (k t)"), bank[:, 6 + b, :]).then_inc(qT_ready, 1)
                since(act, s_used, t)
                for g in range(4):
                    act.wait_ge(s_in_psum, t * 4 + g + 1)
                    nc.scalar.copy(s1[:, 4 * g:4 * g + 4, :].rearrange("p k t -> p (k t)"), bank[:, 2 + g, :]).then_inc(s_ready, 1)

            def selection(t):
                act.wait_ge(shifted, t + 1)
                nc.scalar.activation(top_e[:, :, :], top_e[:, :, :], ACT.Exp).then_inc(exp_done, 1)
                act.wait_ge(picks_in_psum, t + 1)
                for j in range(3):
                    ins = nc.scalar.copy(picksT[:, j, ds(t * P, P)], bank[:, 6, j * P:(j + 1) * P])
                ins.then_inc(picksT_ready, 1)

            act.wait_ge(subln_ready, 1)
            front(0)
            def turn_of(t):
                front(t + 1)
                selection(t)

            turns(act, TILES - 1, turn_of)
            selection(TILES - 1)

        @block.vector
        def _(dve):
            F_STEPS, S_STEPS = 4, 21

            def front(t, part):
                base = t * F_STEPS
                if part == 0:
                    dve.wait_ge(m_loaded, t * 16 + 16)
                    nc.vector.tensor_tensor(sq_o[:, :], m_rows[:, 0:SEG], m_rows[:, 0:SEG], ALU.mult).then_inc(f_step, 1)
                    dve.wait_ge(f_step, base + 1)
                    nc.vector.tensor_reduce(oss[:, :], sq_o[:, :].rearrange("p (h e) -> p h e", h=4), AX_X, ALU.add).then_inc(f_step, 1)
                    dve.wait_ge(f_step, base + 2)
                    nc.vector.tensor_scalar(oss[:, :], oss[:, :], 1.0 / P, EPS, ALU.mult, ALU.add).then_inc(oss_ready, 1)
                if part == 1:
                    dve.wait_ge(ostd_ready, t + 1)
                    nc.vector.reciprocal(orstd[:, :], ostd[:, :]).then_inc(f_step, 1)
                    dve.wait_ge(f_step, base + 3)
                    m4 = m_rows[:, 0:SEG].rearrange("p (h e) -> p h e", h=4)
                    nc.vector.tensor_tensor(m4, m4, orstd[:, :].unsqueeze(2).broadcast_to([P, 4, P]), ALU.mult).then_inc(m_ready, 1)
                if part == 2:
                    dve.wait_ge(h_in_psum, t + 1)
                    dve.wait_ge(x_loaded, t * 16 + 16)
                    since(dve, hT_in_psum, t * 2)
                    nc.vector.tensor_tensor(h[:, :], bank[:, 2:4, :].rearrange("p b c -> p (b c)"), x_rows[:, :], ALU.add).then_inc(h_ready, 1)
                if part == 3:
                    dve.wait_ge(hss_ready, t + 1)
                    nc.vector.tensor_scalar(hss[:, :], hss[:, :], 1.0 / D, EPS, ALU.mult, ALU.add).then_inc(hvar_ready, 1)
                    dve.wait_ge(hstd_ready, t + 1)
                    nc.vector.reciprocal(hrstd[:, :], hstd[:, :]).then_inc(f_step, 1)
                    dve.wait_ge(f_step, base + 4)
                    since(dve, x2T_in_psum, t * 2)
                    nc.vector.tensor_scalar(xr[:, :], h[:, :], hrstd[:, 0:1], None, ALU.mult).then_inc(xr_ready, 1)
                if part == 4:
                    for b in range(2):
                        dve.wait_ge(x2T_in_psum, t * 2 + b + 1)
                        nc.vector.tensor_tensor(
                            x2T[:, 4 * b:4 * b + 4, ds(t * P, P)], bank[:, 4 + b, :].rearrange("p (k t) -> p k t", k=4),
                            g2T[:, 4 * b:4 * b + 4].unsqueeze(2).broadcast_to([P, 4, P]), ALU.mult).then_inc(x2T_ready, 1)

            def top16(n, src, rest, vals, idx, s, t, last_read):
                def hold():
                    dve.wait_ge(s_step, t * S_STEPS + s.now)
                    nc.vector.memset(gate[:, s.n:s.n + 1], 0.0)

                for half in range(2):
                    part = slice(8 * half, 8 * half + 8)
                    data = rest if half else src
                    for g in range(n):
                        ins = nc.vector.max(vals[:, g, part], data[:, g, :])
                    ins.then_inc(s_step, s.up())
                    hold()
                    for g in range(n):
                        ins = nc.vector.max_index(idx[:, g, part], vals[:, g, part], data[:, g, :])
                        if not half:
                            ins = nc.vector.match_replace(rest[:, g, :], vals[:, g, part], src[:, g, :], -3e38)
                    ins.then_inc(s_step, s.up())
                    if not half:
                        hold()
                    if not half and last_read is not None:
                        dve.wait_ge(s_step, t * S_STEPS + s.now)
                        nc.vector.memset(gate[:, 21:22], 0.0).then_inc(last_read, 1)
                    yield

            def selection(t, s):
                now = lambda: t * S_STEPS + s.now
                dve.wait_ge(s_ready, t * 4 + 4)
                nc.vector.memset(gate[:, 22:23], 0.0)
                yield from top16(2 * PH, s1, s2, best, at, s, t, s_used)
                dve.wait_ge(s_step, now())
                nc.vector.tensor_copy(at_f[:, :, :], at[:, :, :]).then_inc(s_step, s.up())
                nc.vector.tensor_tensor(
                    cand[:, :, :].rearrange("p h (a b) -> p h a b", a=TOPK),
                    best[:, 0:PH, :].unsqueeze(3).broadcast_to([P, PH, TOPK, TOPK]),
                    best[:, PH:2 * PH, :].unsqueeze(2).broadcast_to([P, PH, TOPK, TOPK]), ALU.add).then_inc(s_step, s.up())
                yield
                dve.wait_ge(s_step, now())
                nc.vector.memset(gate[:, 23:24], 0.0)
                yield from top16(PH, cand, cand2, top, top_at, s, t, None)
                dve.wait_ge(s_step, now())
                since(dve, exp_done, t)
                nc.vector.tensor_tensor(top_e[:, :, :], top[:, :, :], top[:, :, 0:1].broadcast_to([P, PH, TOPK]),
                                        ALU.subtract).then_inc(shifted, 1)
                nc.vector.tensor_scalar(side[:, 0, :, :], top_at[:, :, :], 4, None, ALU.logical_shift_right).then_inc(s_step, s.up())
                nc.vector.tensor_scalar(side[:, 1, :, :], top_at[:, :, :], TOPK - 1, None, ALU.bitwise_and).then_inc(s_step, s.up())
                dve.wait_ge(s_step, now())
                nc.vector.tensor_copy(side_f[:, :, :, :].rearrange("p c h s -> p (c h s)"),
                                      side[:, :, :, :].rearrange("p c h s -> p (c h s)")).then_inc(s_step, s.up())
                since(dve, picks_in_psum, t)
                for c in range(2):
                    dve.wait_ge(s_step, now())
                    nc.vector.tensor_tensor(
                        onehot[:, :, :, :], side_f[:, c, :, :].unsqueeze(3).broadcast_to([P, PH, TOPK, TOPK]),
                        iota[:, 0:TOPK].unsqueeze(1).unsqueeze(1).broadcast_to([P, PH, TOPK, TOPK]),
                        ALU.is_equal).then_inc(s_step, s.up())
                    dve.wait_ge(s_step, now())
                    nc.vector.tensor_tensor(
                        onehot[:, :, :, :], onehot[:, :, :, :],
                        at_f[:, c * PH:(c + 1) * PH, :].unsqueeze(2).broadcast_to([P, PH, TOPK, TOPK]),
                        ALU.mult).then_inc(s_step, s.up())
                    dve.wait_ge(s_step, now())
                    nc.vector.tensor_reduce(picks[:, c, :, :], onehot[:, :, :, :], AX_X, ALU.add).then_inc(s_step, s.up())
                dve.wait_ge(exp_done, t + 1)
                nc.vector.tensor_reduce(gsum[:, :], top_e[:, :, :], AX_X, ALU.add).then_inc(s_step, s.up())
                dve.wait_ge(s_step, now())
                nc.vector.reciprocal(gsum[:, :], gsum[:, :]).then_inc(s_step, s.up())
                dve.wait_ge(s_step, now())
                nc.vector.tensor_tensor(picks[:, 2, :, :], top_e[:, :, :], gsum[:, :].unsqueeze(2).broadcast_to([P, PH, TOPK]),
                                        ALU.mult).then_inc(picks_ready, 1)
                assert s.n == S_STEPS, s.n
                yield

            dve.wait_ge(consts_loaded, 64)
            nc.vector.tensor_scalar(subln[:, :], subln[:, :], 1.0 - LAM_INIT, None, ALU.mult).then_inc(subln_ready, 1)
            for part in range(5):
                front(0, part)
            def turn_of(t):
                parts = iter(range(5))
                front(t + 1, next(parts))
                for _ in selection(t, Steps()):
                    for part in [next(parts, None)]:
                        if part is not None:
                            front(t + 1, part)

            turns(dve, TILES - 1, turn_of)
            for _ in selection(TILES - 1, Steps()):
                pass


E_GROUP = 8


def spread_gates(nc, io, sems, bank, picksT):
    with ExitStack() as ctx:
        def sb(name, shape, dt=F32):
            return ctx.enter_context(nc.sbuf_tensor(name, shape, dt))

        iota = sb("iota5", [P, P])
        row1 = [sb(f"onehot_i1_{r}", [P, E_GROUP, P]) for r in range(2)]
        row2 = [sb(f"gated_i2_{r}", [P, E_GROUP, P]) for r in range(2)]
        stage = [sb(f"stage{r}", [P, P, HD]) for r in range(2)]

        iota_loaded = sems("iota5_loaded")
        rows_ready = sems("rows_ready")
        rows_used = sems("rows_used")
        staged = sems("staged")
        stored = [sems(f"stage_stored{r}") for r in range(2)]
        PER_STAGE = HD // E_GROUP
        PER_TURN = 2 * PER_STAGE
        block = ctx.enter_context(nc.Block())

        @block.sync
        def _(sp):
            sp.dma_start(iota[:, :], io["iota"]).then_inc(iota_loaded, 16)
            def turn_of(t):
                for r in range(2):
                    sp.wait_ge(staged, t * PER_TURN + (r + 1) * PER_STAGE)
                    sp.dma_start(io["gates"][:, :, ds(t * P + r * HD, HD)], stage[r][:, :, :]).then_inc(stored[r], 16)

            turns(sp, TILES, turn_of)
            for r in range(2):
                sp.wait_ge(stored[r], 16 * TILES)

        @block.vector
        def _(dve):
            dve.wait_ge(iota_loaded, 16)
            def turn_of(t):
                for g in range(PER_TURN):
                    since(dve, rows_used, t * PER_TURN + max(0, g - 1))
                    for j in range(E_GROUP):
                        tok = ds(t * P + (g * E_GROUP + j), 1)
                        nc.vector.tensor_scalar(row1[g % 2][:, j, :], iota[:, :], picksT[:, 0, tok], None, ALU.is_equal)
                        ins = nc.vector.tensor_scalar(row2[g % 2][:, j, :], iota[:, :], picksT[:, 1, tok],
                                                      picksT[:, 2, tok], ALU.is_equal, ALU.mult)
                    ins.then_inc(rows_ready, 1)

            turns(dve, TILES, turn_of)

        @block.tensor
        def _(pe):
            def turn_of(t):
                for g in range(PER_TURN):
                    pe.wait_ge(rows_ready, t * PER_TURN + (g + 1))
                    since(pe, staged, t * PER_TURN + max(0, g - 3))
                    for j in range(E_GROUP):
                        ins = nc.tensor.matmul(bank[:, 2 * (g % 4) + j // 4, (j % 4) * P:(j % 4 + 1) * P],
                                               row1[g % 2][:, j, :], row2[g % 2][:, j, :], start=True, stop=True)
                    ins.then_inc(rows_used, 1)

            turns(pe, TILES, turn_of)

        @block.scalar
        def _(act):
            def turn_of(t):
                for g in range(PER_TURN):
                    r, at = g // PER_STAGE, g % PER_STAGE * E_GROUP
                    act.wait_ge(rows_used, t * PER_TURN + (g + 1))
                    if at == 0:
                        since(act, stored[r], t * 16)
                    src = bank[:, 2 * (g % 4):2 * (g % 4) + 2, :].rearrange("p b (t i) -> p i (b t)", i=P)
                    nc.scalar.copy(stage[r][:, :, at:at + E_GROUP], src).then_inc(staged, 1)

            turns(act, TILES, turn_of)


BLK = 4
SUPER = P // BLK
TC = 3
CH = NT // TC


def run_experts(nc, io, sems, bank, x2T):
    with ExitStack() as ctx:
        def sb(name, shape, dt=F32):
            return ctx.enter_context(nc.sbuf_tensor(name, shape, dt))

        yT = sb("y_T", [P, KD, NT])
        u = [sb(f"u{j}", [P, KD, P]) for j in range(BLK)]
        g = [sb(f"gates{j}", [P, NT]) for j in range(BLK)]
        v = [sb(f"v_sup{r}", [P, BLK, D]) for r in range(2)]
        coef = [sb(f"coef{r}", [P, BLK, NT]) for r in range(2)]
        act_out = [sb(f"gelu{r}", [P, NT]) for r in range(2)]

        u_loaded = [sems(f"u_loaded{j}") for j in range(BLK)]
        g_loaded = [sems(f"g_loaded{j}") for j in range(BLK)]
        v_loaded = [sems(f"v_sup_loaded{r}") for r in range(2)]
        h_loaded = sems("h5_loaded")
        a_in_psum = sems("a_in_psum")
        gelu_done = sems("gelu_done")
        coef_ready = sems("coef_ready")
        y_in_psum = sems("y_in_psum")
        y_added = sems("y_added")
        y_stored = sems("y_stored")
        window_moved = sems("window_moved")
        AN, YN = BLK * TC, KD * TC

        block = ctx.enter_context(nc.Block())

        def pipeline(eng, a_part, y_part):
            a_part(0, 0)
            a_part(1, 1)
            y_part(0, 0)
            with eng.Fori(1, SUPER // 2) as m:
                a_part(m * 2, 0)
                y_part(m * 2 - 1, 1)
                a_part(m * 2 + 1, 1)
                y_part(m * 2, 0)
            y_part(SUPER - 1, 1)

        @block.sync
        def _(sp):
            sp.dma_start(yT[:, :, :], io["hT"][:, :, 0:NT].rearrange("k p t -> p k t")).then_inc(h_loaded, 16)

            def load(s, r):
                for j in range(BLK):
                    i2 = s * BLK + j
                    since(sp, a_in_psum, s * AN + (j + 1) * TC - AN)
                    sp.dma_start(u[j][:, :, :], io["u"][ds(i2, 1), :, :].rearrange("a p (k e) -> (a p) k e", e=P)).then_inc(u_loaded[j], 16)
                    since(sp, coef_ready, s * BLK + (j + 1 - BLK))
                    sp.dma_start(g[j][:, :], io["gates"][:, ds(i2, 1), 0:NT].rearrange("p a t -> p (a t)")).then_inc(g_loaded[j], 16)
                since(sp, y_in_psum, s * YN - YN)
                sp.dma_start(v[r][:, :, :], io["v"][:, ds(s * BLK, BLK), :]).then_inc(v_loaded[r], 16)

            pipeline(sp, load, lambda s, r: None)
            for k in range(KD):
                sp.wait_ge(y_added, SUPER * YN - (KD - 1 - k) * TC)
                sp.dma_start(io["yT"][k, :, :], yT[:, k, :]).then_inc(y_stored, 16)
            sp.wait_ge(y_stored, 16 * KD)

        @block.gpsimd
        def _(pool):
            move = (STATE - DQ) * SEG
            rows = (DB, STATE * SEG)
            n = 0
            for state, out, new in (("state_k", "win_k_out", "kb"), ("state_v", "win_v_out", "vb")):
                src, dst = (io[x].rearrange("b s c -> b (s c)") for x in (state, out))
                pool.dma_start(dst[:, move:], io[new][SEQ:NT, :].rearrange("(b q) c -> b (q c)", q=DQ)).then_inc(window_moved, 16)
                for b in range(DB):
                    n += 1
                    pool.wait_ge(window_moved, 16 * n)
                    pool.dma_start(dst[b, 0:move].rearrange("(a c) -> a c", a=64),
                                   src[b, DQ * SEG:].rearrange("(a c) -> a c", a=64)).then_inc(window_moved, 16)
                n += 1
                pool.wait_ge(window_moved, 16 * n)

        @block.tensor
        def _(pe):
            def activations(s, r):
                for j in range(BLK):
                    pe.wait_ge(u_loaded[j], s * 16 + 16)
                    for c in range(TC):
                        n = j * TC + c
                        since(pe, gelu_done, s * AN + (n - 3))
                        for k in range(KD):
                            ins = nc.tensor.matmul(bank[:, n % 4, 0:CH], u[j][:, k, :], x2T[:, k, c * CH:(c + 1) * CH],
                                                   start=(k == 0), stop=(k == KD - 1))
                        ins.then_inc(a_in_psum, 1)

            def outputs(s, r):
                half = s // 2 if isinstance(s, int) else None
                pe.wait_ge(coef_ready, s * BLK + BLK)
                pe.wait_ge(v_loaded[r], 16 * (s // 2 + 1) if isinstance(s, int) else (s - r) * 8 + 16)
                for n in range(YN):
                    k, c = n // TC, n % TC
                    since(pe, y_added, s * YN + (n - 3))
                    for j in range(BLK):
                        ins = nc.tensor.matmul(bank[:, 4 + n % 4, 0:CH], v[r][:, j, k * P:(k + 1) * P],
                                               coef[r][:, j, c * CH:(c + 1) * CH], start=(j == 0), stop=(j == BLK - 1))
                    ins.then_inc(y_in_psum, 1)

            pipeline(pe, activations, outputs)

        @block.scalar
        def _(act):
            def gelus(s, r):
                for j in range(BLK):
                    since(act, coef_ready, s * BLK + (j - 1))
                    for c in range(TC):
                        n = j * TC + c
                        act.wait_ge(a_in_psum, s * AN + (n + 1))
                        nc.scalar.activation(act_out[j % 2][:, c * CH:(c + 1) * CH], bank[:, n % 4, 0:CH], ACT.Gelu).then_inc(gelu_done, 1)

            pipeline(act, gelus, lambda s, r: None)

        @block.vector
        def _(dve):
            def weigh(s, r):
                since(dve, y_in_psum, s * YN - YN)
                for j in range(BLK):
                    dve.wait_ge(gelu_done, s * AN + (j + 1) * TC)
                    dve.wait_ge(g_loaded[j], s * 16 + 16)
                    nc.vector.tensor_tensor(coef[r][:, j, :], act_out[j % 2][:, :], g[j][:, :], ALU.mult).then_inc(coef_ready, 1)

            def add(s, r):
                since(dve, y_added, s * YN)
                for n in range(YN):
                    k, c = n // TC, n % TC
                    dve.wait_ge(y_in_psum, s * YN + (n + 1))
                    out = yT[:, k, c * CH:(c + 1) * CH]
                    nc.vector.tensor_tensor(out, out, bank[:, 4 + n % 4, 0:CH], ALU.add).then_inc(y_added, 1)

            dve.wait_ge(h_loaded, 16)
            pipeline(dve, weigh, add)


def build(nc, io, phases=9):
    with ExitStack() as ctx:
        bank = ctx.enter_context(nc.psum_tensor("banks", [P, 8, 512], F32))
        ident = ctx.enter_context(nc.sbuf_tensor("ident", [P, P], F32))[:, :]
        neg_lam = ctx.enter_context(nc.sbuf_tensor("neg_lambda", [P, 1], F32))[:, :]

        def phase(run, *args):
            own = []

            def sems(name):
                own.append(nc.alloc_semaphore(name=name))
                return own[-1]

            run(nc, io, sems, *args)
            nc.clear_and_free_semaphores(own)
            nc.all_engine_barrier()

        phase(load_constants, ident)
        phase(project, ident, bank)
        if phases >= 2:
            phase(lambda_column, neg_lam)
            phase(attend_prompt, ident, bank, neg_lam, "a")
            phase(attend_prompt, ident, bank, neg_lam, "b")
        if phases >= 3:
            phase(attend_sample, ident, bank, neg_lam, "a")
            phase(attend_sample, ident, bank, neg_lam, "b")
        if phases >= 4:
            x2T = ctx.enter_context(nc.sbuf_tensor("x2_T", [P, KD, TP], F32))
            with nc.sbuf_tensor("picks_T", [P, 3, TP], F32) as picksT:
                phase(mix_and_route, ident, bank, x2T, picksT)
                phase(spread_gates, bank, picksT)
        if phases >= 5:
            phase(run_experts, bank, x2T)


def slopes(n):
    return 2.0 ** (-8.0 * np.arange(1, n + 1) / n)


def log_branches(d):
    count = sum(((d >= 0) & (d <= w) & (d % dil == 0)).astype(np.int64) for w, dil in DILATIONS)
    return np.where(count > 0, np.log(np.maximum(count, 1).astype(np.float64)), NEG)


def shape_constants():
    d = np.arange(P)[:, None] + (SEQ - P) - np.arange(SEQ)[None, :]
    strips = [np.where(d >= 0, -s * d, NEG) for s in slopes(4)]
    strips += [np.where(log_branches(d) > NEG / 2, log_branches(d) - s * d, NEG) for s in slopes(8)]
    row_q = np.tile(np.arange(DQ), 8)
    new = np.arange(DQ)
    pos_a = np.concatenate([np.arange(PAST), PAST + new])
    da = PAST + row_q[:, None] - pos_a[None, :]
    bias_a = np.where(da >= 0, -np.repeat(slopes(4), 8)[:, None] * da, NEG)
    pos_b = np.concatenate([state_rows(), STATE + new])
    db = STATE + row_q[:, None] - pos_b[None, :]
    bias_b = np.where(log_branches(db) > NEG / 2, log_branches(db) - np.repeat(slopes(8), DQ)[:, None] * db, NEG)
    sel_a = np.zeros((32, 4, DQ))
    sel_b = np.zeros((32, 8, DQ))
    for r in range(32):
        sel_a[r, r // 8, r % DQ] = 1
        sel_b[r, r // DQ, r % DQ] = 1
    second_map = (np.arange(32) // DQ % 2).astype(np.float64)[:, None]
    out = {"ident": np.eye(P), "strips": np.stack(strips), "bias_a": bias_a, "bias_b": bias_b,
           "sel_a": sel_a, "sel_b": sel_b, "second_map": second_map,
           "iota": np.broadcast_to(np.arange(P), (P, P))}
    return {k: np.ascontiguousarray(v, dtype=np.float32) for k, v in out.items()}


def state_rows():
    far = STATE - DILATIONS[1][0]
    step = DILATIONS[2][1]
    return np.concatenate([(np.arange(0, far, step)[:, None] + np.arange(DQ)[None, :]).ravel(),
                           np.arange(far, STATE)])


def lay_out(inp):
    a = {k: np.asarray(v) for k, v in inp.items()}
    c = np.ascontiguousarray
    n_phys = a["cache_a_k"].shape[1]
    x = np.zeros((TP, D), np.float32)
    x[0:SEQ] = a["x_prompt"].reshape(SEQ, D)
    x[SEQ:NT] = a["x_sample"].reshape(NS, D)
    rows = state_rows()
    tiles_b = len(rows) // P
    kb = a["state_b_k"][0][:, rows].reshape(DB, tiles_b, P, 4, P)
    vb = a["state_b_v"][0][:, rows].reshape(DB, tiles_b, P, SEG)
    m = {
        "x": x,
        "g1": c(a["norm1_g"].reshape(KD, P).T), "g2": c(a["norm2_g"].reshape(KD, P).T),
        "w_in": a["w_in"][0], "w_out": a["w_out"][0], "w_q": a["peer_wq"][0],
        "qk_gain": np.concatenate([a["qnorm_a"], a["knorm_a"], a["qnorm_b"], a["knorm_b"]]),
        "lams": np.concatenate([a["lambda_q1"], a["lambda_k1"], a["lambda_q2"], a["lambda_k2"]]),
        "subln": c(a["subln_g"].reshape(P, 1)),
        "cache_k": c(a["cache_a_k"][0].reshape(n_phys, P, 4, P).transpose(0, 3, 2, 1)).reshape(n_phys, P, SEG),
        "cache_v": a["cache_a_v"][0].reshape(n_phys, P, SEG),
        "page_table": a["page_table"].reshape(1, -1),
        "win_k": c(kb.transpose(0, 4, 1, 3, 2)).reshape(DB, P, tiles_b * SEG),
        "win_v": c(vb.transpose(0, 2, 1, 3)).reshape(DB, P, tiles_b * SEG),
        "state_k": a["state_b_k"].reshape(DB, STATE, SEG), "state_v": a["state_b_v"].reshape(DB, STATE, SEG),
        "sub_keys": c(a["peer_subkeys"][0].transpose(1, 3, 0, 2)).reshape(P, 8, P),
        "u": c(a["peer_u"][0].reshape(P, P, KD, P).transpose(1, 3, 2, 0)).reshape(P, P, KD * P),
        "v": a["peer_v"][0].reshape(P, P, D),
    }
    m.update(shape_constants())
    return m


OUTS = {"ka": (TP, SEG), "va": (TP, SEG), "kb": (TP, SEG), "vb": (TP, SEG),
        "win_k_out": (DB, STATE, SEG), "win_v_out": (DB, STATE, SEG), "yT": (KD, P, NT)}
SCRATCH = {"qkT": (16, P, TP), "mix": (TP, D), "gates": (P, P, TP), "hT": (KD, P, TP)}


def kernel(**inputs):
    import concourse.bacc as bacc
    from concourse.bass_utils import run_bass_kernel_spmd as run

    nc = bacc.Bacc("TRN2", target_bir_lowering=False, num_devices=1)
    arrays = lay_out(inputs)
    io = {}
    for name, arr in arrays.items():
        io[name] = nc.dram_tensor(f"in_{name}", arr.shape, mybir.dt.from_np(arr.dtype), kind="ExternalInput").ap()
    for name, shape in OUTS.items():
        io[name] = nc.dram_tensor(f"out_{name}", shape, F32, kind="ExternalOutput").ap()
    for name, shape in SCRATCH.items():
        io[name] = nc.dram_tensor(f"scratch_{name}", shape, F32).ap()
    build(nc, io)
    got = run(nc, [{f"in_{k}": v for k, v in arrays.items()}], core_ids=[0]).results[0]
    o = {name: np.asarray(got[f"out_{name}"]) for name in OUTS}
    y = o["yT"].reshape(D, NT).T
    new = lambda name, width: (o[name][:SEQ].reshape(1, 1, SEQ, -1, width),
                               o[name][SEQ:NT].reshape(1, DB, DQ, -1, width))
    (kap, kas), (vap, vas) = new("ka", P), new("va", P)
    (kbp, _), (vbp, _) = new("kb", HD), new("vb", HD)
    window = (1, DB, STATE, 8, HD)
    return (y[:SEQ].reshape(1, SEQ, D), y[SEQ:].reshape(DB, DQ, D), kap, vap, kas, vas,
            kbp, vbp, o["win_k_out"].reshape(window), o["win_v_out"].reshape(window))
```

```python
from contextlib import ExitStack

import numpy as np
import concourse.bass as bass
from concourse import mybir

F32 = mybir.dt.float32
F32R = mybir.dt.float32r
I32 = mybir.dt.int32
U32 = mybir.dt.uint32
ALU = mybir.AluOpType
ACT = mybir.ActivationFunctionType
AX_X = mybir.AxisListType.X

P = 128
D = 1024
KD = D // P
SEQ = 1024
DB, DQ = 8, 4
NS = DB * DQ
NT = SEQ + NS
TILES = -(-NT // P)
TP = TILES * P
COLS = 3072
SEG = 512
NSEG = COLS // SEG
HD = 64
EPS = 1e-6
NEG = -1e30
PAST, PAGE, STATE = 4096, 128, 2048
PAGES = PAST // PAGE
LAM_INIT = 0.8 - 0.6
DILATIONS = ((128, 1), (512, 4), (2048, 16))
ds = bass.ds


def since(eng, sem, value):
    if not isinstance(value, int) or value > 0:
        eng.wait_ge(sem, value)


def turns(eng, n, body):
    body(0)
    with eng.Fori(1, n) as i:
        body(i)


class Steps:

    def __init__(self, base=0):
        self.base, self.n = base, 0

    def up(self):
        self.n += 1
        return 1

    @property
    def now(self):
        return self.base + self.n


def load_constants(nc, io, sems, ident):
    ident_loaded = sems("ident_loaded")
    pad_zeroed = sems("pad_zeroed")
    with nc.Block() as block:
        @block.sync
        def _(sp):
            sp.dma_start(ident, io["ident"]).then_inc(ident_loaded, 16)
            sp.dma_start(io["mix"][NT:TP, :], io["x"][NT:TP, :]).then_inc(pad_zeroed, 16)
            sp.wait_ge(ident_loaded, 16)
            sp.wait_ge(pad_zeroed, 16)


def project(nc, io, sems, ident, bank):
    with ExitStack() as ctx:
        def sb(name, shape, dt=F32):
            return ctx.enter_context(nc.sbuf_tensor(name, shape, dt))

        w = sb("w_in_sb", [P, KD, COLS])
        x_rows = sb("x_rows", [P, TILES, D])
        xs = sb("x_scaled", [P, D])
        xnT = sb("xn_T", [P, KD, P])
        h = sb("h_rows", [P, COLS])
        hn = sb("h_normed", [P, 4 * SEG])
        sq = sb("squares", [P, 4 * SEG])
        qkT = sb("qk_T", [P, 16, P])
        g1T = sb("g1_T", [P, KD])
        gain = sb("qk_gain", [P, 4, HD])
        ss = sb("x_sumsq", [P, TILES])
        std = sb("x_std", [P, TILES])
        rstd = sb("x_rstd", [P, TILES])
        hss = sb("h_sumsq", [P, 32])
        hstd = sb("h_std", [P, 32])
        hrstd = sb("h_rstd", [P, 32])

        w_loaded = [sems(f"w_loaded{k}") for k in range(KD)]
        gains_loaded = sems("p_gains_loaded")
        x_loaded = sems("x_loaded")
        step = sems("p_dve_step")
        x_squared = sems("x_squared")
        x_var_ready = sems("x_var_ready")
        x_std_ready = sems("x_std_ready")
        xs_ready = sems("xs_ready")
        xT_in_psum = sems("xT_in_psum")
        xnT_ready = sems("xnT_ready")
        xnT_used = sems("xnT_used")
        h_var_ready = sems("h_var_ready")
        h_std_ready = sems("h_std_ready")
        h_dve = sems("h_evac_dve")
        h_act = sems("h_evac_act")
        hn_ready = sems("hn_ready")
        qkT_in_psum = sems("qkT_in_psum")
        qkT_ready = sems("qkT_ready")
        rows_stored = sems("rows_stored")
        qkT_stored = sems("qkT_stored")

        h2 = h[:, :].rearrange("p (a c) -> p a c", a=2)[:, :, 0:2 * SEG]
        hn2 = hn[:, :].rearrange("p (a c) -> p a c", a=2)
        sq2 = sq[:, :].rearrange("p (a c) -> p a c", a=2)
        DVE_STEPS = 5

        block = ctx.enter_context(nc.Block())

        @block.sync
        def _(sp):
            sp.dma_start(x_rows[:, :, :], io["x"].rearrange("(t p) d -> p t d", p=P)).then_inc(x_loaded, 16)
            sp.dma_start(g1T[:, :], io["g1"]).then_inc(gains_loaded, 16)
            sp.dma_start(gain[:, :, :], io["qk_gain"].partition_broadcast(P)).then_inc(gains_loaded, 16)
            for k in range(KD):
                sp.dma_start(w[:, k, :], io["w_in"][k * P:(k + 1) * P, :]).then_inc(w_loaded[k], 16)
            def turn_of(t):
                r = ds(t * P, P)
                sp.wait_ge(hn_ready, t + 1)
                sp.wait_ge(qkT_ready, t * 4 + 4)
                sp.wait_ge(h_act, t * 3 + 3)
                sp.dma_start(io["ka"][r, :], hn[:, SEG:2 * SEG]).then_inc(rows_stored, 16)
                sp.dma_start(io["va"][r, :], h[:, 2 * SEG:3 * SEG]).then_inc(rows_stored, 16)
                sp.dma_start(io["kb"][r, :], hn[:, 3 * SEG:4 * SEG]).then_inc(rows_stored, 16)
                sp.dma_start(io["vb"][r, :], h[:, 5 * SEG:6 * SEG]).then_inc(rows_stored, 16)
                sp.dma_start(io["qkT"][:, :, ds(t * P, P)].rearrange("b p t -> p b t"), qkT[:, :, :]).then_inc(qkT_stored, 16)

            turns(sp, TILES, turn_of)
            sp.wait_ge(rows_stored, 64 * TILES)
            sp.wait_ge(qkT_stored, 16 * TILES)

        @block.vector
        def _(dve):
            dve.wait_ge(gains_loaded, 32)
            for seg in (0, 2):
                nc.vector.tensor_scalar(gain[:, seg, :], gain[:, seg, :], HD ** -0.5, None, ALU.mult).then_inc(step, 1)
            dve.wait_ge(x_squared, TILES)
            nc.vector.tensor_scalar(ss[:, :], ss[:, :], 1.0 / D, EPS, ALU.mult, ALU.add).then_inc(x_var_ready, 1)
            dve.wait_ge(x_std_ready, 1)
            nc.vector.reciprocal(rstd[:, :], std[:, :]).then_inc(step, 1)
            dve.wait_ge(step, 3)

            def scale_rows(t):
                nc.vector.tensor_scalar(xs[:, :], x_rows[:, ds(t, 1), :].rearrange("p a d -> p (a d)"),
                                        rstd[:, ds(t, 1)], None, ALU.mult).then_inc(xs_ready, 1)

            def gain_xT(t):
                since(dve, xnT_used, t * 2)
                for b in range(2):
                    dve.wait_ge(xT_in_psum, t * 2 + b + 1)
                    nc.vector.tensor_tensor(
                        xnT[:, 4 * b:4 * b + 4, :], bank[:, 6 + b, :].rearrange("p (k t) -> p k t", k=4),
                        g1T[:, 4 * b:4 * b + 4].unsqueeze(2).broadcast_to([P, 4, P]), ALU.mult).then_inc(xnT_ready, 1)

            def norm_qk(t):
                s = Steps(t * DVE_STEPS + 3)
                dve.wait_ge(xnT_used, t * 2 + 2)
                since(dve, hn_ready, t)
                for c in (0, 1, 3):
                    nc.vector.tensor_copy(h[:, c * SEG:(c + 1) * SEG], bank[:, c, :]).then_inc(h_dve, 1)
                dve.wait_ge(h_dve, t * 3 + 3)
                dve.wait_ge(h_act, t * 3 + 1)
                nc.vector.tensor_tensor(sq2, h2, h2, ALU.mult).then_inc(step, s.up())
                dve.wait_ge(step, s.now)
                nc.vector.tensor_reduce(hss[:, :], sq[:, :].rearrange("p (g d) -> p g d", d=HD), AX_X,
                                        ALU.add).then_inc(step, s.up())
                dve.wait_ge(step, s.now)
                nc.vector.tensor_scalar(hss[:, :], hss[:, :], 1.0 / HD, EPS, ALU.mult, ALU.add).then_inc(h_var_ready, 1)
                dve.wait_ge(h_std_ready, t + 1)
                nc.vector.reciprocal(hrstd[:, :], hstd[:, :]).then_inc(step, s.up())
                dve.wait_ge(step, s.now)
                since(dve, rows_stored, t * 64)
                since(dve, qkT_in_psum, t * 4)
                for a in range(2):
                    nc.vector.tensor_tensor(
                        hn2[:, a, :].rearrange("p (g d) -> p g d", d=HD), h2[:, a, :].rearrange("p (g d) -> p g d", d=HD),
                        hrstd[:, 16 * a:16 * a + 16].unsqueeze(2).broadcast_to([P, 16, HD]),
                        ALU.mult).then_inc(step, s.up())
                dve.wait_ge(step, s.now)
                assert s.n == DVE_STEPS
                for seg in range(4):
                    hs = hn[:, seg * SEG:(seg + 1) * SEG].rearrange("p (g d) -> p g d", d=HD)
                    ins = nc.vector.tensor_tensor(hs, hs, gain[:, seg, :].unsqueeze(1).broadcast_to([P, 8, HD]), ALU.mult)
                ins.then_inc(hn_ready, 1)

            scale_rows(0)
            gain_xT(0)
            def turn_of(t):
                scale_rows(t + 1)
                gain_xT(t + 1)
                norm_qk(t)

            turns(dve, TILES - 1, turn_of)
            norm_qk(TILES - 1)

        @block.scalar
        def _(act):
            act.wait_ge(x_loaded, 16)
            for t in range(TILES):
                if t:
                    since(act, x_squared, t)
                nc.scalar.activation(sq[:, 0:D], x_rows[:, t, :], ACT.Square,
                                     accum_out=ss[:, t:t + 1]).then_inc(x_squared, 1)
            act.wait_ge(x_var_ready, 1)
            nc.scalar.activation(std[:, :], ss[:, :], ACT.Sqrt).then_inc(x_std_ready, 1)
            def turn_of(t):
                act.wait_ge(xnT_used, t * 2 + 2)
                since(act, rows_stored, t * 64)
                since(act, hn_ready, t)
                for c in (4, 2, 5):
                    nc.scalar.copy(h[:, c * SEG:(c + 1) * SEG], bank[:, c, :]).then_inc(h_act, 1)
                act.wait_ge(h_var_ready, t + 1)
                nc.scalar.activation(hstd[:, :], hss[:, :], ACT.Sqrt).then_inc(h_std_ready, 1)
                since(act, qkT_stored, t * 16)
                for g in range(4):
                    act.wait_ge(qkT_in_psum, t * 4 + g + 1)
                    nc.scalar.copy(qkT[:, 4 * g:4 * g + 4, :].rearrange("p k t -> p (k t)"),
                                   bank[:, 6 + g % 2, :]).then_inc(qkT_ready, 1)

            turns(act, TILES, turn_of)

        @block.tensor
        def _(pe):
            def transpose_x(t):
                pe.wait_ge(xs_ready, t + 1)
                if not (isinstance(t, int) and t == 0):
                    pe.wait_ge(qkT_ready, t * 4 - 4)
                for b in range(2):
                    for j in range(4):
                        k = 4 * b + j
                        ins = nc.tensor.transpose(bank[:, 6 + b, j * P:(j + 1) * P], xs[:, k * P:(k + 1) * P], ident)
                    ins.then_inc(xT_in_psum, 1)

            def products(t, ks):
                for k in ks:
                    if k == 0:
                        since(pe, h_dve, t * 3)
                        since(pe, h_act, t * 3)
                    if k % 4 == 0:
                        pe.wait_ge(xnT_ready, t * 2 + k // 4 + 1)
                    pe.wait_ge(w_loaded[k], 16)
                    for c in range(NSEG):
                        ins = nc.tensor.matmul(bank[:, c, :], xnT[:, k, :], w[:, k, c * SEG:(c + 1) * SEG],
                                               start=(k == 0), stop=(k == KD - 1))
                    if k % 4 == 3:
                        ins.then_inc(xnT_used, 1)

            def transpose_qk(t):
                pe.wait_ge(hn_ready, t + 1)
                for g in range(4):
                    if g >= 2:
                        pe.wait_ge(qkT_ready, t * 4 + g - 1)
                    for j in range(4):
                        c = 4 * g + j
                        ins = nc.tensor.transpose(bank[:, 6 + g % 2, j * P:(j + 1) * P], hn[:, c * P:(c + 1) * P], ident)
                    ins.then_inc(qkT_in_psum, 1)

            transpose_x(0)
            products(0, range(7))
            transpose_x(1)
            products(0, [7])
            with pe.Fori(1, TILES - 1) as t:
                products(t, range(4))
                pe.wait_ge(xnT_ready, t * 2 + 2)
                transpose_qk(t - 1)
                products(t, range(4, 7))
                transpose_x(t + 1)
                products(t, [7])
            products(TILES - 1, range(4))
            pe.wait_ge(xnT_ready, 2 * TILES)
            transpose_qk(TILES - 2)
            products(TILES - 1, range(4, 8))
            transpose_qk(TILES - 1)


UNITS = 4
QT = SEQ // P
NB = 2


def lambda_column(nc, io, sems, out):
    with ExitStack() as ctx:
        def sb(name, shape):
            return ctx.enter_context(nc.sbuf_tensor(name, shape, F32))

        lams = sb("lams", [P, 2, 2, HD])
        prod = sb("lam_prod", [P, 2, HD])
        dots = sb("lam_dots", [P, 2])
        exps = sb("lam_exps", [P, 2])
        diff = sb("lam_diff", [P, 1])
        lams_loaded = sems("lams_loaded")
        step = sems("lam_step")
        dots_ready = sems("lam_dots_ready")
        exps_ready = sems("lam_exps_ready")
        with nc.Block() as block:
            @block.sync
            def _(sp):
                sp.dma_start(lams[:, :, :, :].rearrange("p a b d -> p (a b) d"),
                             io["lams"].partition_broadcast(P)).then_inc(lams_loaded, 16)

            @block.vector
            def _(dve):
                dve.wait_ge(lams_loaded, 16)
                nc.vector.tensor_tensor(prod[:, :, :], lams[:, :, 0, :], lams[:, :, 1, :], ALU.mult).then_inc(step, 1)
                dve.wait_ge(step, 1)
                nc.vector.tensor_reduce(dots[:, :], prod[:, :, :], AX_X, ALU.add).then_inc(dots_ready, 1)
                dve.wait_ge(exps_ready, 1)
                nc.vector.tensor_tensor(diff[:, :], exps[:, 1:2], exps[:, 0:1], ALU.subtract).then_inc(step, 1)
                dve.wait_ge(step, 2)
                nc.vector.tensor_scalar(out, diff[:, :], -LAM_INIT, None, ALU.add).then_inc(step, 1)
                dve.wait_ge(step, 3)

            @block.scalar
            def _(act):
                act.wait_ge(dots_ready, 1)
                nc.scalar.activation(exps[:, :], dots[:, :], ACT.Exp).then_inc(exps_ready, 1)


def attend_prompt(nc, io, sems, ident, bank, neg_lam, mixer):
    a = mixer == "a"
    with ExitStack() as ctx:
        def sb(name, shape, dt=F32):
            return ctx.enter_context(nc.sbuf_tensor(f"{name}_{mixer}", shape, dt))

        def sem(name):
            return sems(f"{name}_{mixer}")

        MW = 1 if a else 2
        q = [sb(f"q{u}", [HD, 2, SEQ]) for u in range(NB)]
        k = [sb(f"k{u}", [HD, 2, SEQ]) for u in range(NB)]
        v = [sb(f"v{u}", [P, QT, P]) for u in range(NB)]
        strip = [sb(f"strip{u}", [P, MW, SEQ]) for u in range(NB)]
        neg_s = sb("neg_scores", [P, 2, SEQ])
        e = sb("exps", [P, 2, 2, SEQ])
        w = sb("weights", [P, 2, 1, SEQ]) if a else e
        wT = sb("weights_T", [P, 2, MW, QT, P])
        neg_max = sb("neg_max", [P, 2, 2])
        den = sb("den", [P, 2, 2])
        rden = sb("rden", [P, 2, 2])
        r2 = sb("r2", [P, 2])
        o = sb("o", [P, 2, P])
        gate = sb("gate", [P, 2 * NB * QT])

        loaded = [sem(f"pr_loaded{u}") for u in range(NB)]
        s_in_psum = sem("s_in_psum")
        s_biased = sem("s_biased")
        exp_done = sem("exp_done")
        step = sem("pr_step")
        w_ready = sem("w_ready")
        wT_in_psum = sem("wT_in_psum")
        wT_ready = sem("wT_ready")
        o_in_psum = sem("o_in_psum")
        o_ready = sem("o_ready")
        o_stored = [sem(f"o_stored{par}") for par in range(2)]

        TURNS = UNITS // NB
        TURN_TILES = NB * QT
        GROUPS = [-(-(i + 1) // 4) for i in range(QT)]
        TURN_GROUPS = NB * MW * sum(GROUPS)
        first_q, first_k = (0, 4) if a else (8, 12)
        v_rows = io["va"] if a else io["vb"]

        def group_at(n):
            return MW * (n // QT * sum(GROUPS) + sum(GROUPS[:n % QT]))

        block = ctx.enter_context(nc.Block())

        @block.sync
        def _(sp):
            def turn_of(turn):
                for u in range(NB):
                    since(sp, o_ready, turn * TURN_TILES)
                    qt = io["qkT"][ds(turn * NB + (first_q + u), 1), :, 0:SEQ]
                    sp.dma_start(q[u][:, :, :], qt.rearrange("a (m d) t -> d (a m) t", m=2)).then_inc(loaded[u], 16)
                    kt = io["qkT"][ds(turn * NB + (first_k + u), 1), :, 0:SEQ]
                    sp.dma_start(k[u][:, :, :], kt.rearrange("a (m d) t -> d (a m) t", m=2)).then_inc(loaded[u], 16)
                    vt = v_rows[0:SEQ, ds(turn * (NB * P) + u * P, P)]
                    sp.dma_start(v[u][:, :, :], vt.rearrange("(j p) e -> p j e", p=P)).then_inc(loaded[u], 16)
                    st = io["strips"][ds(turn * (NB * MW) + (u * MW + (0 if a else 4)), MW), :, :]
                    sp.dma_start(strip[u][:, :, :], st.rearrange("m p c -> p m c")).then_inc(loaded[u], 16)
                for n in range(TURN_TILES):
                    u, i = n // QT, n % QT
                    sp.wait_ge(o_ready, turn * TURN_TILES + (n + 1))
                    sp.dma_start(io["mix"][i * P:(i + 1) * P, ds(turn * (NB * P) + ((0 if a else SEG) + u * P), P)],
                                 o[:, n % 2, :]).then_inc(o_stored[n % 2], 16)

            turns(sp, TURNS, turn_of)
            for par in range(2):
                sp.wait_ge(o_stored[par], 8 * UNITS * QT)

        @block.tensor
        def _(pe):
            def scores(turn, n):
                u, i = n // QT, n % QT
                for m in range(2):
                    since(pe, s_biased, turn * (2 * TURN_TILES) + max(0, 2 * n + m - 1))
                    for c in range(0, (i + 1) * P, 512):
                        width = min(512, (i + 1) * P - c)
                        ins = nc.tensor.matmul(bank[:, 2 * m + c // 512, 0:width], q[u][:, m, i * P:(i + 1) * P],
                                               k[u][:, m, c:c + width], start=True, stop=True)
                    ins.then_inc(s_in_psum, 1)

            def transpose_weights(turn, n):
                i = n % QT
                g = group_at(n)
                if a:
                    pe.wait_ge(w_ready, turn * TURN_TILES + (n + 1))
                for mw in range(MW):
                    if not a:
                        pe.wait_ge(exp_done, turn * (2 * TURN_TILES) + (2 * n + mw + 1))
                    for j0 in range(0, i + 1, 4):
                        since(pe, wT_ready, turn * TURN_GROUPS + max(0, g - 1))
                        for j in range(j0, min(j0 + 4, i + 1)):
                            ins = nc.tensor.transpose(bank[:, 4 + g % 2, (j - j0) * P:(j - j0 + 1) * P],
                                                      w[:, n % 2, mw, j * P:(j + 1) * P], ident)
                        ins.then_inc(wT_in_psum, 1)
                        g += 1

            def weigh_values(turn, n):
                u, i = n // QT, n % QT
                since(pe, o_ready, turn * TURN_TILES + max(0, n - 1))
                width = P // MW
                for mw in range(MW):
                    pe.wait_ge(wT_ready, turn * TURN_GROUPS + (group_at(n) + (mw + 1) * GROUPS[i]))
                    for j in range(i + 1):
                        ins = nc.tensor.matmul(bank[:, 6 + n % 2, mw * width:(mw + 1) * width], wT[:, n % 2, mw, j, :],
                                               v[u][:, j, mw * width:(mw + 1) * width], start=(j == 0), stop=(j == i))
                ins.then_inc(o_in_psum, 1)

            def turn_of(turn):
                pe.wait_ge(loaded[0], turn * 64 + 64)
                scores(turn, 0)
                for n in range(TURN_TILES):
                    if n + 1 == QT:
                        pe.wait_ge(loaded[1], turn * 64 + 64)
                    if n + 1 < TURN_TILES:
                        scores(turn, n + 1)
                    transpose_weights(turn, n)
                    weigh_values(turn, n)

            turns(pe, TURNS, turn_of)

        @block.vector
        def _(dve):
            def bias(turn, n):
                u, i = n // QT, n % QT
                L = (i + 1) * P
                for m in range(2):
                    dve.wait_ge(s_in_psum, turn * (2 * TURN_TILES) + (2 * n + m + 1))
                    since(dve, exp_done, turn * (2 * TURN_TILES) + max(0, 2 * n + m - 1))
                    nc.vector.memset(gate[:, 2 * n + m:2 * n + m + 1], 0.0)
                    nc.vector.tensor_tensor_reduce(
                        neg_s[:, m, 0:L], bank[:, 2 * m:2 * m + 2, :].rearrange("p b c -> p (b c)")[:, 0:L],
                        strip[u][:, m % MW, SEQ - L:SEQ], -1.0, 3e38, ALU.add, ALU.min,
                        neg_max[:, n % 2, m:m + 1]).then_inc(s_biased, 1)

            STEPS = 3 if a else 1

            def combine(turn, n):
                i, par = n % QT, n % 2
                L = (i + 1) * P
                s = Steps(n * STEPS)
                dve.wait_ge(exp_done, turn * (2 * TURN_TILES) + (2 * n + 2))
                nc.vector.reciprocal(rden[:, par, :], den[:, par, :]).then_inc(step, s.up())
                dve.wait_ge(step, turn * (TURN_TILES * STEPS) + s.now)
                if a:
                    nc.vector.tensor_tensor(r2[:, par:par + 1], rden[:, par, 1:2], neg_lam, ALU.mult).then_inc(step, s.up())
                    dve.wait_ge(step, turn * (TURN_TILES * STEPS) + s.now)
                    nc.vector.tensor_scalar(e[:, par, 1, 0:L], e[:, par, 1, 0:L], r2[:, par:par + 1], None,
                                            ALU.mult).then_inc(step, s.up())
                    since(dve, wT_in_psum, turn * TURN_GROUPS + (group_at(n - 1) if n else 0))
                    dve.wait_ge(step, turn * (TURN_TILES * STEPS) + s.now)
                    nc.vector.scalar_tensor_tensor(w[:, par, 0, 0:L], e[:, par, 0, 0:L], rden[:, par, 0:1],
                                                   e[:, par, 1, 0:L], ALU.mult, ALU.add).then_inc(w_ready, 1)

            def output(turn, n):
                par = n % 2
                dve.wait_ge(o_in_psum, turn * TURN_TILES + (n + 1))
                since(dve, o_stored[par], turn * (8 * TURN_TILES) + 16 * (n // 2))
                if a:
                    nc.vector.tensor_copy(o[:, par, :], bank[:, 6 + par, 0:P]).then_inc(o_ready, 1)
                else:
                    for m in range(2):
                        ins = nc.vector.tensor_scalar(o[:, par, m * HD:(m + 1) * HD], bank[:, 6 + par, m * HD:(m + 1) * HD],
                                                      rden[:, par, m:m + 1], None, ALU.mult)
                    ins.then_inc(o_ready, 1)

            def turn_of(turn):
                dve.wait_ge(loaded[0], turn * 64 + 64)
                bias(turn, 0)
                for n in range(TURN_TILES):
                    combine(turn, n)
                    if n + 1 == QT:
                        dve.wait_ge(loaded[1], turn * 64 + 64)
                    if n + 1 < TURN_TILES:
                        bias(turn, n + 1)
                    output(turn, n)

            turns(dve, TURNS, turn_of)

        @block.scalar
        def _(act):
            def exps(turn, n):
                L = (n % QT + 1) * P
                if a:
                    since(act, w_ready, turn * TURN_TILES + max(0, n - 1))
                else:
                    since(act, wT_in_psum, turn * TURN_GROUPS + (group_at(n - 1) if n else 0))
                    since(act, o_ready, turn * TURN_TILES + max(0, n - 1))
                for m in range(2):
                    act.wait_ge(s_biased, turn * (2 * TURN_TILES) + (2 * n + m + 1))
                    nc.scalar.activation(e[:, n % 2, m, 0:L], neg_s[:, m, 0:L], ACT.Exp, bias=neg_max[:, n % 2, m:m + 1],
                                         scale=-1.0, accum_out=den[:, n % 2, m:m + 1]).then_inc(exp_done, 1)

            def take_weights_T(turn, n):
                i = n % QT
                g = group_at(n)
                since(act, o_in_psum, turn * TURN_TILES + max(0, n - 1))
                for mw in range(MW):
                    for j0 in range(0, i + 1, 4):
                        j1 = min(j0 + 4, i + 1)
                        act.wait_ge(wT_in_psum, turn * TURN_GROUPS + (g + 1))
                        nc.scalar.copy(wT[:, n % 2, mw, j0:j1, :].rearrange("p j t -> p (j t)"),
                                       bank[:, 4 + g % 2, 0:(j1 - j0) * P]).then_inc(wT_ready, 1)
                        g += 1

            def turn_of(turn):
                exps(turn, 0)
                for n in range(TURN_TILES):
                    take_weights_T(turn, n)
                    if n + 1 < TURN_TILES:
                        exps(turn, n + 1)

            turns(act, TURNS, turn_of)


PR = P // 4


def attend_sample(nc, io, sems, ident, bank, neg_lam, mixer):
    a = mixer == "a"
    with ExitStack() as ctx:
        def sb(name, shape, dt=F32):
            return ctx.enter_context(nc.sbuf_tensor(f"{name}_s{mixer}", shape, dt))

        def sem(name):
            return sems(f"{name}_s{mixer}")

        TILES_OF = [4] * (PAGES // 4) if a else [4, 3]
        C = len(TILES_OF)
        R = min(4, C)
        KEYS = P * sum(TILES_OF)
        LAG = 2
        FILL = 64 if a else 16
        heads = 4 if a else 8
        width = SEG // heads

        kbuf = [sb(f"keys{r}", [P, 4, 4, P]) for r in range(R)]
        vbuf = [sb(f"values{r}", [P, 4, SEG]) for r in range(R)]
        bias = sb("bias", [P, KEYS + DQ])
        neg_s = sb("neg_scores", [P, KEYS + DQ])
        e = sb("exps", [P, KEYS + DQ])
        eT = sb("exps_T", [P, sum(TILES_OF), P])
        eT_new = sb("exps_T_new", [DQ, P])
        v_new = sb("v_new", [DQ, SEG])
        qs = sb("q_new", [P, 4, NS])
        kn = sb("k_new", [P, 4, NS])
        q_all = sb("q_blocks_all", [P, DB, 4, PR])
        qd = sb("q_blocks", [P, 4, PR])
        kd = sb("k_new_batch", [P, 4, DQ])
        pages = sb("pages", [1, DB * PAGES], I32)
        mins = sb("mins", [P, C + 1])
        neg_max = sb("neg_max", [P, 1])
        den = sb("den", [P, 1])
        rden = sb("rden", [P, 1])
        rvec = sb("rvec", [P, 1])
        second = sb("second_map", [P, 1])
        coef = sb("coef", [P, 1])
        sel = sb("sel", [P, heads, DQ])
        o_rows = sb("o_rows", [P, P])
        o = sb("o", [DQ, SEG])
        gate = sb("gate", [P, C + 1])

        consts_loaded = sem("consts_loaded")
        k_loaded = [sem(f"k_loaded{r}") for r in range(R)]
        v_loaded = [sem(f"v_loaded{r}") for r in range(R)]
        v_new_loaded = sem("v_new_loaded")
        setup = sem("setup")
        qd_ready = sem("qd_ready")
        scored = sem("scored")
        s_biased = sem("s_biased")
        max_ready = sem("max_ready")
        exp_done = sem("exp_done")
        e_transposed = sem("e_transposed")
        eT_ready = sem("eT_ready")
        values_done = sem("values_done")
        step = sem("step")
        o_scaled = sem("o_scaled")
        o_folded = sem("o_folded")
        o_ready = sem("o_ready")
        o_stored = sem("o_stored")
        first_q, first_k = (0, 4) if a else (8, 12)
        new_scores = bank[:, 4, 0:DQ]

        def pages_of(engine, b, c):
            return nc.values_load_multi_w_load_instructions(
                pages[0:1, ds(b * PAGES + 4 * c, 4)], engines=[engine], min_val=0,
                max_val=io["cache_k"].shape[0] - 1)[1]

        block = ctx.enter_context(nc.Block())

        @block.sync
        def _(sp):
            def load_k(b, c):
                r = c % R
                if not (isinstance(b, int) and b * C + c < R):
                    sp.wait_ge(scored, b * (C + 1) + (c - R + 1 if c >= R else c - R))
                if a:
                    for j, page in enumerate(pages_of(mybir.EngineType.SP, b, c)):
                        sp.dma_start(kbuf[r][:, j, :, :].rearrange("p h t -> p (h t)"),
                                     io["cache_k"][ds(page, 1), :, :].rearrange("a p c -> (a p) c")).then_inc(k_loaded[r], 16)
                else:
                    n, at = TILES_OF[c], sum(TILES_OF[:c])
                    sp.dma_start(kbuf[r][:, 0:n, :, :].rearrange("p j h t -> p (j h t)"),
                                 io["win_k"][ds(b, 1), :, at * SEG:(at + n) * SEG].rearrange("a p c -> (a p) c")).then_inc(k_loaded[r], 16)

            sp.dma_start(qs[:, :, :], io["qkT"][first_q:first_q + 4, :, SEQ:NT].rearrange("h p t -> p h t")).then_inc(consts_loaded, 16)
            sp.dma_start(kn[:, :, :], io["qkT"][first_k:first_k + 4, :, SEQ:NT].rearrange("h p t -> p h t")).then_inc(consts_loaded, 16)
            sp.dma_start(bias[:, :], io[f"bias_{mixer}"]).then_inc(consts_loaded, 16)
            sp.dma_start(second[:, :], io["second_map"]).then_inc(consts_loaded, 16)
            sp.dma_start(pages[:, :], io["page_table"]).then_inc(consts_loaded, 16)
            sp.dma_start(sel[:, :, :], io[f"sel_{mixer}"]).then_inc(consts_loaded, 16)
            sp.wait_ge(consts_loaded, 96)
            def keys_of(b):
                for c in range(C):
                    load_k(b, c)

            turns(sp, DB, keys_of)

        @block.gpsimd
        def _(pool):
            def load_v(b, c):
                r = c % R
                if not (isinstance(b, int) and b * C + c < R):
                    pool.wait_ge(values_done, b * C + (c - R + 1))
                if a:
                    for j, page in enumerate(pages_of(mybir.EngineType.Pool, b, c)):
                        pool.dma_start(vbuf[r][:, j, :],
                                     io["cache_v"][ds(page, 1), :, :].rearrange("a p c -> (a p) c")).then_inc(v_loaded[r], 16)
                else:
                    n, at = TILES_OF[c], sum(TILES_OF[:c])
                    pool.dma_start(vbuf[r][:, 0:n, :].rearrange("p j c -> p (j c)"),
                                 io["win_v"][ds(b, 1), :, at * SEG:(at + n) * SEG].rearrange("a p c -> (a p) c")).then_inc(v_loaded[r], 16)
                if c == C - 1:
                    since(pool, values_done, b * C)
                    v_rows = io["va"] if a else io["vb"]
                    pool.dma_start(v_new[:, :], v_rows[ds(b * DQ + SEQ, DQ), :]).then_inc(v_new_loaded, 16)

            def store(b):
                pool.wait_ge(o_ready, b + 1)
                pool.dma_start(io["mix"][ds(b * DQ + SEQ, DQ), (0 if a else SEG):(SEG if a else D)], o[:, :]).then_inc(o_stored, 16)

            pool.wait_ge(consts_loaded, 96)
            for c in range(C):
                load_v(0, c)
            with pool.Fori(1, DB) as b:
                for c in range(C):
                    load_v(b, c)
                    if c == min(2, C - 1):
                        store(b - 1)
            store(DB - 1)
            pool.wait_ge(o_stored, 16 * DB)


        @block.tensor
        def _(pe):
            def scores(b, c):
                n = TILES_OF[c]
                pe.wait_ge(k_loaded[c % R], b * (FILL * (C // R)) + FILL * (c // R + 1))
                if c == 0:
                    pe.wait_ge(qd_ready, b * 2 + 2)
                if not (isinstance(b, int) and b == 0 and c < R):
                    pe.wait_ge(s_biased, b * (C + 1) + (c - R + 1 if c >= R else c - R))
                if c == C - 1:
                    since(pe, s_biased, b * (C + 1))
                    if not isinstance(b, int):
                        pe.wait_ge(o_ready, b - 1)
                for h in range(4):
                    ins = nc.tensor.matmul(bank[h * PR:(h + 1) * PR, c % R, 0:n * P], qd[:, h, :],
                                           kbuf[c % R][:, 0:n, h, :], start=True, stop=True)
                ins.then_inc(scored, 1)
                if c == C - 1:
                    for h in range(4):
                        ins = nc.tensor.matmul(bank[h * PR:(h + 1) * PR, 4, 0:DQ], qd[:, h, :],
                                               kd[:, h, :], start=True, stop=True)
                    ins.then_inc(scored, 1)

            def transpose_exps(b):
                pe.wait_ge(exp_done, b + 1)
                for c in range(C):
                    n, at = TILES_OF[c], sum(TILES_OF[:c])
                    since(pe, eT_ready, b * C + max(0, c - 1))
                    for j in range(n):
                        ins = nc.tensor.transpose(bank[:, 5 + c % 2, j * P:(j + 1) * P],
                                                  e[:, (at + j) * P:(at + j + 1) * P], ident)
                    if c == 0:
                        ins = nc.tensor.transpose(bank[0:DQ, 7, P:2 * P], e[:, KEYS:KEYS + DQ], ident)
                    ins.then_inc(e_transposed, 1)

            def values(b, c):
                n, at = TILES_OF[c], sum(TILES_OF[:c])
                pe.wait_ge(v_loaded[c % R], b * (FILL * (C // R)) + FILL * (c // R + 1))
                pe.wait_ge(eT_ready, b * C + (c + 1))
                if c == 0:
                    since(pe, o_scaled, b)
                if c == C - 1:
                    pe.wait_ge(v_new_loaded, b * 16 + 16)
                for j in range(n):
                    for h in range(4):
                        ins = nc.tensor.matmul(bank[h * PR:(h + 1) * PR, 7, 0:P], eT[:, at + j, h * PR:(h + 1) * PR],
                                               vbuf[c % R][:, j, h * P:(h + 1) * P], start=(c == 0 and j == 0), stop=False)
                if c == C - 1:
                    for h in range(4):
                        ins = nc.tensor.matmul(bank[h * PR:(h + 1) * PR, 7, 0:P], eT_new[:, h * PR:(h + 1) * PR],
                                               v_new[:, h * P:(h + 1) * P], start=False, stop=True)
                ins.then_inc(values_done, 1)

            def fold(b):
                pe.wait_ge(o_scaled, b + 1)
                since(pe, o_ready, b)
                pe.wait_ge(s_biased, min(b + 2, DB) * (C + 1) if isinstance(b, int) else b * (C + 1) + 2 * (C + 1))
                for h in range(heads):
                    ins = nc.tensor.matmul(bank[0:DQ, 4, h * width:(h + 1) * width], sel[:, h, :],
                                           o_rows[:, 0:P] if a else o_rows[:, h % 2 * HD:(h % 2 + 1) * HD],
                                           start=True, stop=True)
                ins.then_inc(o_folded, 1)

            pe.wait_ge(consts_loaded, 96)
            for c in range(C):
                scores(0, c)
            def turn_of(b):
                for c in range(C):
                    scores(b + 1, c)
                    if c == LAG - 1:
                        transpose_exps(b)
                    if c >= LAG:
                        values(b, c - LAG)
                for c in range(C - LAG, C):
                    values(b, c)
                fold(b)

            turns(pe, DB - 1, turn_of)
            transpose_exps(DB - 1)
            for c in range(C):
                values(DB - 1, c)
            fold(DB - 1)

        @block.vector
        def _(dve):
            nc.vector.memset(q_all[:, :, :, :], 0.0).then_inc(setup, 1)
            dve.wait_ge(consts_loaded, 96)
            dve.wait_ge(setup, 1)
            for h in range(4):
                for m in range(2):
                    half = slice(m * HD, (m + 1) * HD)
                    col = m * DQ
                    nc.vector.tensor_copy(q_all[half, :, h, col:col + DQ],
                                          qs[half, h, :].rearrange("p (b q) -> p b q", q=DQ)).then_inc(setup, 1)
            nc.vector.tensor_scalar(coef[:, :], second[:, :], -1.0 if a else 0.0, 1.0, ALU.mult, ALU.add).then_inc(setup, 1)
            dve.wait_ge(setup, 10)
            if a:
                nc.vector.scalar_tensor_tensor(coef[:, :], second[:, :], neg_lam, coef[:, :],
                                               ALU.mult, ALU.add).then_inc(setup, 1)
                dve.wait_ge(setup, 11)

            def blocks(b):
                since(dve, scored, b * (C + 1))
                nc.vector.tensor_copy(kd[:, :, :], kn[:, :, ds(b * DQ, DQ)]).then_inc(qd_ready, 1)
                nc.vector.tensor_copy(qd[:, :, :], q_all[:, ds(b, 1), :, :].rearrange("p a h r -> p (a h) r")).then_inc(qd_ready, 1)

            def bias_scores(b, c):
                n = KEYS if c == C else sum(TILES_OF[:c]) * P
                w = DQ if c == C else TILES_OF[c] * P
                src = new_scores if c == C else bank[:, c % R, 0:w]
                dve.wait_ge(scored, b * (C + 1) + (c + 1))
                since(dve, exp_done, b)
                nc.vector.memset(gate[:, c:c + 1], 0.0)
                nc.vector.tensor_tensor_reduce(neg_s[:, n:n + w], src, bias[:, n:n + w], -1.0, 3e38, ALU.add, ALU.min,
                                               mins[:, c:c + 1]).then_inc(s_biased, 1)
                if c == C:
                    dve.wait_ge(s_biased, b * (C + 1) + (C + 1))
                    nc.vector.tensor_reduce(neg_max[:, :], mins[:, :], AX_X, ALU.min).then_inc(max_ready, 1)

            def scale_output(b):
                dve.wait_ge(exp_done, b + 1)
                nc.vector.reciprocal(rden[:, :], den[:, :]).then_inc(step, 1)
                dve.wait_ge(step, b * 2 + 1)
                nc.vector.tensor_tensor(rvec[:, :], rden[:, :], coef[:, :], ALU.mult).then_inc(step, 1)
                dve.wait_ge(step, b * 2 + 2)

            def take_output(b):
                dve.wait_ge(values_done, b * C + C)
                since(dve, o_folded, b)
                nc.vector.tensor_scalar(o_rows[:, :], bank[:, 7, 0:P], rvec[:, :], None, ALU.mult).then_inc(o_scaled, 1)
                dve.wait_ge(o_folded, b + 1)
                since(dve, o_stored, b * 16)
                nc.vector.tensor_copy(o[:, :], bank[0:DQ, 4, :]).then_inc(o_ready, 1)

            blocks(0)
            for c in range(C + 1):
                bias_scores(0, c)
            def turn_of(b):
                scale_output(b)
                blocks(b + 1)
                for c in range(C + 1):
                    bias_scores(b + 1, c)
                take_output(b)

            turns(dve, DB - 1, turn_of)
            scale_output(DB - 1)
            take_output(DB - 1)

        @block.scalar
        def _(act):
            def exps(b):
                act.wait_ge(max_ready, b + 1)
                since(act, e_transposed, b * C)
                since(act, step, b * 2)
                nc.scalar.activation(e[:, :], neg_s[:, :], ACT.Exp, bias=neg_max[:, :], scale=-1.0,
                                     accum_out=den[:, :]).then_inc(exp_done, 1)

            def take_exps_T(b):
                since(act, values_done, b * C)
                for c in range(C):
                    n, at = TILES_OF[c], sum(TILES_OF[:c])
                    act.wait_ge(e_transposed, b * C + (c + 1))
                    if c == 0:
                        nc.scalar.copy(eT_new[:, :], bank[0:DQ, 7, P:2 * P])
                    nc.scalar.copy(eT[:, at:at + n, :].rearrange("p j r -> p (j r)"),
                                   bank[:, 5 + c % 2, 0:n * P]).then_inc(eT_ready, 1)

            exps(0)
            def turn_of(b):
                take_exps_T(b)
                exps(b + 1)

            turns(act, DB - 1, turn_of)
            take_exps_T(DB - 1)


PH = 8
TOPK = 16
PICKS = PH * TOPK


def mix_and_route(nc, io, sems, ident, bank, picksT):
    with ExitStack() as ctx:
        def sb(name, shape, dt=F32):
            return ctx.enter_context(nc.sbuf_tensor(name, shape, dt))

        w_out = sb("w_out_sb", [P, KD, D])
        w_q = sb("w_q_sb", [P, KD, D])
        sub_keys = sb("sub_keys_sb", [P, PH, P])
        iota = sb("iota_sb", [P, P])
        g2T = sb("g2_T", [P, KD])
        subln = sb("subln_sb", [P, 1])
        m_rows = sb("mixed_rows", [P, D])
        x_rows = sb("x_rows4", [P, D])
        sq = sb("squares4", [P, D])
        oss = sb("o_sumsq", [P, 4])
        ostd = sb("o_std", [P, 4])
        orstd = sb("o_rstd", [P, 4])
        mT = sb("mixed_T", [P, KD, P])
        h = sb("h_rows4", [P, D])
        hss = sb("h_sumsq4", [P, 1])
        hstd = sb("h_std4", [P, 1])
        hrstd = sb("h_rstd4", [P, 1])
        hT = sb("h_T", [P, KD, P])
        xr = sb("h_scaled", [P, D])
        x2T = sb("x2_T", [P, KD, P])
        qT = sb("peer_q_T", [P, PH, P])
        s1 = sb("key_scores", [P, 2 * PH, P])
        s2 = sb("key_scores_rest", [P, 2 * PH, P])
        best = sb("best_scores", [P, 2 * PH, TOPK])
        at = sb("best_at", [P, 2 * PH, TOPK], U32)
        at_f = sb("best_at_f", [P, 2 * PH, TOPK])
        cand = sb("cand", [P, PH, TOPK * TOPK])
        cand2 = sb("cand_rest", [P, PH, TOPK * TOPK])
        top = sb("top_scores", [P, PH, TOPK])
        top_at = sb("top_at", [P, PH, TOPK], U32)
        side = sb("top_side", [P, 2, PH, TOPK], U32)
        side_f = sb("top_side_f", [P, 2, PH, TOPK])
        onehot = sb("onehot", [P, PH, TOPK, TOPK])
        sq_o = sb("squares_o", [P, SEG])
        top_e = sb("top_exps", [P, PH, TOPK])
        gsum = sb("gate_sum", [P, PH])
        picks = sb("picks", [P, 3, PH, TOPK])
        gate = sb("gate4", [P, 24])

        weights_loaded = sems("w4_loaded")
        consts_loaded = sems("c4_loaded")
        m_loaded = sems("m_loaded")
        x_loaded = sems("x4_loaded")
        f_step = sems("front_step")
        s_step = sems("selection_step")
        subln_ready = sems("subln_ready")
        oss_ready = sems("oss_ready")
        ostd_ready = sems("ostd_ready")
        m_ready = sems("m_ready")
        mT_in_psum = sems("mT_in_psum")
        mT_ready = sems("mT_ready")
        h_in_psum = sems("h_in_psum")
        h_ready = sems("h4_ready")
        hss_ready = sems("hss_ready")
        hvar_ready = sems("hvar4_ready")
        hstd_ready = sems("hstd_ready")
        xr_ready = sems("xr_ready")
        hT_in_psum = sems("hT_in_psum")
        hT_ready = sems("hT_ready")
        hT_stored = sems("hT_stored")
        x2T_stored = sems("x2T_stored")
        x2T_in_psum = sems("x2T_in_psum")
        x2T_ready = sems("x2T_ready")
        q_in_psum = sems("q_in_psum")
        qT_ready = sems("qT_ready")
        s_in_psum = sems("ks_in_psum")
        s_ready = sems("ks_ready")
        s_used = sems("ks_used")
        shifted = sems("top_shifted")
        exp_done = sems("top_exp_done")
        picks_ready = sems("picks_ready")
        picks_in_psum = sems("picks_in_psum")
        picksT_ready = sems("picksT_ready")

        block = ctx.enter_context(nc.Block())

        @block.sync
        def _(sp):
            sp.dma_start(g2T[:, :], io["g2"]).then_inc(consts_loaded, 16)
            sp.dma_start(subln[:, :], io["subln"]).then_inc(consts_loaded, 16)
            sp.dma_start(sub_keys[:, :, :], io["sub_keys"]).then_inc(consts_loaded, 16)
            sp.dma_start(iota[:, :], io["iota"]).then_inc(consts_loaded, 16)
            sp.dma_start(m_rows[:, :], io["mix"][0:P, :]).then_inc(m_loaded, 16)
            sp.dma_start(x_rows[:, :], io["x"][0:P, :]).then_inc(x_loaded, 16)
            sp.dma_start(w_out[:, :, :], io["w_out"].rearrange("(k p) c -> p k c", p=P)).then_inc(weights_loaded, 16)
            sp.dma_start(w_q[:, :, :], io["w_q"].rearrange("(k p) c -> p k c", p=P)).then_inc(weights_loaded, 16)
            def turn_of(t):
                sp.wait_ge(mT_in_psum, t * 2 + 2)
                sp.dma_start(m_rows[:, :], io["mix"][ds(t * P + P, P), :]).then_inc(m_loaded, 16)
                sp.wait_ge(h_ready, t + 1)
                sp.wait_ge(hT_ready, t * 2 + 2)
                sp.wait_ge(x2T_ready, t * 2 + 2)
                sp.dma_start(x_rows[:, :], io["x"][ds(t * P + P, P), :]).then_inc(x_loaded, 16)
                sp.dma_start(io["hT"][:, :, ds(t * P, P)].rearrange("k p t -> p k t"), hT[:, :, :]).then_inc(hT_stored, 16)
                sp.dma_start(io["x2T"][:, :, ds(t * P, P)].rearrange("k p t -> p k t"), x2T[:, :, :]).then_inc(x2T_stored, 16)

            turns(sp, TILES - 1, turn_of)
            sp.wait_ge(hT_ready, 2 * TILES)
            sp.wait_ge(x2T_ready, 2 * TILES)
            sp.dma_start(io["x2T"][:, :, (TILES - 1) * P:TP].rearrange("k p t -> p k t"), x2T[:, :, :]).then_inc(x2T_stored, 16)
            sp.wait_ge(x2T_stored, 16 * TILES)
            sp.dma_start(io["hT"][:, :, (TILES - 1) * P:TP].rearrange("k p t -> p k t"), hT[:, :, :]).then_inc(hT_stored, 16)
            sp.wait_ge(hT_stored, 16 * TILES)

        @block.tensor
        def _(pe):
            def front(t):
                pe.wait_ge(m_ready, t + 1)
                since(pe, x2T_ready, t * 2)
                since(pe, hT_ready, t * 2)
                for b in range(2):
                    for j in range(4):
                        ins = nc.tensor.transpose(bank[:, b, j * P:(j + 1) * P], m_rows[:, (4 * b + j) * P:(4 * b + j + 1) * P], ident)
                    ins.then_inc(mT_in_psum, 1)
                since(pe, s_ready, t * 4)
                for k in range(KD):
                    if k % 4 == 0:
                        pe.wait_ge(mT_ready, t * 2 + k // 4 + 1)
                    for c in range(2):
                        ins = nc.tensor.matmul(bank[:, 2 + c, :], mT[:, k, :], w_out[:, k, c * 512:(c + 1) * 512],
                                               start=(k == 0), stop=(k == KD - 1))
                ins.then_inc(h_in_psum, 1)
                pe.wait_ge(h_ready, t + 1)
                for b in range(2):
                    for j in range(4):
                        ins = nc.tensor.transpose(bank[:, b, j * P:(j + 1) * P], h[:, (4 * b + j) * P:(4 * b + j + 1) * P], ident)
                    ins.then_inc(hT_in_psum, 1)
                pe.wait_ge(xr_ready, t + 1)
                for b in range(2):
                    for j in range(4):
                        ins = nc.tensor.transpose(bank[:, 4 + b, j * P:(j + 1) * P], xr[:, (4 * b + j) * P:(4 * b + j + 1) * P], ident)
                    ins.then_inc(x2T_in_psum, 1)
                since(pe, picksT_ready, t - 1)
                since(pe, qT_ready, t * 2)
                pe.wait_ge(x2T_ready, t * 2 + 2)
                for hd in range(PH):
                    for k in range(KD):
                        ins = nc.tensor.matmul(bank[:, 6 + hd // 4, (hd % 4) * P:(hd % 4 + 1) * P],
                                               w_q[:, k, hd * P:(hd + 1) * P], x2T[:, k, :],
                                               start=(k == 0), stop=(k == KD - 1))
                    if hd % 4 == 3:
                        ins.then_inc(q_in_psum, 1)
                pe.wait_ge(qT_ready, t * 2 + 2)
                for c in range(2):
                    half = slice(c * HD, (c + 1) * HD)
                    for hd in range(PH):
                        ins = nc.tensor.matmul(bank[:, 2 + 2 * c + hd // 4, (hd % 4) * P:(hd % 4 + 1) * P],
                                               qT[half, hd, :], sub_keys[half, hd, :], start=True, stop=True)
                        if hd % 4 == 3:
                            ins.then_inc(s_in_psum, 1)

            def transpose_picks(t):
                pe.wait_ge(picks_ready, t + 1)
                for j in range(3):
                    ins = nc.tensor.transpose(bank[:, 6, j * P:(j + 1) * P], picks[:, j, :, :].rearrange("p h s -> p (h s)"), ident)
                ins.then_inc(picks_in_psum, 1)

            pe.wait_ge(weights_loaded, 32)
            pe.wait_ge(consts_loaded, 64)
            front(0)
            front(1)
            transpose_picks(0)
            with pe.Fori(2, TILES) as t:
                front(t)
                transpose_picks(t - 1)
            transpose_picks(TILES - 1)

        @block.scalar
        def _(act):
            def front(t):
                act.wait_ge(oss_ready, t + 1)
                nc.scalar.activation(ostd[:, :], oss[:, :], ACT.Sqrt).then_inc(ostd_ready, 1)
                for b in range(2):
                    act.wait_ge(mT_in_psum, t * 2 + b + 1)
                    dst = mT[:, 4 * b:4 * b + 4, :].rearrange("p k t -> p (k t)")
                    if b == 0:
                        nc.scalar.activation(dst, bank[:, b, :], ACT.Copy, scale=subln[:, 0:1]).then_inc(mT_ready, 1)
                    else:
                        nc.scalar.copy(dst, bank[:, b, :]).then_inc(mT_ready, 1)
                act.wait_ge(h_ready, t + 1)
                nc.scalar.activation(sq[:, :], h[:, :], ACT.Square, accum_out=hss[:, :]).then_inc(hss_ready, 1)
                act.wait_ge(hvar_ready, t + 1)
                nc.scalar.activation(hstd[:, :], hss[:, :], ACT.Sqrt).then_inc(hstd_ready, 1)
                since(act, hT_stored, t * 16)
                for b in range(2):
                    act.wait_ge(hT_in_psum, t * 2 + b + 1)
                    nc.scalar.copy(hT[:, 4 * b:4 * b + 4, :].rearrange("p k t -> p (k t)"), bank[:, b, :]).then_inc(hT_ready, 1)
                for b in range(2):
                    act.wait_ge(q_in_psum, t * 2 + b + 1)
                    nc.scalar.copy(qT[:, 4 * b:4 * b + 4, :].rearrange("p k t -> p (k t)"), bank[:, 6 + b, :]).then_inc(qT_ready, 1)
                since(act, s_used, t)
                for g in range(4):
                    act.wait_ge(s_in_psum, t * 4 + g + 1)
                    nc.scalar.copy(s1[:, 4 * g:4 * g + 4, :].rearrange("p k t -> p (k t)"), bank[:, 2 + g, :]).then_inc(s_ready, 1)

            def selection(t):
                act.wait_ge(shifted, t + 1)
                nc.scalar.activation(top_e[:, :, :], top_e[:, :, :], ACT.Exp).then_inc(exp_done, 1)
                act.wait_ge(picks_in_psum, t + 1)
                for j in range(3):
                    ins = nc.scalar.copy(picksT[:, j, ds(t * P, P)], bank[:, 6, j * P:(j + 1) * P])
                ins.then_inc(picksT_ready, 1)

            act.wait_ge(subln_ready, 1)
            front(0)
            def turn_of(t):
                front(t + 1)
                selection(t)

            turns(act, TILES - 1, turn_of)
            selection(TILES - 1)

        @block.vector
        def _(dve):
            F_STEPS, S_STEPS = 4, 21

            def front(t, part):
                base = t * F_STEPS
                if part == 0:
                    dve.wait_ge(m_loaded, t * 16 + 16)
                    nc.vector.tensor_tensor(sq_o[:, :], m_rows[:, 0:SEG], m_rows[:, 0:SEG], ALU.mult).then_inc(f_step, 1)
                    dve.wait_ge(f_step, base + 1)
                    nc.vector.tensor_reduce(oss[:, :], sq_o[:, :].rearrange("p (h e) -> p h e", h=4), AX_X, ALU.add).then_inc(f_step, 1)
                    dve.wait_ge(f_step, base + 2)
                    nc.vector.tensor_scalar(oss[:, :], oss[:, :], 1.0 / P, EPS, ALU.mult, ALU.add).then_inc(oss_ready, 1)
                if part == 1:
                    dve.wait_ge(ostd_ready, t + 1)
                    nc.vector.reciprocal(orstd[:, :], ostd[:, :]).then_inc(f_step, 1)
                    dve.wait_ge(f_step, base + 3)
                    m4 = m_rows[:, 0:SEG].rearrange("p (h e) -> p h e", h=4)
                    nc.vector.tensor_tensor(m4, m4, orstd[:, :].unsqueeze(2).broadcast_to([P, 4, P]), ALU.mult).then_inc(m_ready, 1)
                if part == 2:
                    dve.wait_ge(h_in_psum, t + 1)
                    dve.wait_ge(x_loaded, t * 16 + 16)
                    since(dve, hT_in_psum, t * 2)
                    nc.vector.tensor_tensor(h[:, :], bank[:, 2:4, :].rearrange("p b c -> p (b c)"), x_rows[:, :], ALU.add).then_inc(h_ready, 1)
                if part == 3:
                    dve.wait_ge(hss_ready, t + 1)
                    nc.vector.tensor_scalar(hss[:, :], hss[:, :], 1.0 / D, EPS, ALU.mult, ALU.add).then_inc(hvar_ready, 1)
                    dve.wait_ge(hstd_ready, t + 1)
                    nc.vector.reciprocal(hrstd[:, :], hstd[:, :]).then_inc(f_step, 1)
                    dve.wait_ge(f_step, base + 4)
                    since(dve, x2T_in_psum, t * 2)
                    nc.vector.tensor_scalar(xr[:, :], h[:, :], hrstd[:, 0:1], None, ALU.mult).then_inc(xr_ready, 1)
                if part == 4:
                    since(dve, x2T_stored, t * 16)
                    since(dve, q_in_psum, t * 2)
                    for b in range(2):
                        dve.wait_ge(x2T_in_psum, t * 2 + b + 1)
                        nc.vector.tensor_tensor(
                            x2T[:, 4 * b:4 * b + 4, :], bank[:, 4 + b, :].rearrange("p (k t) -> p k t", k=4),
                            g2T[:, 4 * b:4 * b + 4].unsqueeze(2).broadcast_to([P, 4, P]), ALU.mult).then_inc(x2T_ready, 1)

            def top16(n, src, rest, vals, idx, s, t, last_read):
                def hold():
                    dve.wait_ge(s_step, t * S_STEPS + s.now)
                    nc.vector.memset(gate[:, s.n:s.n + 1], 0.0)

                for half in range(2):
                    part = slice(8 * half, 8 * half + 8)
                    data = rest if half else src
                    for g in range(n):
                        ins = nc.vector.max(vals[:, g, part], data[:, g, :])
                    ins.then_inc(s_step, s.up())
                    hold()
                    for g in range(n):
                        ins = nc.vector.max_index(idx[:, g, part], vals[:, g, part], data[:, g, :])
                        if not half:
                            ins = nc.vector.match_replace(rest[:, g, :], vals[:, g, part], src[:, g, :], -3e38)
                    ins.then_inc(s_step, s.up())
                    if not half:
                        hold()
                    if not half and last_read is not None:
                        dve.wait_ge(s_step, t * S_STEPS + s.now)
                        nc.vector.memset(gate[:, 21:22], 0.0).then_inc(last_read, 1)
                    yield

            def selection(t, s):
                now = lambda: t * S_STEPS + s.now
                dve.wait_ge(s_ready, t * 4 + 4)
                nc.vector.memset(gate[:, 22:23], 0.0)
                yield from top16(2 * PH, s1, s2, best, at, s, t, s_used)
                dve.wait_ge(s_step, now())
                nc.vector.tensor_copy(at_f[:, :, :], at[:, :, :]).then_inc(s_step, s.up())
                nc.vector.tensor_tensor(
                    cand[:, :, :].rearrange("p h (a b) -> p h a b", a=TOPK),
                    best[:, 0:PH, :].unsqueeze(3).broadcast_to([P, PH, TOPK, TOPK]),
                    best[:, PH:2 * PH, :].unsqueeze(2).broadcast_to([P, PH, TOPK, TOPK]), ALU.add).then_inc(s_step, s.up())
                yield
                dve.wait_ge(s_step, now())
                nc.vector.memset(gate[:, 23:24], 0.0)
                yield from top16(PH, cand, cand2, top, top_at, s, t, None)
                dve.wait_ge(s_step, now())
                since(dve, exp_done, t)
                nc.vector.tensor_tensor(top_e[:, :, :], top[:, :, :], top[:, :, 0:1].broadcast_to([P, PH, TOPK]),
                                        ALU.subtract).then_inc(shifted, 1)
                nc.vector.tensor_scalar(side[:, 0, :, :], top_at[:, :, :], 4, None, ALU.logical_shift_right).then_inc(s_step, s.up())
                nc.vector.tensor_scalar(side[:, 1, :, :], top_at[:, :, :], TOPK - 1, None, ALU.bitwise_and).then_inc(s_step, s.up())
                dve.wait_ge(s_step, now())
                nc.vector.tensor_copy(side_f[:, :, :, :].rearrange("p c h s -> p (c h s)"),
                                      side[:, :, :, :].rearrange("p c h s -> p (c h s)")).then_inc(s_step, s.up())
                since(dve, picks_in_psum, t)
                for c in range(2):
                    dve.wait_ge(s_step, now())
                    nc.vector.tensor_tensor(
                        onehot[:, :, :, :], side_f[:, c, :, :].unsqueeze(3).broadcast_to([P, PH, TOPK, TOPK]),
                        iota[:, 0:TOPK].unsqueeze(1).unsqueeze(1).broadcast_to([P, PH, TOPK, TOPK]),
                        ALU.is_equal).then_inc(s_step, s.up())
                    dve.wait_ge(s_step, now())
                    nc.vector.tensor_tensor(
                        onehot[:, :, :, :], onehot[:, :, :, :],
                        at_f[:, c * PH:(c + 1) * PH, :].unsqueeze(2).broadcast_to([P, PH, TOPK, TOPK]),
                        ALU.mult).then_inc(s_step, s.up())
                    dve.wait_ge(s_step, now())
                    nc.vector.tensor_reduce(picks[:, c, :, :], onehot[:, :, :, :], AX_X, ALU.add).then_inc(s_step, s.up())
                dve.wait_ge(exp_done, t + 1)
                nc.vector.tensor_reduce(gsum[:, :], top_e[:, :, :], AX_X, ALU.add).then_inc(s_step, s.up())
                dve.wait_ge(s_step, now())
                nc.vector.reciprocal(gsum[:, :], gsum[:, :]).then_inc(s_step, s.up())
                dve.wait_ge(s_step, now())
                nc.vector.tensor_tensor(picks[:, 2, :, :], top_e[:, :, :], gsum[:, :].unsqueeze(2).broadcast_to([P, PH, TOPK]),
                                        ALU.mult).then_inc(picks_ready, 1)
                assert s.n == S_STEPS, s.n
                yield

            dve.wait_ge(consts_loaded, 64)
            nc.vector.tensor_scalar(subln[:, :], subln[:, :], 1.0 - LAM_INIT, None, ALU.mult).then_inc(subln_ready, 1)
            for part in range(5):
                front(0, part)
            def turn_of(t):
                parts = iter(range(5))
                front(t + 1, next(parts))
                for _ in selection(t, Steps()):
                    for part in [next(parts, None)]:
                        if part is not None:
                            front(t + 1, part)

            turns(dve, TILES - 1, turn_of)
            for _ in selection(TILES - 1, Steps()):
                pass


E_GROUP = 8
RING = 4


def spread_gates(nc, io, sems, bank, picksT):
    with ExitStack() as ctx:
        def sb(name, shape, dt=F32):
            return ctx.enter_context(nc.sbuf_tensor(name, shape, dt))

        iota = sb("iota5", [P, P])
        row1 = [sb(f"onehot_i1_{r}", [P, E_GROUP, P]) for r in range(RING)]
        row2 = [sb(f"gated_i2_{r}", [P, E_GROUP, P]) for r in range(RING)]
        stage = [sb(f"stage{r}", [P, P, P]) for r in range(2)]

        gate = sb("gate5", [P, 2 * P // E_GROUP])

        iota_loaded = sems("iota5_loaded")
        places_ready = sems("places_ready")
        plain_ready = sems("plain_ready")
        gated_ready = sems("gated_ready")
        rows_used = sems("rows_used")
        staged = sems("staged")
        stored = [sems(f"stage_stored{r}") for r in range(2)]
        PER_TILE = P // E_GROUP
        PER_TURN = 2 * PER_TILE
        FULL = NT // P
        REST = NT % P
        block = ctx.enter_context(nc.Block())

        def tiles(eng, body):
            turns(eng, FULL // 2, lambda t: body(t, PER_TURN))
            body(FULL // 2, REST // E_GROUP)

        @block.sync
        def _(sp):
            sp.dma_start(iota[:, :], io["iota"]).then_inc(iota_loaded, 16)
            def store(t):
                for r in range(2):
                    sp.wait_ge(staged, t * PER_TURN + (r + 1) * PER_TILE)
                    sp.dma_start(io["gates"][:, :, ds(t * (2 * P) + r * P, P)], stage[r][:, :, :]).then_inc(stored[r], 16)

            turns(sp, FULL // 2, store)
            sp.wait_ge(staged, FULL * PER_TILE + REST // E_GROUP)
            sp.dma_start(io["gates"][:, :, FULL * P:NT], stage[0][:, :, 0:REST]).then_inc(stored[0], 16)
            sp.wait_ge(stored[0], 16 * (FULL // 2 + 1))
            sp.wait_ge(stored[1], 16 * (FULL // 2))

        @block.vector
        def _(dve):
            dve.wait_ge(iota_loaded, 16)
            def one_hots(t, groups):
                for g in range(groups):
                    since(dve, rows_used, t * PER_TURN + (g - RING + 1))
                    toks = ds(t * (2 * P) + g * E_GROUP, E_GROUP)
                    nc.vector.memset(gate[:, g:g + 1], 0.0)
                    for c, row, ready in ((1, row2, plain_ready), (0, row1, places_ready)):
                        nc.vector.tensor_tensor(row[g % RING][:, :, :], iota[:, :].unsqueeze(1).broadcast_to([P, E_GROUP, P]),
                                                picksT[:, c, toks].unsqueeze(2).broadcast_to([P, E_GROUP, P]),
                                                ALU.is_equal).then_inc(ready, 1)

            tiles(dve, one_hots)

        @block.gpsimd
        def _(pool):
            def gated(t, groups):
                for g in range(groups):
                    pool.wait_ge(plain_ready, t * PER_TURN + (g + 1))
                    toks = ds(t * (2 * P) + g * E_GROUP, E_GROUP)
                    nc.gpsimd.tensor_tensor(row2[g % RING][:, :, :], row2[g % RING][:, :, :],
                                            picksT[:, 2, toks].unsqueeze(2).broadcast_to([P, E_GROUP, P]),
                                            ALU.mult).then_inc(gated_ready, 1)

            tiles(pool, gated)

        @block.tensor
        def _(pe):
            def products(t, groups):
                for g in range(groups):
                    pe.wait_ge(places_ready, t * PER_TURN + (g + 1))
                    pe.wait_ge(gated_ready, t * PER_TURN + (g + 1))
                    since(pe, staged, t * PER_TURN + max(0, g - 3))
                    for j in range(E_GROUP):
                        ins = nc.tensor.matmul(bank[:, 2 * (g % 4) + j // 4, (j % 4) * P:(j % 4 + 1) * P],
                                               row1[g % RING][:, j, :], row2[g % RING][:, j, :], start=True, stop=True)
                    ins.then_inc(rows_used, 1)

            tiles(pe, products)

        @block.scalar
        def _(act):
            def take_products(t, groups):
                for g in range(groups):
                    r, at = g // PER_TILE, g % PER_TILE * E_GROUP
                    act.wait_ge(rows_used, t * PER_TURN + (g + 1))
                    if at == 0:
                        since(act, stored[r], t * 16)
                    src = bank[:, 2 * (g % 4):2 * (g % 4) + 2, :].rearrange("p b (t i) -> p i (b t)", i=P)
                    nc.scalar.copy(stage[r][:, :, at:at + E_GROUP], src).then_inc(staged, 1)

            tiles(act, take_products)


BLK = 2
SUPER = P // BLK
TC = 3
CH = NT // TC


def run_experts(nc, io, sems, bank):
    with ExitStack() as ctx:
        def sb(name, shape, dt=F32):
            return ctx.enter_context(nc.sbuf_tensor(name, shape, dt))

        x2 = [sb(f"x2_{part}", [P, KD, NT], F32R) for part in ("hi", "lo")]
        yT = sb("y_T", [P, KD, NT])
        u_raw = [sb(f"u_raw{j}", [P, KD * P]) for j in range(BLK)]
        u = [[sb(f"u_{part}{j}", [P, KD * P], F32R) for part in ("hi", "lo")] for j in range(BLK)]
        v_raw = [sb(f"v_raw{j}", [P, D]) for j in range(BLK)]
        v = [[sb(f"v_{part}{j}", [P, D], F32R) for part in ("hi", "lo")] for j in range(BLK)]
        g = [sb(f"gates{j}", [P, NT]) for j in range(BLK)]
        w = [sb(f"gelu{j}", [P, NT]) for j in range(BLK)]
        coef = [[[sb(f"coef_{part}{r}{j}", [P, NT], F32R) for part in ("hi", "lo")] for j in range(BLK)] for r in range(2)]

        u_loaded = [sems(f"u_loaded{j}") for j in range(BLK)]
        g_loaded = [sems(f"g_loaded{j}") for j in range(BLK)]
        v_loaded = [sems(f"v_loaded{j}") for j in range(BLK)]
        x_loaded = [sems(f"x5_loaded{j}") for j in range(BLK)]
        x_hi, x_lo = sems("x2_hi_ready"), sems("x2_lo_ready")
        h_loaded = sems("h5_loaded")
        u_hi, u_lo = sems("u_hi_ready"), sems("u_lo_ready")
        v_hi, v_lo = sems("v_hi_ready"), sems("v_lo_ready")
        a_in_psum = sems("a_in_psum")
        gelu_done = sems("gelu_done")
        weighed = sems("weighed")
        coef_hi, coef_lo = sems("coef_hi_ready"), sems("coef_lo_ready")
        y_in_psum = sems("y_in_psum")
        y_added = sems("y_added")
        y_stored = sems("y_stored")
        window_moved = sems("window_moved")
        AN, YN = BLK * TC, KD * TC

        block = ctx.enter_context(nc.Block())

        def pipeline(eng, a_part, y_part):
            a_part(0, 0)
            a_part(1, 1)
            y_part(0, 0)
            with eng.Fori(1, SUPER // 2 - 1) as m:
                a_part(m * 2, 0)
                y_part(m * 2 - 1, 1)
                a_part(m * 2 + 1, 1)
                y_part(m * 2, 0)
            a_part(SUPER - 2, 0)
            y_part(SUPER - 3, 1)
            a_part(SUPER - 1, 1)
            y_part(SUPER - 2, 0)
            y_part(SUPER - 1, 1)

        @block.sync
        def _(sp):
            for k in range(KD):
                since(sp, x_lo, k - 1)
                sp.dma_start(w[k % 2][:, :], io["x2T"][k, :, 0:NT]).then_inc(x_loaded[k % 2], 16)
                if k == 1:
                    sp.dma_start(u_raw[0][:, :], io["u"][0, :, :]).then_inc(u_loaded[0], 16)
                    sp.dma_start(v_raw[0][:, :], io["v"][:, 0, :]).then_inc(v_loaded[0], 16)
                    sp.dma_start(v_raw[1][:, :], io["v"][:, 1, :]).then_inc(v_loaded[1], 16)
                    sp.dma_start(g[0][:, :], io["gates"][:, 0, 0:NT]).then_inc(g_loaded[0], 16)
            sp.dma_start(yT[:, :, :], io["hT"][:, :, 0:NT].rearrange("k p t -> p k t")).then_inc(h_loaded, 16)

            def load(s, r):
                for j in range(BLK):
                    i, n = s * BLK + j, (j + 1) % BLK
                    if isinstance(s, int) and i == P - 1:
                        continue
                    since(sp, u_lo, i)
                    sp.dma_start(u_raw[n][:, :], io["u"][ds(i + 1, 1), :, :].rearrange("a p c -> (a p) c")).then_inc(u_loaded[n], 16)
                    since(sp, weighed, i)
                    sp.dma_start(g[n][:, :], io["gates"][:, ds(i + 1, 1), 0:NT].rearrange("p a t -> p (a t)")).then_inc(g_loaded[n], 16)

            def load_v(s, r):
                if isinstance(s, int) and s == SUPER - 1:
                    return
                for j in range(BLK):
                    sp.wait_ge(v_lo, s * BLK + (j + 1))
                    sp.dma_start(v_raw[j][:, :], io["v"][:, ds(s * BLK + (BLK + j), 1), :].rearrange("p a d -> p (a d)")).then_inc(v_loaded[j], 16)

            pipeline(sp, load, load_v)
            for k in range(KD):
                sp.wait_ge(y_added, SUPER * YN - (KD - 1 - k) * TC)
                sp.dma_start(io["yT"][k, :, :], yT[:, k, :]).then_inc(y_stored, 16)
            sp.wait_ge(y_stored, 16 * KD)

        @block.gpsimd
        def _(pool):
            move = (STATE - DQ) * SEG
            n = 0
            for state, out, new in (("state_k", "win_k_out", "kb"), ("state_v", "win_v_out", "vb")):
                src, dst = (io[x].rearrange("b s c -> b (s c)") for x in (state, out))
                pool.dma_start(dst[:, move:], io[new][SEQ:NT, :].rearrange("(b q) c -> b (q c)", q=DQ)).then_inc(window_moved, 16)
                for b in range(DB):
                    n += 1
                    pool.wait_ge(window_moved, 16 * n)
                    pool.dma_start(dst[b, 0:move].rearrange("(a c) -> a c", a=64),
                                   src[b, DQ * SEG:].rearrange("(a c) -> a c", a=64)).then_inc(window_moved, 16)
                n += 1
                pool.wait_ge(window_moved, 16 * n)

        @block.tensor
        def _(pe):
            def activations(s, r):
                for j in range(BLK):
                    pe.wait_ge(u_hi, s * BLK + (j + 1))
                    pe.wait_ge(u_lo, s * BLK + (j + 1))
                    for c in range(TC):
                        n = j * TC + c
                        since(pe, gelu_done, s * AN + (n - 3))
                        for k in range(KD):
                            for a, b in ((0, 0), (0, 1), (1, 0)):
                                ins = nc.tensor.matmul(bank[:, (AN * r + n) % 4, 0:CH], u[j][a][:, k * P:(k + 1) * P],
                                                       x2[b][:, k, c * CH:(c + 1) * CH], start=(k == 0 and a == b),
                                                       stop=(k == KD - 1 and a == 1))
                        ins.then_inc(a_in_psum, 1)

            def outputs(s, r):
                pe.wait_ge(coef_lo, s * BLK + BLK)
                pe.wait_ge(v_lo, s * BLK + BLK)
                for n in range(YN):
                    k, c = n // TC, n % TC
                    since(pe, y_added, s * YN + (n - 3))
                    for j in range(BLK):
                        for a, b in ((0, 0), (0, 1), (1, 0)):
                            ins = nc.tensor.matmul(bank[:, 4 + n % 4, 0:CH], v[j][a][:, k * P:(k + 1) * P],
                                                   coef[r][j][b][:, c * CH:(c + 1) * CH], start=(j == 0 and a == b),
                                                   stop=(j == BLK - 1 and a == 1))
                    ins.then_inc(y_in_psum, 1)

            pe.wait_ge(x_lo, KD)
            pipeline(pe, activations, outputs)

        @block.scalar
        def _(act):
            def split_u(i, j):
                act.wait_ge(u_loaded[j], 8 * i + (16 - 8 * j))
                since(act, a_in_psum, (i - 1) * TC)
                nc.scalar.copy(u[j][0][:, :], u_raw[j][:, :]).then_inc(u_hi, 1)

            def split_v(s):
                for j in range(BLK):
                    act.wait_ge(v_loaded[j], s * 16 + 16)
                    since(act, y_in_psum, s * YN)
                    nc.scalar.copy(v[j][0][:, :], v_raw[j][:, :]).then_inc(v_hi, 1)

            def gelus(s, r):
                if not (isinstance(s, int) and s == 0):
                    split_v(s - 1)
                for j in range(BLK):
                    i = s * BLK + j
                    if not (isinstance(s, int) and i == P - 1):
                        split_u(i + 1, (j + 1) % BLK)
                    since(act, coef_lo, i - 1)
                    for c in range(TC):
                        n = j * TC + c
                        act.wait_ge(a_in_psum, s * AN + (n + 1))
                        nc.scalar.activation(w[j][:, c * CH:(c + 1) * CH], bank[:, (AN * r + n) % 4, 0:CH], ACT.Gelu).then_inc(gelu_done, 1)

            for k in range(KD):
                act.wait_ge(x_loaded[k % 2], 16 * (k // 2 + 1))
                nc.scalar.copy(x2[0][:, k, :], w[k % 2][:, :]).then_inc(x_hi, 1)
            act.wait_ge(x_lo, KD)
            split_u(0, 0)
            pipeline(act, gelus, lambda s, r: None)
            split_v(SUPER - 1)

        @block.vector
        def _(dve):
            def rest(out, raw, hi, ready):
                nc.vector.tensor_tensor(out, raw, hi.bitcast(F32), ALU.subtract).then_inc(ready, 1)

            def split_u(i, j):
                dve.wait_ge(u_hi, i + 1)
                rest(u[j][1][:, :], u_raw[j][:, :], u[j][0][:, :], u_lo)

            def split_v(s):
                for j in range(BLK):
                    dve.wait_ge(v_hi, s * BLK + (j + 1))
                    rest(v[j][1][:, :], v_raw[j][:, :], v[j][0][:, :], v_lo)

            def weigh(s, r):
                if not (isinstance(s, int) and s == 0):
                    split_v(s - 1)
                for j in range(BLK):
                    i = s * BLK + j
                    if not (isinstance(s, int) and i == P - 1):
                        split_u(i + 1, (j + 1) % BLK)
                    dve.wait_ge(gelu_done, s * AN + (j + 1) * TC)
                    dve.wait_ge(g_loaded[j], s * 16 + 16)
                    nc.vector.tensor_tensor(w[j][:, :], w[j][:, :], g[j][:, :], ALU.mult).then_inc(weighed, 1)
                    dve.wait_ge(weighed, i + 1)
                    since(dve, y_in_psum, s * YN - YN)
                    nc.vector.tensor_copy(coef[r][j][0][:, :], w[j][:, :]).then_inc(coef_hi, 1)
                    dve.wait_ge(coef_hi, i + 1)
                    rest(coef[r][j][1][:, :], w[j][:, :], coef[r][j][0][:, :], coef_lo)

            def add(s, r):
                since(dve, y_added, s * YN)
                for n in range(YN):
                    k, c = n // TC, n % TC
                    dve.wait_ge(y_in_psum, s * YN + (n + 1))
                    out = yT[:, k, c * CH:(c + 1) * CH]
                    nc.vector.tensor_tensor(out, out, bank[:, 4 + n % 4, 0:CH], ALU.add).then_inc(y_added, 1)

            def add_last(s, r):
                if isinstance(s, int) and s == SUPER - 1:
                    split_v(s)
                add(s, r)

            for k in range(KD):
                dve.wait_ge(x_hi, k + 1)
                rest(x2[1][:, k, :], w[k % 2][:, :], x2[0][:, k, :], x_lo)
            split_u(0, 0)
            dve.wait_ge(h_loaded, 16)
            pipeline(dve, weigh, add_last)


def build(nc, io, phases=9):
    with ExitStack() as ctx:
        bank = ctx.enter_context(nc.psum_tensor("banks", [P, 8, 512], F32))
        ident = ctx.enter_context(nc.sbuf_tensor("ident", [P, P], F32))[:, :]
        neg_lam = ctx.enter_context(nc.sbuf_tensor("neg_lambda", [P, 1], F32))[:, :]

        def phase(run, *args):
            own = []

            def sems(name):
                own.append(nc.alloc_semaphore(name=name))
                return own[-1]

            run(nc, io, sems, *args)
            nc.clear_and_free_semaphores(own)
            nc.all_engine_barrier()

        phase(load_constants, ident)
        phase(project, ident, bank)
        if phases >= 2:
            phase(lambda_column, neg_lam)
            phase(attend_prompt, ident, bank, neg_lam, "a")
            phase(attend_prompt, ident, bank, neg_lam, "b")
        if phases >= 3:
            phase(attend_sample, ident, bank, neg_lam, "a")
            phase(attend_sample, ident, bank, neg_lam, "b")
        if phases >= 4:
            with nc.sbuf_tensor("picks_T", [P, 3, TP], F32) as picksT:
                phase(mix_and_route, ident, bank, picksT)
                phase(spread_gates, bank, picksT)
        if phases >= 5:
            phase(run_experts, bank)


def slopes(n):
    return 2.0 ** (-8.0 * np.arange(1, n + 1) / n)


def log_branches(d):
    count = sum(((d >= 0) & (d <= w) & (d % dil == 0)).astype(np.int64) for w, dil in DILATIONS)
    return np.where(count > 0, np.log(np.maximum(count, 1).astype(np.float64)), NEG)


def shape_constants():
    d = np.arange(P)[:, None] + (SEQ - P) - np.arange(SEQ)[None, :]
    strips = [np.where(d >= 0, -s * d, NEG) for s in slopes(4)]
    strips += [np.where(log_branches(d) > NEG / 2, log_branches(d) - s * d, NEG) for s in slopes(8)]
    used = np.arange(P).reshape(4, PR)[:, 0:2 * DQ].ravel()
    row_q = np.tile(np.arange(DQ), 8)
    new = np.arange(DQ)
    bias_a, bias_b = np.zeros((P, PAST + DQ)), np.zeros((P, len(state_rows()) + DQ))
    pos_a = np.concatenate([np.arange(PAST), PAST + new])
    da = PAST + row_q[:, None] - pos_a[None, :]
    bias_a[used] = np.where(da >= 0, -np.repeat(slopes(4), 8)[:, None] * da, NEG)
    pos_b = np.concatenate([state_rows(), STATE + new])
    db = STATE + row_q[:, None] - pos_b[None, :]
    bias_b[used] = np.where(log_branches(db) > NEG / 2, log_branches(db) - np.repeat(slopes(8), DQ)[:, None] * db, NEG)
    sel_a = np.zeros((P, 4, DQ))
    sel_b = np.zeros((P, 8, DQ))
    second_map = np.zeros((P, 1))
    for i, r in enumerate(used):
        sel_a[r, i // 8, i % DQ] = 1
        sel_b[r, i // DQ, i % DQ] = 1
        second_map[r] = i // DQ % 2
    out = {"ident": np.eye(P), "strips": np.stack(strips), "bias_a": bias_a, "bias_b": bias_b,
           "sel_a": sel_a, "sel_b": sel_b, "second_map": second_map,
           "iota": np.broadcast_to(np.arange(P), (P, P))}
    return {k: np.ascontiguousarray(v, dtype=np.float32) for k, v in out.items()}


def state_rows():
    far = STATE - DILATIONS[1][0]
    step = DILATIONS[2][1]
    return np.concatenate([(np.arange(0, far, step)[:, None] + np.arange(DQ)[None, :]).ravel(),
                           np.arange(far, STATE)])


def lay_out(inp):
    a = {k: np.asarray(v) for k, v in inp.items()}
    c = np.ascontiguousarray
    n_phys = a["cache_a_k"].shape[1]
    x = np.zeros((TP, D), np.float32)
    x[0:SEQ] = a["x_prompt"].reshape(SEQ, D)
    x[SEQ:NT] = a["x_sample"].reshape(NS, D)
    rows = state_rows()
    tiles_b = len(rows) // P
    kb = a["state_b_k"][0][:, rows].reshape(DB, tiles_b, P, 4, P)
    vb = a["state_b_v"][0][:, rows].reshape(DB, tiles_b, P, SEG)
    m = {
        "x": x,
        "g1": c(a["norm1_g"].reshape(KD, P).T), "g2": c(a["norm2_g"].reshape(KD, P).T),
        "w_in": a["w_in"][0], "w_out": a["w_out"][0], "w_q": a["peer_wq"][0],
        "qk_gain": np.concatenate([a["qnorm_a"], a["knorm_a"], a["qnorm_b"], a["knorm_b"]]),
        "lams": np.concatenate([a["lambda_q1"], a["lambda_k1"], a["lambda_q2"], a["lambda_k2"]]),
        "subln": c(a["subln_g"].reshape(P, 1)),
        "cache_k": c(a["cache_a_k"][0].reshape(n_phys, P, 4, P).transpose(0, 3, 2, 1)).reshape(n_phys, P, SEG),
        "cache_v": a["cache_a_v"][0].reshape(n_phys, P, SEG),
        "page_table": a["page_table"].reshape(1, -1),
        "win_k": c(kb.transpose(0, 4, 1, 3, 2)).reshape(DB, P, tiles_b * SEG),
        "win_v": c(vb.transpose(0, 2, 1, 3)).reshape(DB, P, tiles_b * SEG),
        "state_k": a["state_b_k"].reshape(DB, STATE, SEG), "state_v": a["state_b_v"].reshape(DB, STATE, SEG),
        "sub_keys": c(a["peer_subkeys"][0].transpose(1, 3, 0, 2)).reshape(P, 8, P),
        "u": c(a["peer_u"][0].reshape(P, P, KD, P).transpose(1, 3, 2, 0)).reshape(P, P, KD * P),
        "v": a["peer_v"][0].reshape(P, P, D),
    }
    m.update(shape_constants())
    return m


OUTS = {"ka": (TP, SEG), "va": (TP, SEG), "kb": (TP, SEG), "vb": (TP, SEG),
        "win_k_out": (DB, STATE, SEG), "win_v_out": (DB, STATE, SEG), "yT": (KD, P, NT)}
SCRATCH = {"qkT": (16, P, TP), "mix": (TP, D), "gates": (P, P, TP), "hT": (KD, P, TP), "x2T": (KD, P, TP)}


def kernel(**inputs):
    import concourse.bacc as bacc
    from concourse.bass_utils import run_bass_kernel_spmd as run

    nc = bacc.Bacc("TRN2", target_bir_lowering=False, num_devices=1)
    arrays = lay_out(inputs)
    io = {}
    for name, arr in arrays.items():
        io[name] = nc.dram_tensor(f"in_{name}", arr.shape, mybir.dt.from_np(arr.dtype), kind="ExternalInput").ap()
    for name, shape in OUTS.items():
        io[name] = nc.dram_tensor(f"out_{name}", shape, F32, kind="ExternalOutput").ap()
    for name, shape in SCRATCH.items():
        io[name] = nc.dram_tensor(f"scratch_{name}", shape, F32).ap()
    build(nc, io)
    got = run(nc, [{f"in_{k}": v for k, v in arrays.items()}], core_ids=[0]).results[0]
    o = {name: np.asarray(got[f"out_{name}"]) for name in OUTS}
    y = o["yT"].reshape(D, NT).T
    new = lambda name, width: (o[name][:SEQ].reshape(1, 1, SEQ, -1, width),
                               o[name][SEQ:NT].reshape(1, DB, DQ, -1, width))
    (kap, kas), (vap, vas) = new("ka", P), new("va", P)
    (kbp, _), (vbp, _) = new("kb", HD), new("vb", HD)
    window = (1, DB, STATE, 8, HD)
    return (y[:SEQ].reshape(1, SEQ, D), y[SEQ:].reshape(DB, DQ, D), kap, vap, kas, vas,
            kbp, vbp, o["win_k_out"].reshape(window), o["win_v_out"].reshape(window))
```

```python
from contextlib import ExitStack

import numpy as np
import concourse.bass as bass
from concourse import mybir

F32 = mybir.dt.float32
F32R = mybir.dt.float32r
BF16 = mybir.dt.bfloat16
I32 = mybir.dt.int32
U32 = mybir.dt.uint32
ALU = mybir.AluOpType
ACT = mybir.ActivationFunctionType
AX_X = mybir.AxisListType.X

P = 128
D = 1024
KD = D // P
SEQ = 1024
DB, DQ = 8, 4
NS = DB * DQ
NT = SEQ + NS
TILES = -(-NT // P)
TP = TILES * P
COLS = 3072
SEG = 512
NSEG = COLS // SEG
HD = 64
EPS = 1e-6
NEG = -1e30
PAST, PAGE, STATE = 4096, 128, 2048
PAGES = PAST // PAGE
LAM_INIT = 0.8 - 0.6
DILATIONS = ((128, 1), (512, 4), (2048, 16))
ds = bass.ds


def since(eng, sem, value):
    if not isinstance(value, int) or value > 0:
        eng.wait_ge(sem, value)


def turns(eng, n, body):
    body(0)
    if n > 1:
        with eng.Fori(1, n) as i:
            body(i)


class Steps:

    def __init__(self, base=0):
        self.base, self.n = base, 0

    def up(self):
        self.n += 1
        return 1

    @property
    def now(self):
        return self.base + self.n


def load_constants(nc, io, sems, ident):
    ident_loaded = sems("ident_loaded")
    pad_zeroed = sems("pad_zeroed")
    with nc.Block() as block:
        @block.sync
        def _(sp):
            sp.dma_start(ident, io["ident"]).then_inc(ident_loaded, 16)
            sp.dma_start(io["mix"][NT:TP, :], io["x"][NT:TP, :]).then_inc(pad_zeroed, 16)
            sp.wait_ge(ident_loaded, 16)
            sp.wait_ge(pad_zeroed, 16)


def project(nc, io, sems, ident, bank):
    with ExitStack() as ctx:
        def sb(name, shape, dt=F32):
            return ctx.enter_context(nc.sbuf_tensor(name, shape, dt))

        KH = KD // 2
        w_raw = sb("w_raw", [P, 2, KH, SEG])
        w = [[sb(f"w_{part}{r}", [P, 2, KH, SEG], F32R) for part in ("hi", "lo")] for r in range(2)]
        xn = sb("xn_T", [P, KD, TP])
        x = [[sb(f"x_{part}{r}", [P, KD, P], F32R) for part in ("hi", "lo")] for r in range(3)]
        x_rows = [sb(f"x_rows{r}", [P, D]) for r in range(2)]
        x_sq = sb("x_squares", [P, D])
        xs = sb("x_scaled", [P, D])
        h = [sb(f"h_rows{r}", [P, SEG]) for r in range(3)]
        sq = sb("squares", [P, SEG])
        hn = [sb(f"h_normed{r}", [P, SEG]) for r in range(3)]
        qkT = [sb(f"qk_T{r}", [P, 4, P]) for r in range(3)]
        g1T = sb("g1_T", [P, KD])
        gain = sb("qk_gain", [P, 4, HD])
        eps = sb("eps1", [P, 1])
        ss = sb("x_sumsq", [P, 1])
        std = sb("x_std", [P, 1])
        rstd = sb("x_rstd", [P, 1])
        hss = sb("h_sumsq", [P, 8])
        hstd = sb("h_std", [P, 8])
        hrstd = sb("h_rstd", [P, 8])

        gains_loaded, consts_ready = sems("p_gains_loaded"), sems("p_consts_ready")
        w_loaded = [sems(f"w_loaded{half}") for half in range(2)]
        w_hi, w_lo = sems("w_hi_ready"), sems("w_lo_ready")
        x_loaded = [sems(f"x_loaded{r}") for r in range(2)]
        x_squared, x_std_ready = sems("x_squared"), sems("x_std_ready")
        x_rstd_ready, xs_ready = sems("x_rstd_ready"), sems("xs_ready")
        xT_in_psum, xn_ready = sems("xT_in_psum"), sems("xn_ready")
        x_hi, x_lo = sems("x_hi_ready"), sems("x_lo_ready")
        made = sems("products_made")
        squared = sems("h_squared")
        h_ready = sems("h_ready")
        hss_ready, hstd_ready = sems("hss1_ready"), sems("hstd1_ready")
        hn_step, hn_ready = sems("hn_step"), sems("hn_ready")
        qkT_in_psum, qkT_ready = sems("qkT_in_psum"), sems("qkT_ready")
        h_stored, hn_stored, qkT_stored = ([sems(f"{name}_stored{r}") for r in range(3)] for name in ("h", "hn", "qkT"))

        QK, K, V = (0, 1, 3, 4), (1, 4), (2, 5)
        PAIRS = TILES // 2

        def tile(m, slot):
            return m * 2 + slot % 2

        def step(c, m, slot):
            return m * 2 + (c * TILES + slot % 2)

        def nth(c, m, slot):
            return m * 2 + (sum(s < c for s in QK) * TILES + slot % 2)

        def stores(kind, c, m, slot):
            before = sum(s < c for s in kind)
            if slot == 2:
                return 16 * before
            base = 16 * PAIRS * before
            return m * 16 + base if c in kind else base

        def tiles(eng, c, body, between=lambda half: None):
            peeled = PAIRS if c == 0 else 2 if c in (K[0], V[0]) else 1
            for m in range(peeled):
                for slot in range(2):
                    body(m, slot)
                    if m == 0:
                        between(slot)
            if c:
                with eng.Fori(peeled, PAIRS) as m:
                    for slot in range(2):
                        body(m, slot)
            body(PAIRS, 2)

        def before(c, m, slot):
            if slot == 2:
                return c, PAIRS - 1, 1
            if slot == 1:
                return c, m, 0
            if isinstance(m, int) and m == 0:
                return (c - 1, PAIRS, 2) if c else None
            return c, m - 1, 1

        def to_prepare(c, m, slot, far):
            return tile(m, slot) + far if c == 0 and tile(m, slot) + far < TILES else None

        block = ctx.enter_context(nc.Block())

        @block.sync
        def _(sp):
            def load_w(c):
                for half in range(2):
                    since(sp, w_lo, 2 * c - 1 + half)
                    at = half * KH * P
                    sp.dma_start(w_raw[:, half, :, :], io["w_in"][at:at + KH * P, c * SEG:(c + 1) * SEG].rearrange(
                        "(k p) c -> p k c", p=P)).then_inc(w_loaded[half], 16)

            sp.dma_start(g1T[:, :], io["g1"]).then_inc(gains_loaded, 16)
            sp.dma_start(gain[:, :, :], io["qk_gain"].partition_broadcast(P)).then_inc(gains_loaded, 16)
            load_w(0)
            load_w(1)
            for c in range(NSEG):
                def store(m, slot):
                    r = ds(tile(m, slot) * P, P)
                    if c in V:
                        sp.wait_ge(h_ready, step(c, m, slot) + 1)
                        sp.dma_start(io["va" if c == 2 else "vb"][r, :], h[slot][:, :]).then_inc(h_stored[slot], 16)
                    else:
                        sp.wait_ge(qkT_ready, nth(c, m, slot) + 1)
                        if c in K:
                            sp.dma_start(io["ka" if c == 1 else "kb"][r, :], hn[slot][:, :]).then_inc(hn_stored[slot], 16)
                        at = 4 * QK.index(c)
                        sp.dma_start(io["qkT"][at:at + 4, :, r].rearrange("b p t -> p b t"), qkT[slot][:, :, :]).then_inc(qkT_stored[slot], 16)

                tiles(sp, c, store, lambda half: load_w(c + 2) if half and c + 2 < NSEG else None)
            for slot in range(3):
                m = 0 if slot == 2 else PAIRS
                sp.wait_ge(h_stored[slot], stores(V, NSEG, m, slot))
                sp.wait_ge(hn_stored[slot], stores(K, NSEG, m, slot))
                sp.wait_ge(qkT_stored[slot], stores(QK, NSEG, m, slot))

        @block.gpsimd
        def _(pool):
            for t in range(TILES):
                since(pool, xs_ready, t - 1)
                pool.dma_start(x_rows[t % 2][:, :], io["x"][t * P:(t + 1) * P, :]).then_inc(x_loaded[t % 2], 16)

        @block.tensor
        def _(pe):
            def transpose_x(t):
                pe.wait_ge(xs_ready, t + 1)
                since(pe, xn_ready, t)
                for b in range(2):
                    for j in range(4):
                        k = 4 * b + j
                        ins = nc.tensor.transpose(bank[:, 3 + b, j * P:(j + 1) * P], xs[:, k * P:(k + 1) * P], ident)
                ins.then_inc(xT_in_psum, 1)

            def products(c, m, slot):
                pe.wait_ge(x_lo, step(c, m, slot) + 1)
                since(pe, h_ready, step(c, m, slot) - 1)
                for k in range(KD):
                    if k % KH == 0:
                        pe.wait_ge(w_lo, 2 * c + k // KH + 1)
                    for a, b in ((0, 0), (0, 1), (1, 0)):
                        ins = nc.tensor.matmul(bank[:, slot, :], x[slot][a][:, k, :], w[c % 2][b][:, k // KH, k % KH, :],
                                               start=(k == 0 and a == b), stop=(k == KD - 1 and a == 1))
                ins.then_inc(made, 1)

            def transpose_qk(c, m, slot):
                n = nth(c, m, slot)
                pe.wait_ge(hn_ready, n + 1)
                since(pe, qkT_ready, n - 1)
                for j in range(4):
                    ins = nc.tensor.transpose(bank[:, 5 + slot, j * P:(j + 1) * P], hn[slot][:, j * P:(j + 1) * P], ident)
                ins.then_inc(qkT_in_psum, 1)

            transpose_x(0)
            transpose_x(1)
            for c in range(NSEG):
                def body(m, slot):
                    products(c, m, slot)
                    t = to_prepare(c, m, slot, 2)
                    if t is not None:
                        transpose_x(t)
                    last = before(c, m, slot)
                    if last and last[0] in QK:
                        transpose_qk(*last)

                tiles(pe, c, body)

        @block.vector
        def _(dve):
            def scale_x(t, r):
                dve.wait_ge(x_std_ready, t + 1)
                nc.vector.reciprocal(rstd[:, :], std[:, :]).then_inc(x_rstd_ready, 1)
                dve.wait_ge(x_rstd_ready, t + 1)
                since(dve, xT_in_psum, t)
                nc.vector.tensor_scalar(xs[:, :], x_rows[r][:, :], rstd[:, 0:1], None, ALU.mult).then_inc(xs_ready, 1)

            def gain_xT(t):
                dve.wait_ge(xT_in_psum, t + 1)
                nc.vector.tensor_tensor(
                    xn[:, :, ds(t * P, P)].rearrange("p (b k) t -> p b k t", b=2),
                    bank[:, 3:5, :].rearrange("p b (k t) -> p b k t", k=4),
                    g1T[:, :].rearrange("p (b k) -> p b k", b=2).unsqueeze(3).broadcast_to([P, 2, 4, P]), ALU.mult).then_inc(xn_ready, 1)

            def split_x(c, m, slot):
                t = tile(m, slot)
                dve.wait_ge(x_hi, step(c, m, slot) + 1)
                nc.vector.tensor_tensor(x[slot][1][:, :, :], xn[:, :, ds(t * P, P)], x[slot][0][:, :, :].bitcast(F32),
                                        ALU.subtract).then_inc(x_lo, 1)

            def split_w(c, half):
                dve.wait_ge(w_hi, 2 * c + half + 1)
                nc.vector.tensor_tensor(w[c % 2][1][:, half, :, :], w_raw[:, half, :, :],
                                        w[c % 2][0][:, half, :, :].bitcast(F32), ALU.subtract).then_inc(w_lo, 1)

            def norm_qk(c, m, slot):
                n = nth(c, m, slot)
                dve.wait_ge(squared, n + 1)
                dve.wait_ge(h_ready, step(c, m, slot) + 1)
                nc.vector.tensor_reduce(hss[:, :], sq[:, :].rearrange("p (g d) -> p g d", d=HD), AX_X, ALU.add).then_inc(hss_ready, 1)
                dve.wait_ge(hstd_ready, n + 1)
                nc.vector.reciprocal(hrstd[:, :], hstd[:, :]).then_inc(hn_step, 1)
                dve.wait_ge(hn_step, n * 2 + 1)
                since(dve, hn_stored[slot], stores(K, c, m, slot))
                since(dve, qkT_in_psum, n - 1)
                hs = hn[slot][:, :].rearrange("p (g d) -> p g d", d=HD)
                nc.vector.tensor_tensor(hs, h[slot][:, :].rearrange("p (g d) -> p g d", d=HD),
                                        hrstd[:, :].unsqueeze(2).broadcast_to([P, 8, HD]), ALU.mult).then_inc(hn_step, 1)
                dve.wait_ge(hn_step, n * 2 + 2)
                nc.vector.tensor_tensor(hs, hs, gain[:, QK.index(c), :].unsqueeze(1).broadcast_to([P, 8, HD]),
                                        ALU.mult).then_inc(hn_ready, 1)

            nc.vector.memset(eps[:, :], EPS).then_inc(consts_ready, 1)
            dve.wait_ge(gains_loaded, 32)
            for seg in (0, 2):
                nc.vector.tensor_scalar(gain[:, seg, :], gain[:, seg, :], HD ** -0.5, None, ALU.mult).then_inc(consts_ready, 1)
            dve.wait_ge(consts_ready, 3)
            scale_x(0, 0)
            gain_xT(0)
            scale_x(1, 1)
            split_w(0, 0)
            split_w(0, 1)
            for c in range(NSEG):
                def body(m, slot):
                    split_x(c, m, slot)
                    last = before(c, m, slot)
                    if last and last[0] in QK:
                        norm_qk(*last)
                    t = to_prepare(c, m, slot, 1)
                    if t is not None:
                        gain_xT(t)
                    t = to_prepare(c, m, slot, 2)
                    if t is not None:
                        scale_x(t, t % 2)

                tiles(dve, c, body, lambda half: split_w(c + 1, half) if c + 1 < NSEG else None)

        @block.scalar
        def _(act):
            def std_x(t, r):
                act.wait_ge(x_loaded[r], 16 * (t // 2 + 1))
                since(act, x_std_ready, t)
                nc.scalar.activation(x_sq[:, :], x_rows[r][:, :], ACT.Square, accum_out=ss[:, :]).then_inc(x_squared, 1)
                act.wait_ge(x_squared, t + 1)
                since(act, x_rstd_ready, t)
                nc.scalar.activation(std[:, :], ss[:, :], ACT.Sqrt, bias=eps[:, :], scale=1.0 / D).then_inc(x_std_ready, 1)

            def split_x(c, m, slot):
                if c == 0:
                    act.wait_ge(xn_ready, tile(m, slot) + 1)
                since(act, made, step(c, m, slot) - 1)
                nc.scalar.copy(x[slot][0][:, :, :], xn[:, :, ds(tile(m, slot) * P, P)]).then_inc(x_hi, 1)

            def split_w(c, half):
                act.wait_ge(w_loaded[half], 16 * (c + 1))
                since(act, made, (c - 1) * TILES)
                nc.scalar.copy(w[c % 2][0][:, half, :, :], w_raw[:, half, :, :]).then_inc(w_hi, 1)

            def take_products(c, m, slot):
                n = nth(c, m, slot)
                act.wait_ge(made, step(c, m, slot) + 1)
                since(act, hn_ready, n - 1 if c in QK else nth(c, 0, 0))
                since(act, h_stored[slot], stores(V, c, m, slot))
                if c in QK:
                    since(act, hss_ready, n)
                    nc.scalar.activation(sq[:, :], bank[:, slot, :], ACT.Square).then_inc(squared, 1)
                nc.scalar.copy(h[slot][:, :], bank[:, slot, :]).then_inc(h_ready, 1)
                if c in QK:
                    act.wait_ge(hss_ready, n + 1)
                    nc.scalar.activation(hstd[:, :], hss[:, :], ACT.Sqrt, bias=eps[:, :], scale=1.0 / HD).then_inc(hstd_ready, 1)

            def take_qkT(c, m, slot):
                act.wait_ge(qkT_in_psum, nth(c, m, slot) + 1)
                since(act, qkT_stored[slot], stores(QK, c, m, slot))
                nc.scalar.copy(qkT[slot][:, :, :].rearrange("p k t -> p (k t)"), bank[:, 5 + slot, :]).then_inc(qkT_ready, 1)

            act.wait_ge(consts_ready, 1)
            std_x(0, 0)
            std_x(1, 1)
            split_w(0, 0)
            split_w(0, 1)
            for c in range(NSEG):
                def body(m, slot):
                    t = to_prepare(c, m, slot, 2)
                    if t is not None:
                        std_x(t, t % 2)
                    split_x(c, m, slot)
                    last = before(c, m, slot)
                    if last:
                        take_products(*last)
                        last = before(*last)
                    if last and last[0] in QK:
                        take_qkT(*last)

                tiles(act, c, body, lambda half: split_w(c + 1, half) if c + 1 < NSEG else None)
            take_products(NSEG - 1, PAIRS, 2)


UNITS = 4
QT = SEQ // P
NB = 2


def lambda_column(nc, io, sems, out):
    with ExitStack() as ctx:
        def sb(name, shape):
            return ctx.enter_context(nc.sbuf_tensor(name, shape, F32))

        lams = sb("lams", [P, 2, 2, HD])
        prod = sb("lam_prod", [P, 2, HD])
        dots = sb("lam_dots", [P, 2])
        exps = sb("lam_exps", [P, 2])
        diff = sb("lam_diff", [P, 1])
        lams_loaded = sems("lams_loaded")
        step = sems("lam_step")
        dots_ready = sems("lam_dots_ready")
        exps_ready = sems("lam_exps_ready")
        with nc.Block() as block:
            @block.sync
            def _(sp):
                sp.dma_start(lams[:, :, :, :].rearrange("p a b d -> p (a b) d"),
                             io["lams"].partition_broadcast(P)).then_inc(lams_loaded, 16)

            @block.vector
            def _(dve):
                dve.wait_ge(lams_loaded, 16)
                nc.vector.tensor_tensor(prod[:, :, :], lams[:, :, 0, :], lams[:, :, 1, :], ALU.mult).then_inc(step, 1)
                dve.wait_ge(step, 1)
                nc.vector.tensor_reduce(dots[:, :], prod[:, :, :], AX_X, ALU.add).then_inc(dots_ready, 1)
                dve.wait_ge(exps_ready, 1)
                nc.vector.tensor_tensor(diff[:, :], exps[:, 1:2], exps[:, 0:1], ALU.subtract).then_inc(step, 1)
                dve.wait_ge(step, 2)
                nc.vector.tensor_scalar(out, diff[:, :], -LAM_INIT, None, ALU.add).then_inc(step, 1)
                dve.wait_ge(step, 3)

            @block.scalar
            def _(act):
                act.wait_ge(dots_ready, 1)
                nc.scalar.activation(exps[:, :], dots[:, :], ACT.Exp).then_inc(exps_ready, 1)


def attend_prompt(nc, io, sems, ident, bank, neg_lam, mixer):
    a = mixer == "a"
    with ExitStack() as ctx:
        def sb(name, shape, dt=F32):
            return ctx.enter_context(nc.sbuf_tensor(f"{name}_{mixer}", shape, dt))

        def sem(name):
            return sems(f"{name}_{mixer}")

        MW = 1 if a else 2
        q = [sb(f"q{u}", [P, 2, SEQ]) for u in range(NB)]
        k = [sb(f"k{u}", [P, SEQ]) for u in range(NB)]
        v = [sb(f"v{u}", [P, QT, P]) for u in range(NB)]
        strip = [sb(f"strip{u}", [P, MW, SEQ]) for u in range(NB)]
        neg_s = sb("neg_scores", [P, 2, SEQ])
        e = sb("exps", [P, 2, 2, SEQ])
        w = sb("weights", [P, 2, 1, SEQ]) if a else e
        wT = sb("weights_T", [P, 2, MW, QT, P])
        neg_max = sb("neg_max", [P, 2, 2])
        den = sb("den", [P, 4, 2])
        rden = sb("rden", [P, 4, 2])
        r2 = sb("r2", [P, 2])
        o = sb("o", [P, 2, P])
        gate = sb("gate", [P, 2 * NB * QT])

        loaded = [sem(f"pr_loaded{u}") for u in range(NB)]
        zeroed = sem("zeroed")
        s_in_psum = sem("s_in_psum")
        s_biased = sem("s_biased")
        exp_done = sem("exp_done")
        step = sem("pr_step")
        w_ready = sem("w_ready")
        wT_in_psum = sem("wT_in_psum")
        wT_ready = sem("wT_ready")
        o_in_psum = sem("o_in_psum")
        o_ready = sem("o_ready")
        o_stored = [sem(f"o_stored{par}") for par in range(2)]

        TURNS = UNITS // NB
        TURN_TILES = NB * QT
        GROUPS = [-(-(i + 1) // 4) for i in range(QT)]
        TURN_GROUPS = NB * MW * sum(GROUPS)
        first_q, first_k = (0, 4) if a else (8, 12)
        v_rows = io["va"] if a else io["vb"]

        def group_at(n):
            return MW * (n // QT * sum(GROUPS) + sum(GROUPS[:n % QT]))

        block = ctx.enter_context(nc.Block())

        @block.sync
        def _(sp):
            sp.wait_ge(zeroed, 2 * NB)
            def load(turn, u):
                qt = io["qkT"][ds(turn * NB + (first_q + u), 1), :, 0:SEQ]
                for m in range(2):
                    half = slice(m * HD, (m + 1) * HD)
                    sp.dma_start(q[u][half, m, :], qt[:, half, :].rearrange("a p t -> (a p) t")).then_inc(loaded[u], 16)
                kt = io["qkT"][ds(turn * NB + (first_k + u), 1), :, 0:SEQ]
                sp.dma_start(k[u][:, :], kt.rearrange("a p t -> (a p) t")).then_inc(loaded[u], 16)
                vt = v_rows[0:SEQ, ds(turn * (NB * P) + u * P, P)]
                sp.dma_start(v[u][:, :, :], vt.rearrange("(j p) e -> p j e", p=P)).then_inc(loaded[u], 16)
                st = io["strips"][ds(turn * (NB * MW) + (u * MW + (0 if a else 4)), MW), :, :]
                sp.dma_start(strip[u][:, :, :], st.rearrange("m p c -> p m c")).then_inc(loaded[u], 16)

            def store(turn, n):
                u, i = n // QT, n % QT
                sp.wait_ge(o_ready, turn * TURN_TILES + (n + 1))
                sp.dma_start(io["mix"][i * P:(i + 1) * P, ds(turn * (NB * P) + ((0 if a else SEG) + u * P), P)],
                             o[:, n % 2, :]).then_inc(o_stored[n % 2], 16)

            def turn_of(turn):
                for n in range(TURN_TILES):
                    store(turn, n)
                    if n % QT == QT - 1:
                        load(turn + 1, n // QT)

            for u in range(NB):
                load(0, u)
            turns(sp, TURNS - 1, turn_of)
            for n in range(TURN_TILES):
                store(TURNS - 1, n)
            for par in range(2):
                sp.wait_ge(o_stored[par], 8 * UNITS * QT)

        @block.gpsimd
        def _(pool):
            for u in range(NB):
                for m in range(2):
                    nc.gpsimd.memset(q[u][(1 - m) * HD:(2 - m) * HD, m, :], 0.0).then_inc(zeroed, 1)

        @block.tensor
        def _(pe):
            def scores(turn, n):
                u, i = n // QT, n % QT
                for m in range(2):
                    since(pe, s_biased, turn * (2 * TURN_TILES) + max(0, 2 * n + m - 1))
                    for c in range(0, (i + 1) * P, 512):
                        width = min(512, (i + 1) * P - c)
                        ins = nc.tensor.matmul(bank[:, 2 * m + c // 512, 0:width], q[u][:, m, i * P:(i + 1) * P],
                                               k[u][:, c:c + width], start=True, stop=True)
                    ins.then_inc(s_in_psum, 1)

            def transpose_weights(turn, n):
                i = n % QT
                g = group_at(n)
                if a:
                    pe.wait_ge(w_ready, turn * TURN_TILES + (n + 1))
                for mw in range(MW):
                    if not a:
                        pe.wait_ge(exp_done, turn * (2 * TURN_TILES) + (2 * n + mw + 1))
                    for j0 in range(0, i + 1, 4):
                        since(pe, wT_ready, turn * TURN_GROUPS + max(0, g - 1))
                        for j in range(j0, min(j0 + 4, i + 1)):
                            ins = nc.tensor.transpose(bank[:, 4 + g % 2, (j - j0) * P:(j - j0 + 1) * P],
                                                      w[:, n % 2, mw, j * P:(j + 1) * P], ident)
                        ins.then_inc(wT_in_psum, 1)
                        g += 1

            def weigh_values(turn, n):
                u, i = n // QT, n % QT
                since(pe, o_ready, turn * TURN_TILES + max(0, n - 1))
                width = P // MW
                for mw in range(MW):
                    pe.wait_ge(wT_ready, turn * TURN_GROUPS + (group_at(n) + (mw + 1) * GROUPS[i]))
                    for j in range(i + 1):
                        ins = nc.tensor.matmul(bank[:, 6 + n % 2, mw * width:(mw + 1) * width], wT[:, n % 2, mw, j, :],
                                               v[u][:, j, mw * width:(mw + 1) * width], start=(j == 0), stop=(j == i))
                ins.then_inc(o_in_psum, 1)

            def turn_of(turn):
                pe.wait_ge(zeroed, 2 * NB)
                pe.wait_ge(loaded[0], turn * 80 + 80)
                scores(turn, 0)
                for n in range(TURN_TILES):
                    if n + 1 == QT:
                        pe.wait_ge(loaded[1], turn * 80 + 80)
                    if n + 1 < TURN_TILES:
                        scores(turn, n + 1)
                    transpose_weights(turn, n)
                    if n:
                        weigh_values(turn, n - 1)
                weigh_values(turn, TURN_TILES - 1)

            turns(pe, TURNS, turn_of)

        @block.vector
        def _(dve):
            def bias(turn, n):
                u, i = n // QT, n % QT
                L = (i + 1) * P
                for m in range(2):
                    dve.wait_ge(s_in_psum, turn * (2 * TURN_TILES) + (2 * n + m + 1))
                    since(dve, exp_done, turn * (2 * TURN_TILES) + max(0, 2 * n + m - 1))
                    nc.vector.memset(gate[:, 2 * n + m:2 * n + m + 1], 0.0)
                    nc.vector.tensor_tensor_reduce(
                        neg_s[:, m, 0:L], bank[:, 2 * m:2 * m + 2, :].rearrange("p b c -> p (b c)")[:, 0:L],
                        strip[u][:, m % MW, SEQ - L:SEQ], -1.0, 3e38, ALU.add, ALU.min,
                        neg_max[:, n % 2, m:m + 1]).then_inc(s_biased, 1)

            STEPS = 3 if a else 1

            def combine(turn, n):
                i, par = n % QT, n % 2
                L = (i + 1) * P
                s = Steps(n * STEPS)
                dve.wait_ge(exp_done, turn * (2 * TURN_TILES) + (2 * n + 2))
                nc.vector.reciprocal(rden[:, n % 4, :], den[:, n % 4, :]).then_inc(step, s.up())
                dve.wait_ge(step, turn * (TURN_TILES * STEPS) + s.now)
                if a:
                    nc.vector.tensor_tensor(r2[:, par:par + 1], rden[:, n % 4, 1:2], neg_lam, ALU.mult).then_inc(step, s.up())
                    dve.wait_ge(step, turn * (TURN_TILES * STEPS) + s.now)
                    nc.vector.tensor_scalar(e[:, par, 1, 0:L], e[:, par, 1, 0:L], r2[:, par:par + 1], None,
                                            ALU.mult).then_inc(step, s.up())
                    since(dve, wT_in_psum, turn * TURN_GROUPS + (group_at(n - 1) if n else 0))
                    dve.wait_ge(step, turn * (TURN_TILES * STEPS) + s.now)
                    nc.vector.scalar_tensor_tensor(w[:, par, 0, 0:L], e[:, par, 0, 0:L], rden[:, n % 4, 0:1],
                                                   e[:, par, 1, 0:L], ALU.mult, ALU.add).then_inc(w_ready, 1)

            def output(turn, n):
                par = n % 2
                dve.wait_ge(o_in_psum, turn * TURN_TILES + (n + 1))
                since(dve, o_stored[par], turn * (8 * TURN_TILES) + 16 * (n // 2))
                if a:
                    nc.vector.tensor_copy(o[:, par, :], bank[:, 6 + par, 0:P]).then_inc(o_ready, 1)
                else:
                    for m in range(2):
                        ins = nc.vector.tensor_scalar(o[:, par, m * HD:(m + 1) * HD], bank[:, 6 + par, m * HD:(m + 1) * HD],
                                                      rden[:, n % 4, m:m + 1], None, ALU.mult)
                    ins.then_inc(o_ready, 1)

            def turn_of(turn):
                dve.wait_ge(loaded[0], turn * 80 + 80)
                bias(turn, 0)
                for n in range(TURN_TILES):
                    combine(turn, n)
                    if n + 1 == QT:
                        dve.wait_ge(loaded[1], turn * 80 + 80)
                    if n + 1 < TURN_TILES:
                        bias(turn, n + 1)
                    if n:
                        output(turn, n - 1)
                output(turn, TURN_TILES - 1)

            turns(dve, TURNS, turn_of)

        @block.scalar
        def _(act):
            def exps(turn, n):
                L = (n % QT + 1) * P
                if a:
                    since(act, w_ready, turn * TURN_TILES + max(0, n - 1))
                else:
                    since(act, wT_in_psum, turn * TURN_GROUPS + (group_at(n - 1) if n else 0))
                    since(act, o_ready, turn * TURN_TILES + max(0, n - 3))
                for m in range(2):
                    act.wait_ge(s_biased, turn * (2 * TURN_TILES) + (2 * n + m + 1))
                    nc.scalar.activation(e[:, n % 2, m, 0:L], neg_s[:, m, 0:L], ACT.Exp, bias=neg_max[:, n % 2, m:m + 1],
                                         scale=-1.0, accum_out=den[:, n % 4, m:m + 1]).then_inc(exp_done, 1)

            def take_weights_T(turn, n):
                i = n % QT
                g = group_at(n)
                since(act, o_in_psum, turn * TURN_TILES + max(0, n - 1))
                for mw in range(MW):
                    for j0 in range(0, i + 1, 4):
                        j1 = min(j0 + 4, i + 1)
                        act.wait_ge(wT_in_psum, turn * TURN_GROUPS + (g + 1))
                        nc.scalar.copy(wT[:, n % 2, mw, j0:j1, :].rearrange("p j t -> p (j t)"),
                                       bank[:, 4 + g % 2, 0:(j1 - j0) * P]).then_inc(wT_ready, 1)
                        g += 1

            def turn_of(turn):
                exps(turn, 0)
                for n in range(TURN_TILES):
                    take_weights_T(turn, n)
                    if n + 1 < TURN_TILES:
                        exps(turn, n + 1)

            turns(act, TURNS, turn_of)


PR = P // 4


def attend_sample(nc, io, sems, ident, bank, neg_lam, mixer):
    a = mixer == "a"
    with ExitStack() as ctx:
        def sb(name, shape, dt=F32):
            return ctx.enter_context(nc.sbuf_tensor(f"{name}_s{mixer}", shape, dt))

        def sem(name):
            return sems(f"{name}_s{mixer}")

        TILES_OF = [4] * (PAGES // 4) if a else [2, 2, 2, 1]
        C = len(TILES_OF)
        R = min(4, C)
        KEYS = P * sum(TILES_OF)
        LAG = 2
        FILL = 64 if a else 16
        heads = 4 if a else 8
        width = SEG // heads

        kbuf = [sb(f"keys{r}", [P, 4, 4, P]) for r in range(R)]
        vbuf = [sb(f"values{r}", [P, 4, SEG]) for r in range(R)]
        bias = sb("bias", [P, KEYS + DQ])
        neg_s = sb("neg_scores", [P, KEYS + DQ])
        e = sb("exps", [P, KEYS + DQ])
        eT = sb("exps_T", [P, sum(TILES_OF), P])
        eT_new = sb("exps_T_new", [DQ, P])
        v_new = sb("v_new", [DQ, SEG])
        qs = sb("q_new", [P, 4, NS])
        kn = sb("k_new", [P, 4, NS])
        q_all = sb("q_blocks_all", [P, DB, 4, PR])
        qd = sb("q_blocks", [P, 4, PR])
        kd = sb("k_new_batch", [P, 4, DQ])
        pages = sb("pages", [1, DB * PAGES], I32)
        mins = sb("mins", [P, C + 1])
        neg_max = sb("neg_max", [P, 1])
        den = sb("den", [P, 1])
        rden = sb("rden", [P, 1])
        rvec = sb("rvec", [P, 1])
        second = sb("second_map", [P, 1])
        coef = sb("coef", [P, 1])
        sel = sb("sel", [P, heads, DQ])
        o_rows = sb("o_rows", [P, P])
        o = sb("o", [DQ, SEG])
        gate = sb("gate", [P, C + 1])

        consts_loaded = sem("consts_loaded")
        k_loaded = [sem(f"k_loaded{r}") for r in range(R)]
        v_loaded = [sem(f"v_loaded{r}") for r in range(R)]
        v_new_loaded = sem("v_new_loaded")
        setup = sem("setup")
        qd_ready = sem("qd_ready")
        scored = sem("scored")
        s_biased = sem("s_biased")
        max_ready = sem("max_ready")
        exp_done = sem("exp_done")
        e_transposed = sem("e_transposed")
        eT_ready = sem("eT_ready")
        values_done = sem("values_done")
        step = sem("step")
        o_scaled = sem("o_scaled")
        o_folded = sem("o_folded")
        o_ready = sem("o_ready")
        o_stored = sem("o_stored")
        first_q, first_k = (0, 4) if a else (8, 12)
        new_scores = bank[:, 4, 0:DQ]

        def pages_of(engine, b, c):
            return nc.values_load_multi_w_load_instructions(
                pages[0:1, ds(b * PAGES + 4 * c, 4)], engines=[engine], min_val=0,
                max_val=io["cache_k"].shape[0] - 1)[1]

        block = ctx.enter_context(nc.Block())

        @block.sync
        def _(sp):
            def load_k(b, c):
                r = c % R
                if not (isinstance(b, int) and b * C + c < R):
                    sp.wait_ge(scored, b * (C + 1) + (c - R + 1 if c >= R else c - R))
                if a:
                    for j, page in enumerate(pages_of(mybir.EngineType.SP, b, c)):
                        sp.dma_start(kbuf[r][:, j, :, :].rearrange("p h t -> p (h t)"),
                                     io["cache_k"][ds(page, 1), :, :].rearrange("a p c -> (a p) c")).then_inc(k_loaded[r], 16)
                else:
                    n, at = TILES_OF[c], sum(TILES_OF[:c])
                    sp.dma_start(kbuf[r][:, 0:n, :, :].rearrange("p j h t -> p (j h t)"),
                                 io["win_k"][ds(b, 1), :, at * SEG:(at + n) * SEG].rearrange("a p c -> (a p) c")).then_inc(k_loaded[r], 16)

            sp.dma_start(qs[:, :, :], io["qkT"][first_q:first_q + 4, :, SEQ:NT].rearrange("h p t -> p h t")).then_inc(consts_loaded, 16)
            sp.dma_start(kn[:, :, :], io["qkT"][first_k:first_k + 4, :, SEQ:NT].rearrange("h p t -> p h t")).then_inc(consts_loaded, 16)
            sp.dma_start(bias[:, :], io[f"bias_{mixer}"]).then_inc(consts_loaded, 16)
            sp.dma_start(second[:, :], io["second_map"]).then_inc(consts_loaded, 16)
            sp.dma_start(pages[:, :], io["page_table"]).then_inc(consts_loaded, 16)
            sp.dma_start(sel[:, :, :], io[f"sel_{mixer}"]).then_inc(consts_loaded, 16)
            sp.wait_ge(consts_loaded, 96)
            def keys_of(b):
                for c in range(C):
                    load_k(b, c)

            turns(sp, DB, keys_of)

        @block.gpsimd
        def _(pool):
            def load_v(b, c):
                r = c % R
                if not (isinstance(b, int) and b * C + c < R):
                    pool.wait_ge(values_done, b * C + (c - R + 1))
                if a:
                    for j, page in enumerate(pages_of(mybir.EngineType.Pool, b, c)):
                        pool.dma_start(vbuf[r][:, j, :],
                                     io["cache_v"][ds(page, 1), :, :].rearrange("a p c -> (a p) c")).then_inc(v_loaded[r], 16)
                else:
                    n, at = TILES_OF[c], sum(TILES_OF[:c])
                    pool.dma_start(vbuf[r][:, 0:n, :].rearrange("p j c -> p (j c)"),
                                 io["win_v"][ds(b, 1), :, at * SEG:(at + n) * SEG].rearrange("a p c -> (a p) c")).then_inc(v_loaded[r], 16)
                if c == C - 1:
                    since(pool, values_done, b * C)
                    v_rows = io["va"] if a else io["vb"]
                    pool.dma_start(v_new[:, :], v_rows[ds(b * DQ + SEQ, DQ), :]).then_inc(v_new_loaded, 16)

            def store(b):
                pool.wait_ge(o_ready, b + 1)
                pool.dma_start(io["mix"][ds(b * DQ + SEQ, DQ), (0 if a else SEG):(SEG if a else D)], o[:, :]).then_inc(o_stored, 16)

            pool.wait_ge(consts_loaded, 96)
            for c in range(C):
                load_v(0, c)
            with pool.Fori(1, DB) as b:
                for c in range(C):
                    load_v(b, c)
                    if c == min(2, C - 1):
                        store(b - 1)
            store(DB - 1)
            pool.wait_ge(o_stored, 16 * DB)


        @block.tensor
        def _(pe):
            def scores(b, c):
                n = TILES_OF[c]
                pe.wait_ge(k_loaded[c % R], b * (FILL * (C // R)) + FILL * (c // R + 1))
                if c == 0:
                    pe.wait_ge(qd_ready, b * 2 + 2)
                if not (isinstance(b, int) and b == 0 and c < R):
                    pe.wait_ge(s_biased, b * (C + 1) + (c - R + 1 if c >= R else c - R))
                if c == C - 1:
                    since(pe, s_biased, b * (C + 1))
                    if not isinstance(b, int):
                        pe.wait_ge(o_ready, b - 1)
                for h in range(4):
                    ins = nc.tensor.matmul(bank[h * PR:(h + 1) * PR, c % R, 0:n * P], qd[:, h, :],
                                           kbuf[c % R][:, 0:n, h, :], start=True, stop=True)
                ins.then_inc(scored, 1)
                if c == C - 1:
                    for h in range(4):
                        ins = nc.tensor.matmul(bank[h * PR:(h + 1) * PR, 4, 0:DQ], qd[:, h, :],
                                               kd[:, h, :], start=True, stop=True)
                    ins.then_inc(scored, 1)

            def transpose_exps(b):
                pe.wait_ge(exp_done, b + 1)
                for c in range(C):
                    n, at = TILES_OF[c], sum(TILES_OF[:c])
                    since(pe, eT_ready, b * C + max(0, c - 1))
                    for j in range(n):
                        ins = nc.tensor.transpose(bank[:, 5 + c % 2, j * P:(j + 1) * P],
                                                  e[:, (at + j) * P:(at + j + 1) * P], ident)
                    if c == 0:
                        ins = nc.tensor.transpose(bank[0:DQ, 7, P:2 * P], e[:, KEYS:KEYS + DQ], ident)
                    ins.then_inc(e_transposed, 1)

            def values(b, c):
                n, at = TILES_OF[c], sum(TILES_OF[:c])
                pe.wait_ge(v_loaded[c % R], b * (FILL * (C // R)) + FILL * (c // R + 1))
                pe.wait_ge(eT_ready, b * C + (c + 1))
                if c == 0:
                    since(pe, o_scaled, b)
                if c == C - 1:
                    pe.wait_ge(v_new_loaded, b * 16 + 16)
                for j in range(n):
                    for h in range(4):
                        ins = nc.tensor.matmul(bank[h * PR:(h + 1) * PR, 7, 0:P], eT[:, at + j, h * PR:(h + 1) * PR],
                                               vbuf[c % R][:, j, h * P:(h + 1) * P], start=(c == 0 and j == 0), stop=False)
                if c == C - 1:
                    for h in range(4):
                        ins = nc.tensor.matmul(bank[h * PR:(h + 1) * PR, 7, 0:P], eT_new[:, h * PR:(h + 1) * PR],
                                               v_new[:, h * P:(h + 1) * P], start=False, stop=True)
                ins.then_inc(values_done, 1)

            def fold(b):
                pe.wait_ge(o_scaled, b + 1)
                since(pe, o_ready, b)
                pe.wait_ge(s_biased, min(b + 2, DB) * (C + 1) if isinstance(b, int) else b * (C + 1) + 2 * (C + 1))
                for h in range(heads):
                    ins = nc.tensor.matmul(bank[0:DQ, 4, h * width:(h + 1) * width], sel[:, h, :],
                                           o_rows[:, 0:P] if a else o_rows[:, h % 2 * HD:(h % 2 + 1) * HD],
                                           start=True, stop=True)
                ins.then_inc(o_folded, 1)

            pe.wait_ge(consts_loaded, 96)
            for c in range(C):
                scores(0, c)
            def turn_of(b):
                for c in range(C):
                    scores(b + 1, c)
                    if c == LAG - 1:
                        transpose_exps(b)
                    if c >= LAG:
                        values(b, c - LAG)
                for c in range(C - LAG, C):
                    values(b, c)
                fold(b)

            turns(pe, DB - 1, turn_of)
            transpose_exps(DB - 1)
            for c in range(C):
                values(DB - 1, c)
            fold(DB - 1)

        @block.vector
        def _(dve):
            nc.vector.memset(q_all[:, :, :, :], 0.0).then_inc(setup, 1)
            dve.wait_ge(consts_loaded, 96)
            dve.wait_ge(setup, 1)
            for h in range(4):
                for m in range(2):
                    half = slice(m * HD, (m + 1) * HD)
                    col = m * DQ
                    nc.vector.tensor_copy(q_all[half, :, h, col:col + DQ],
                                          qs[half, h, :].rearrange("p (b q) -> p b q", q=DQ)).then_inc(setup, 1)
            nc.vector.tensor_scalar(coef[:, :], second[:, :], -1.0 if a else 0.0, 1.0, ALU.mult, ALU.add).then_inc(setup, 1)
            dve.wait_ge(setup, 10)
            if a:
                nc.vector.scalar_tensor_tensor(coef[:, :], second[:, :], neg_lam, coef[:, :],
                                               ALU.mult, ALU.add).then_inc(setup, 1)
                dve.wait_ge(setup, 11)

            def blocks(b):
                since(dve, scored, b * (C + 1))
                nc.vector.tensor_copy(kd[:, :, :], kn[:, :, ds(b * DQ, DQ)]).then_inc(qd_ready, 1)
                nc.vector.tensor_copy(qd[:, :, :], q_all[:, ds(b, 1), :, :].rearrange("p a h r -> p (a h) r")).then_inc(qd_ready, 1)

            def bias_scores(b, c):
                n = KEYS if c == C else sum(TILES_OF[:c]) * P
                w = DQ if c == C else TILES_OF[c] * P
                src = new_scores if c == C else bank[:, c % R, 0:w]
                dve.wait_ge(scored, b * (C + 1) + (c + 1))
                since(dve, exp_done, b)
                nc.vector.memset(gate[:, c:c + 1], 0.0)
                nc.vector.tensor_tensor_reduce(neg_s[:, n:n + w], src, bias[:, n:n + w], -1.0, 3e38, ALU.add, ALU.min,
                                               mins[:, c:c + 1]).then_inc(s_biased, 1)
                if c == C:
                    dve.wait_ge(s_biased, b * (C + 1) + (C + 1))
                    nc.vector.tensor_reduce(neg_max[:, :], mins[:, :], AX_X, ALU.min).then_inc(max_ready, 1)

            def scale_output(b):
                dve.wait_ge(exp_done, b + 1)
                nc.vector.reciprocal(rden[:, :], den[:, :]).then_inc(step, 1)
                dve.wait_ge(step, b * 2 + 1)
                nc.vector.tensor_tensor(rvec[:, :], rden[:, :], coef[:, :], ALU.mult).then_inc(step, 1)
                dve.wait_ge(step, b * 2 + 2)

            def take_output(b):
                dve.wait_ge(values_done, b * C + C)
                since(dve, o_folded, b)
                nc.vector.tensor_scalar(o_rows[:, :], bank[:, 7, 0:P], rvec[:, :], None, ALU.mult).then_inc(o_scaled, 1)
                dve.wait_ge(o_folded, b + 1)
                since(dve, o_stored, b * 16)
                nc.vector.tensor_copy(o[:, :], bank[0:DQ, 4, :]).then_inc(o_ready, 1)

            blocks(0)
            for c in range(C + 1):
                bias_scores(0, c)
            def turn_of(b):
                scale_output(b)
                blocks(b + 1)
                for c in range(C + 1):
                    bias_scores(b + 1, c)
                take_output(b)

            turns(dve, DB - 1, turn_of)
            scale_output(DB - 1)
            take_output(DB - 1)

        @block.scalar
        def _(act):
            def exps(b):
                act.wait_ge(max_ready, b + 1)
                since(act, e_transposed, b * C)
                since(act, step, b * 2)
                nc.scalar.activation(e[:, :], neg_s[:, :], ACT.Exp, bias=neg_max[:, :], scale=-1.0,
                                     accum_out=den[:, :]).then_inc(exp_done, 1)

            def take_exps_T(b):
                since(act, values_done, b * C)
                for c in range(C):
                    n, at = TILES_OF[c], sum(TILES_OF[:c])
                    act.wait_ge(e_transposed, b * C + (c + 1))
                    if c == 0:
                        nc.scalar.copy(eT_new[:, :], bank[0:DQ, 7, P:2 * P])
                    nc.scalar.copy(eT[:, at:at + n, :].rearrange("p j r -> p (j r)"),
                                   bank[:, 5 + c % 2, 0:n * P]).then_inc(eT_ready, 1)

            exps(0)
            def turn_of(b):
                take_exps_T(b)
                exps(b + 1)

            turns(act, DB - 1, turn_of)
            take_exps_T(DB - 1)


PH = 8
TOPK = 16
PICKS = PH * TOPK


def mix_and_route(nc, io, sems, ident, bank):
    with ExitStack() as ctx:
        def sb(name, shape, dt=F32):
            return ctx.enter_context(nc.sbuf_tensor(name, shape, dt))

        w_out = sb("w_out_sb", [P, KD, D])
        w_q = sb("w_q_sb", [P, KD, D])
        sub_keys = sb("sub_keys_sb", [P, PH, 2, P])
        iota = sb("iota_sb", [P, P])
        g2T = sb("g2_T", [P, KD])
        subln = sb("subln_sb", [P, 1])
        m_rows = sb("mixed_rows", [P, D])
        x_rows = sb("x_rows4", [P, D])
        sq = sb("squares4", [P, D])
        oss = sb("o_sumsq", [P, 4])
        ostd = sb("o_std", [P, 4])
        orstd = sb("o_rstd", [P, 4])
        mT = sb("mixed_T", [P, KD, P])
        h = sb("h_rows4", [P, D])
        hss = sb("h_sumsq4", [P, 1])
        hstd = sb("h_std4", [P, 1])
        hrstd = sb("h_rstd4", [P, 1])
        hT = sb("h_T", [P, KD, P])
        xr = sb("h_scaled", [P, D])
        x2T = sb("x2_T", [P, KD, P])
        qT = sb("peer_q_T", [P, PH, P])
        s1 = sb("key_scores", [P, 2 * PH, P])
        s2 = sb("key_scores_rest", [P, 2 * PH, P])
        best = sb("best_scores", [P, 2 * PH, TOPK])
        at = sb("best_at", [P, 2 * PH, TOPK], U32)
        at_f = sb("best_at_f", [P, 2 * PH, TOPK])
        cand = sb("cand", [P, PH, TOPK * TOPK])
        cand2 = sb("cand_rest", [P, PH, TOPK * TOPK])
        top = sb("top_scores", [P, PH, TOPK])
        top_at = sb("top_at", [P, PH, TOPK], U32)
        side = sb("top_side", [P, 2, PH, TOPK], U32)
        side_f = sb("top_side_f", [P, 2, PH, TOPK])
        onehot = [sb(f"onehot{c}", [P, PH, TOPK, TOPK]) for c in range(2)]
        eps = sb("eps", [P, 1])
        top_e = sb("top_exps", [P, PH, TOPK])
        gsum = sb("gate_sum", [P, PH])
        picks = sb("picks", [P, 3, PH, TOPK])
        picksT = sb("picks_T", [P, 3, TP])
        gate = sb("gate4", [P, 24])

        w_out_loaded, w_q_loaded = sems("w_out_loaded"), sems("w_q_loaded")
        consts_loaded = sems("c4_loaded")
        zeroed = sems("zeroed4")
        m_loaded = sems("m_loaded")
        x_loaded = sems("x4_loaded")
        f_step = sems("front_step")
        s_step = sems("selection_step")
        subln_ready = sems("subln_ready")
        oss_ready = sems("oss_ready")
        ostd_ready = sems("ostd_ready")
        m_ready = sems("m_ready")
        mT_in_psum = sems("mT_in_psum")
        mT_ready = sems("mT_ready")
        h_in_psum = sems("h_in_psum")
        h_ready = sems("h4_ready")
        hss_ready = sems("hss_ready")
        hrstd_ready = sems("hrstd_ready")
        place_equal = sems("place_equal")
        place_valued = sems("place_valued")
        hstd_ready = sems("hstd_ready")
        xr_ready = sems("xr_ready")
        hT_in_psum = sems("hT_in_psum")
        hT_ready = sems("hT_ready")
        hT_stored = sems("hT_stored")
        x2T_stored = sems("x2T_stored")
        x2T_in_psum = sems("x2T_in_psum")
        x2T_ready = sems("x2T_ready")
        q_in_psum = sems("q_in_psum")
        qT_ready = sems("qT_ready")
        s_in_psum = sems("ks_in_psum")
        s_ready = sems("ks_ready")
        s_used = sems("ks_used")
        shifted = sems("top_shifted")
        exp_done = sems("top_exp_done")
        picks_ready = sems("picks_ready")
        picks_in_psum = sems("picks_in_psum")
        picksT_ready = sems("picksT_ready")
        picksT_stored = sems("picksT_stored")

        block = ctx.enter_context(nc.Block())

        @block.sync
        def _(sp):
            sp.dma_start(g2T[:, :], io["g2"]).then_inc(consts_loaded, 16)
            sp.dma_start(subln[:, :], io["subln"]).then_inc(consts_loaded, 16)
            sp.wait_ge(zeroed, 1)
            for c in range(2):
                half = slice(c * HD, (c + 1) * HD)
                sp.dma_start(sub_keys[half, :, c, :], io["sub_keys"][half, :, :]).then_inc(consts_loaded, 16)
            sp.dma_start(iota[:, :], io["iota"]).then_inc(consts_loaded, 16)
            sp.dma_start(m_rows[:, :], io["mix"][0:P, :]).then_inc(m_loaded, 16)
            sp.dma_start(x_rows[:, :], io["x"][0:P, :]).then_inc(x_loaded, 16)
            sp.dma_start(w_out[:, :, :], io["w_out"].rearrange("(k p) c -> p k c", p=P)).then_inc(w_out_loaded, 16)
            sp.dma_start(w_q[:, :, :], io["w_q"].rearrange("(k p) c -> p k c", p=P)).then_inc(w_q_loaded, 16)
            def turn_of(t):
                sp.wait_ge(mT_in_psum, t * 2 + 2)
                sp.dma_start(m_rows[:, :], io["mix"][ds(t * P + P, P), :]).then_inc(m_loaded, 16)
                sp.wait_ge(h_ready, t + 1)
                sp.wait_ge(hT_ready, t * 2 + 2)
                sp.wait_ge(x2T_ready, t * 2 + 2)
                sp.dma_start(x_rows[:, :], io["x"][ds(t * P + P, P), :]).then_inc(x_loaded, 16)
                sp.dma_start(io["hT"][:, :, ds(t * P, P)].rearrange("k p t -> p k t"), hT[:, :, :]).then_inc(hT_stored, 16)
                sp.dma_start(io["x2T"][:, :, ds(t * P, P)].rearrange("k p t -> p k t"), x2T[:, :, :]).then_inc(x2T_stored, 16)

            turns(sp, TILES - 1, turn_of)
            sp.wait_ge(hT_ready, 2 * TILES)
            sp.wait_ge(x2T_ready, 2 * TILES)
            sp.dma_start(io["x2T"][:, :, (TILES - 1) * P:TP].rearrange("k p t -> p k t"), x2T[:, :, :]).then_inc(x2T_stored, 16)
            sp.wait_ge(x2T_stored, 16 * TILES)
            sp.dma_start(io["hT"][:, :, (TILES - 1) * P:TP].rearrange("k p t -> p k t"), hT[:, :, :]).then_inc(hT_stored, 16)
            for n, cols in ((TILES - 1, slice(0, TP - P)), (TILES, slice(TP - P, TP))):
                sp.wait_ge(picksT_ready, n)
                sp.dma_start(io["picksT"][:, :, cols], picksT[:, :, cols]).then_inc(picksT_stored, 16)
            sp.wait_ge(hT_stored, 16 * TILES)
            sp.wait_ge(picksT_stored, 32)

        @block.tensor
        def _(pe):
            def front(t):
                pe.wait_ge(m_ready, t + 1)
                since(pe, x2T_ready, t * 2)
                since(pe, hT_ready, t * 2)
                for b in range(2):
                    for j in range(4):
                        ins = nc.tensor.transpose(bank[:, b, j * P:(j + 1) * P], m_rows[:, (4 * b + j) * P:(4 * b + j + 1) * P], ident)
                    ins.then_inc(mT_in_psum, 1)
                since(pe, s_ready, t * 4)
                pe.wait_ge(w_out_loaded, 16)
                for k in range(KD):
                    if k % 4 == 0:
                        pe.wait_ge(mT_ready, t * 2 + k // 4 + 1)
                    for c in range(2):
                        ins = nc.tensor.matmul(bank[:, 2 + c, :], mT[:, k, :], w_out[:, k, c * 512:(c + 1) * 512],
                                               start=(k == 0), stop=(k == KD - 1))
                ins.then_inc(h_in_psum, 1)
                pe.wait_ge(h_ready, t + 1)
                for b in range(2):
                    for j in range(4):
                        ins = nc.tensor.transpose(bank[:, b, j * P:(j + 1) * P], h[:, (4 * b + j) * P:(4 * b + j + 1) * P], ident)
                    ins.then_inc(hT_in_psum, 1)
                pe.wait_ge(xr_ready, t + 1)
                for b in range(2):
                    for j in range(4):
                        ins = nc.tensor.transpose(bank[:, 4 + b, j * P:(j + 1) * P], xr[:, (4 * b + j) * P:(4 * b + j + 1) * P], ident)
                    ins.then_inc(x2T_in_psum, 1)
                since(pe, picksT_ready, t - 1)
                since(pe, qT_ready, t * 2)
                pe.wait_ge(x2T_ready, t * 2 + 2)
                pe.wait_ge(w_q_loaded, 16)
                for hd in range(PH):
                    for k in range(KD):
                        ins = nc.tensor.matmul(bank[:, 6 + hd // 4, (hd % 4) * P:(hd % 4 + 1) * P],
                                               w_q[:, k, hd * P:(hd + 1) * P], x2T[:, k, :],
                                               start=(k == 0), stop=(k == KD - 1))
                    if hd % 4 == 3:
                        ins.then_inc(q_in_psum, 1)
                pe.wait_ge(qT_ready, t * 2 + 2)
                for hd in range(PH):
                    ins = nc.tensor.matmul(bank[:, 2 + hd // 2, (hd % 2) * 2 * P:(hd % 2 + 1) * 2 * P], qT[:, hd, :],
                                           sub_keys[:, hd, :, :].rearrange("p c n -> p (c n)"), start=True, stop=True)
                    if hd % 2:
                        ins.then_inc(s_in_psum, 1)

            def transpose_picks(t):
                pe.wait_ge(picks_ready, t + 1)
                for j in range(3):
                    ins = nc.tensor.transpose(bank[:, 6, j * P:(j + 1) * P], picks[:, j, :, :].rearrange("p h s -> p (h s)"), ident)
                ins.then_inc(picks_in_psum, 1)

            pe.wait_ge(consts_loaded, 80)
            front(0)
            front(1)
            transpose_picks(0)
            with pe.Fori(2, TILES) as t:
                front(t)
                transpose_picks(t - 1)
            transpose_picks(TILES - 1)

        @block.scalar
        def _(act):
            def std_mixed(t):
                act.wait_ge(m_loaded, t * 16 + 16)
                for hd in range(4):
                    cols = slice(hd * P, (hd + 1) * P)
                    nc.scalar.activation(sq[:, cols], m_rows[:, cols], ACT.Square,
                                         accum_out=oss[:, hd:hd + 1]).then_inc(oss_ready, 1)
                act.wait_ge(oss_ready, t * 4 + 4)
                nc.scalar.activation(ostd[:, :], oss[:, :], ACT.Sqrt, bias=eps[:, :], scale=1.0 / P).then_inc(ostd_ready, 1)

            def front(t):
                for b in range(2):
                    act.wait_ge(mT_in_psum, t * 2 + b + 1)
                    dst = mT[:, 4 * b:4 * b + 4, :].rearrange("p k t -> p (k t)")
                    if b == 0:
                        nc.scalar.activation(dst, bank[:, b, :], ACT.Copy, scale=subln[:, 0:1]).then_inc(mT_ready, 1)
                    else:
                        nc.scalar.copy(dst, bank[:, b, :]).then_inc(mT_ready, 1)
                act.wait_ge(h_ready, t + 1)
                nc.scalar.activation(sq[:, :], h[:, :], ACT.Square, accum_out=hss[:, :]).then_inc(hss_ready, 1)
                act.wait_ge(hss_ready, t + 1)
                nc.scalar.activation(hstd[:, :], hss[:, :], ACT.Sqrt, bias=eps[:, :], scale=1.0 / D).then_inc(hstd_ready, 1)
                act.wait_ge(hrstd_ready, t + 1)
                since(act, x2T_in_psum, t * 2)
                nc.scalar.activation(xr[:, :], h[:, :], ACT.Copy, scale=hrstd[:, 0:1]).then_inc(xr_ready, 1)
                since(act, hT_stored, t * 16)
                for b in range(2):
                    act.wait_ge(hT_in_psum, t * 2 + b + 1)
                    nc.scalar.copy(hT[:, 4 * b:4 * b + 4, :].rearrange("p k t -> p (k t)"), bank[:, b, :]).then_inc(hT_ready, 1)
                since(act, x2T_stored, t * 16)
                since(act, q_in_psum, t * 2)
                for b in range(2):
                    act.wait_ge(x2T_in_psum, t * 2 + b + 1)
                    for k in range(4 * b, 4 * b + 4):
                        ins = nc.scalar.activation(x2T[:, k, :], bank[:, 4 + b, (k - 4 * b) * P:(k - 4 * b + 1) * P],
                                                   ACT.Copy, scale=g2T[:, k:k + 1])
                    ins.then_inc(x2T_ready, 1)
                if not (isinstance(t, int) and t == TILES - 1):
                    std_mixed(t + 1)
                for b in range(2):
                    act.wait_ge(q_in_psum, t * 2 + b + 1)
                    nc.scalar.copy(qT[:, 4 * b:4 * b + 4, :].rearrange("p k t -> p (k t)"), bank[:, 6 + b, :]).then_inc(qT_ready, 1)
                since(act, s_used, t)
                sides = s1[:, :, :].rearrange("p (c h) n -> p h c n", c=2)
                for g in range(4):
                    act.wait_ge(s_in_psum, t * 4 + g + 1)
                    nc.scalar.copy(sides[:, 2 * g:2 * g + 2, :, :],
                                   bank[:, 2 + g, :].rearrange("p (h c n) -> p h c n", h=2, c=2)).then_inc(s_ready, 1)

            def selection(t):
                act.wait_ge(shifted, t + 1)
                nc.scalar.activation(top_e[:, :, :], top_e[:, :, :], ACT.Exp).then_inc(exp_done, 1)
                act.wait_ge(picks_in_psum, t + 1)
                for j in range(3):
                    ins = nc.scalar.copy(picksT[:, j, ds(t * P, P)], bank[:, 6, j * P:(j + 1) * P])
                ins.then_inc(picksT_ready, 1)

            act.wait_ge(subln_ready, 2)
            std_mixed(0)
            front(0)
            def turn_of(t):
                front(t + 1)
                selection(t)

            turns(act, TILES - 2, turn_of)
            turn_of(TILES - 2)
            selection(TILES - 1)

        @block.gpsimd
        def _(pool):
            nc.gpsimd.memset(sub_keys[:, :, :, :], 0.0).then_inc(zeroed, 1)

            def values(t):
                pool.wait_ge(place_equal, t * 2 + 1)
                nc.gpsimd.tensor_tensor(
                    onehot[0][:, :, :, :], onehot[0][:, :, :, :],
                    at_f[:, 0:PH, :].unsqueeze(2).broadcast_to([P, PH, TOPK, TOPK]),
                    ALU.mult).then_inc(place_valued, 1)

            turns(pool, TILES, values)

        @block.vector
        def _(dve):
            S_STEPS = 18

            def norm_mixed(t):
                dve.wait_ge(ostd_ready, t + 1)
                nc.vector.reciprocal(orstd[:, :], ostd[:, :]).then_inc(f_step, 1)
                dve.wait_ge(f_step, t + 1)
                m4 = m_rows[:, 0:SEG].rearrange("p (h e) -> p h e", h=4)
                nc.vector.tensor_tensor(m4, m4, orstd[:, :].unsqueeze(2).broadcast_to([P, 4, P]), ALU.mult).then_inc(m_ready, 1)

            def add_residual(t):
                dve.wait_ge(h_in_psum, t + 1)
                dve.wait_ge(x_loaded, t * 16 + 16)
                since(dve, hT_in_psum, t * 2)
                nc.vector.tensor_tensor(h[:, :], bank[:, 2:4, :].rearrange("p b c -> p (b c)"), x_rows[:, :], ALU.add).then_inc(h_ready, 1)

            def invert_norm(t):
                dve.wait_ge(hstd_ready, t + 1)
                nc.vector.reciprocal(hrstd[:, :], hstd[:, :]).then_inc(hrstd_ready, 1)

            def top16(n, src, rest, vals, idx, s, t, last_read):
                def hold():
                    dve.wait_ge(s_step, t * S_STEPS + s.now)
                    nc.vector.memset(gate[:, s.n:s.n + 1], 0.0)

                for half in range(2):
                    part = slice(8 * half, 8 * half + 8)
                    data = rest if half else src
                    for g in range(n):
                        ins = nc.vector.max(vals[:, g, part], data[:, g, :])
                    ins.then_inc(s_step, s.up())
                    hold()
                    for g in range(n):
                        ins = nc.vector.max_index(idx[:, g, part], vals[:, g, part], data[:, g, :])
                        if not half:
                            ins = nc.vector.match_replace(rest[:, g, :], vals[:, g, part], src[:, g, :], -3e38)
                    ins.then_inc(s_step, s.up())
                    if not half:
                        hold()
                    if not half and last_read is not None:
                        dve.wait_ge(s_step, t * S_STEPS + s.now)
                        nc.vector.memset(gate[:, 21:22], 0.0).then_inc(last_read, 1)
                    yield

            def selection(t, s):
                now = lambda: t * S_STEPS + s.now
                dve.wait_ge(s_ready, t * 4 + 4)
                nc.vector.memset(gate[:, 22:23], 0.0)
                yield from top16(2 * PH, s1, s2, best, at, s, t, s_used)
                dve.wait_ge(s_step, now())
                nc.vector.tensor_copy(at_f[:, :, :], at[:, :, :]).then_inc(s_step, s.up())
                nc.vector.tensor_tensor(
                    cand[:, :, :].rearrange("p h (a b) -> p h a b", a=TOPK),
                    best[:, 0:PH, :].unsqueeze(3).broadcast_to([P, PH, TOPK, TOPK]),
                    best[:, PH:2 * PH, :].unsqueeze(2).broadcast_to([P, PH, TOPK, TOPK]), ALU.add).then_inc(s_step, s.up())
                yield
                dve.wait_ge(s_step, now())
                nc.vector.memset(gate[:, 23:24], 0.0)
                yield from top16(PH, cand, cand2, top, top_at, s, t, None)
                dve.wait_ge(s_step, now())
                since(dve, exp_done, t)
                nc.vector.tensor_tensor(top_e[:, :, :], top[:, :, :], top[:, :, 0:1].broadcast_to([P, PH, TOPK]),
                                        ALU.subtract).then_inc(shifted, 1)
                nc.vector.tensor_scalar(side[:, 0, :, :], top_at[:, :, :], 4, None, ALU.logical_shift_right).then_inc(s_step, s.up())
                nc.vector.tensor_scalar(side[:, 1, :, :], top_at[:, :, :], TOPK - 1, None, ALU.bitwise_and).then_inc(s_step, s.up())
                dve.wait_ge(s_step, now())
                nc.vector.tensor_copy(side_f[:, :, :, :].rearrange("p c h s -> p (c h s)"),
                                      side[:, :, :, :].rearrange("p c h s -> p (c h s)")).then_inc(s_step, s.up())
                since(dve, picks_in_psum, t)
                dve.wait_ge(s_step, now())
                for c in range(2):
                    nc.vector.tensor_tensor(
                        onehot[c][:, :, :, :], side_f[:, c, :, :].unsqueeze(3).broadcast_to([P, PH, TOPK, TOPK]),
                        iota[:, 0:TOPK].unsqueeze(1).unsqueeze(1).broadcast_to([P, PH, TOPK, TOPK]),
                        ALU.is_equal).then_inc(place_equal, 1)
                dve.wait_ge(place_equal, t * 2 + 2)
                nc.vector.tensor_tensor(
                    onehot[1][:, :, :, :], onehot[1][:, :, :, :],
                    at_f[:, PH:2 * PH, :].unsqueeze(2).broadcast_to([P, PH, TOPK, TOPK]),
                    ALU.mult).then_inc(s_step, s.up())
                dve.wait_ge(place_valued, t + 1)
                nc.vector.tensor_reduce(picks[:, 0, :, :], onehot[0][:, :, :, :], AX_X, ALU.add).then_inc(s_step, s.up())
                dve.wait_ge(s_step, now() - 1)
                nc.vector.tensor_reduce(picks[:, 1, :, :], onehot[1][:, :, :, :], AX_X, ALU.add).then_inc(s_step, s.up())
                dve.wait_ge(exp_done, t + 1)
                nc.vector.tensor_reduce(gsum[:, :], top_e[:, :, :], AX_X, ALU.add).then_inc(s_step, s.up())
                dve.wait_ge(s_step, now())
                nc.vector.reciprocal(gsum[:, :], gsum[:, :]).then_inc(s_step, s.up())
                dve.wait_ge(s_step, now())
                nc.vector.tensor_tensor(picks[:, 2, :, :], top_e[:, :, :], gsum[:, :].unsqueeze(2).broadcast_to([P, PH, TOPK]),
                                        ALU.mult).then_inc(picks_ready, 1)
                assert s.n == S_STEPS, s.n
                yield

            dve.wait_ge(consts_loaded, 80)
            nc.vector.tensor_scalar(subln[:, :], subln[:, :], 1.0 - LAM_INIT, None, ALU.mult).then_inc(subln_ready, 1)
            nc.vector.memset(eps[:, :], EPS).then_inc(subln_ready, 1)
            norm_mixed(0)
            add_residual(0)
            invert_norm(0)
            def turn_of(t):
                norm_mixed(t + 1)
                parts = iter((None, add_residual, invert_norm))
                for _ in selection(t, Steps()):
                    part = next(parts, None)
                    if part:
                        part(t + 1)

            turns(dve, TILES - 1, turn_of)
            for _ in selection(TILES - 1, Steps()):
                pass


E_GROUP = 8
RING = 4
HALF = P // 2
PIECES = NT // HALF
REST = NT % HALF


def spread_gates(nc, io, sems, bank, x2):
    with ExitStack() as ctx:
        def sb(name, shape, dt=F32):
            return ctx.enter_context(nc.sbuf_tensor(name, shape, dt))

        iota = sb("iota5", [P, P])
        picksT = sb("picks_T5", [P, 3, TP])
        row1 = [sb(f"onehot_i1_{r}", [P, E_GROUP, P]) for r in range(RING)]
        row2 = [sb(f"gated_i2_{r}", [P, E_GROUP, P]) for r in range(RING)]
        stage = [sb(f"stage{r}", [P, P * HALF]) for r in range(2)]

        gate = sb("gate5", [P, P // E_GROUP])

        picks_loaded = sems("picks_loaded")
        places_ready = sems("places_ready")
        plain_ready = sems("plain_ready")
        gated_ready = sems("gated_ready")
        rows_used = sems("rows_used")
        staged = sems("staged")
        stored = [sems(f"stage_stored{r}") for r in range(2)]
        x2_raw = sb("x2_raw", [P, NT])
        x_loaded = sems("x5_loaded")
        x_hi, x_lo = sems("x2_hi_ready"), sems("x2_lo_ready")
        PER_PIECE = HALF // E_GROUP
        PER_TURN = 2 * PER_PIECE
        assert PIECES // 2 == KD
        block = ctx.enter_context(nc.Block())

        def tiles(eng, body):
            turns(eng, PIECES // 2, lambda t: body(t, PER_TURN))
            body(PIECES // 2, REST // E_GROUP)

        @block.sync
        def _(sp):
            sp.dma_start(iota[:, :], io["iota"]).then_inc(picks_loaded, 16)
            sp.dma_start(picksT[:, :, :], io["picksT"]).then_inc(picks_loaded, 16)
            sp.dma_start(x2_raw[:, :], io["x2T"][0, :, 0:NT]).then_inc(x_loaded, 16)

            def load_x(t):
                sp.wait_ge(x_lo, t + 1)
                sp.dma_start(x2_raw[:, :], io["x2T"][ds(t + 1, 1), :, 0:NT].rearrange("a p t -> (a p) t")).then_inc(x_loaded, 16)

            def store(t):
                for r in range(2):
                    sp.wait_ge(staged, t * PER_TURN + (r + 1) * PER_PIECE)
                    sp.dma_start(io["gates"][:, ds(t * (2 * P * HALF) + r * (P * HALF), P * HALF)],
                                 stage[r][:, :]).then_inc(stored[r], 16)

            def turn_of(t):
                load_x(t)
                store(t)

            turns(sp, KD - 1, turn_of)
            store(KD - 1)
            sp.wait_ge(staged, PIECES * PER_PIECE + REST // E_GROUP)
            sp.dma_start(io["gates"][:, PIECES * P * HALF:], stage[0][:, 0:P * REST]).then_inc(stored[0], 16)
            sp.wait_ge(stored[0], 16 * (PIECES // 2 + 1))
            sp.wait_ge(stored[1], 16 * (PIECES // 2))

        @block.vector
        def _(dve):
            dve.wait_ge(picks_loaded, 32)
            def one_hots(t, groups):
                for g in range(groups):
                    since(dve, rows_used, t * PER_TURN + (g - RING + 1))
                    toks = ds(t * P + g * E_GROUP, E_GROUP)
                    nc.vector.memset(gate[:, g:g + 1], 0.0)
                    if g == 2 and groups == PER_TURN:
                        dve.wait_ge(x_hi, t + 1)
                        nc.vector.tensor_tensor(x2[1][:, ds(t, 1), :].rearrange("p a t -> p (a t)"), x2_raw[:, :],
                                                x2[0][:, ds(t, 1), :].rearrange("p a t -> p (a t)").bitcast(F32),
                                                ALU.subtract).then_inc(x_lo, 1)
                    for c, row, ready in ((1, row2, plain_ready), (0, row1, places_ready)):
                        nc.vector.tensor_tensor(row[g % RING][:, :, :], iota[:, :].unsqueeze(1).broadcast_to([P, E_GROUP, P]),
                                                picksT[:, c, toks].unsqueeze(2).broadcast_to([P, E_GROUP, P]),
                                                ALU.is_equal).then_inc(ready, 1)

            tiles(dve, one_hots)

        @block.gpsimd
        def _(pool):
            pool.wait_ge(picks_loaded, 32)
            def gated(t, groups):
                for g in range(groups):
                    pool.wait_ge(plain_ready, t * PER_TURN + (g + 1))
                    toks = ds(t * P + g * E_GROUP, E_GROUP)
                    nc.gpsimd.tensor_tensor(row2[g % RING][:, :, :], row2[g % RING][:, :, :],
                                            picksT[:, 2, toks].unsqueeze(2).broadcast_to([P, E_GROUP, P]),
                                            ALU.mult).then_inc(gated_ready, 1)

            tiles(pool, gated)

        @block.tensor
        def _(pe):
            def products(t, groups):
                for g in range(groups):
                    pe.wait_ge(places_ready, t * PER_TURN + (g + 1))
                    pe.wait_ge(gated_ready, t * PER_TURN + (g + 1))
                    since(pe, staged, t * PER_TURN + max(0, g - 3))
                    for j in range(E_GROUP):
                        ins = nc.tensor.matmul(bank[:, 2 * (g % 4) + j // 4, (j % 4) * P:(j % 4 + 1) * P],
                                               row1[g % RING][:, j, :], row2[g % RING][:, j, :], start=True, stop=True)
                    ins.then_inc(rows_used, 1)

            tiles(pe, products)

        @block.scalar
        def _(act):
            def take_products(t, groups):
                if groups == PER_TURN:
                    act.wait_ge(x_loaded, t * 16 + 16)
                    nc.scalar.copy(x2[0][:, ds(t, 1), :].rearrange("p a t -> p (a t)"), x2_raw[:, :]).then_inc(x_hi, 1)
                width = HALF if groups == PER_TURN else REST
                for g in range(groups):
                    r, at = g // PER_PIECE, g % PER_PIECE * E_GROUP
                    act.wait_ge(rows_used, t * PER_TURN + (g + 1))
                    if at == 0:
                        since(act, stored[r], t * 16)
                    src = bank[:, 2 * (g % 4):2 * (g % 4) + 2, :].rearrange("p b (t i) -> p i (b t)", i=P)
                    dst = stage[r][:, 0:P * width].rearrange("p (i t) -> p i t", i=P)
                    nc.scalar.copy(dst[:, :, at:at + E_GROUP], src).then_inc(staged, 1)

            tiles(act, take_products)


BLK = 2
SUPER = P // BLK
TC = 3
CH = NT // TC


def run_experts(nc, io, sems, bank, x2):
    with ExitStack() as ctx:
        def sb(name, shape, dt=F32):
            return ctx.enter_context(nc.sbuf_tensor(name, shape, dt))

        yT = sb("y_T", [P, KD, NT])
        u_raw = [sb(f"u_raw{j}", [P, KD * P]) for j in range(BLK)]
        u = [[sb(f"u_{part}{j}", [P, KD * P], F32R) for part in ("hi", "lo")] for j in range(BLK)]
        v_raw = [sb(f"v_raw{j}", [P, D]) for j in range(BLK)]
        v = [[sb(f"v_{part}{j}", [P, D], F32R) for part in ("hi", "lo")] for j in range(BLK)]
        g = [sb(f"gates{j}", [P, NT]) for j in range(BLK)]
        w = [sb(f"gelu{j}", [P, NT]) for j in range(BLK)]
        coef = [[[sb(f"coef_{part}{r}{j}", [P, NT], F32R) for part in ("hi", "lo")] for j in range(BLK)] for r in range(2)]

        u_loaded = [sems(f"u_loaded{j}") for j in range(BLK)]
        g_loaded = [sems(f"g_loaded{j}") for j in range(BLK)]
        v_loaded = [sems(f"v_loaded{j}") for j in range(BLK)]
        h_loaded = sems("h5_loaded")
        u_hi, u_lo = sems("u_hi_ready"), sems("u_lo_ready")
        v_hi, v_lo = sems("v_hi_ready"), sems("v_lo_ready")
        a_in_psum = sems("a_in_psum")
        gelu_done = sems("gelu_done")
        weighed = sems("weighed")
        coef_hi, coef_lo = sems("coef_hi_ready"), sems("coef_lo_ready")
        y_in_psum = sems("y_in_psum")
        y_added = sems("y_added")
        y_stored = sems("y_stored")
        window_moved = sems("window_moved")
        AN, YN = BLK * TC, KD * TC

        block = ctx.enter_context(nc.Block())

        def pipeline(eng, a_part, y_part):
            a_part(0, 0)
            a_part(1, 1)
            y_part(0, 0)
            with eng.Fori(1, SUPER // 2 - 1) as m:
                a_part(m * 2, 0)
                y_part(m * 2 - 1, 1)
                a_part(m * 2 + 1, 1)
                y_part(m * 2, 0)
            a_part(SUPER - 2, 0)
            y_part(SUPER - 3, 1)
            a_part(SUPER - 1, 1)
            y_part(SUPER - 2, 0)
            y_part(SUPER - 1, 1)

        @block.sync
        def _(sp):
            def load_gates(n, i):
                full = io["gates"][:, 0:PIECES * P * HALF].rearrange("p (q i t) -> p q (i t)", q=PIECES, i=P)
                sp.dma_start(g[n][:, 0:PIECES * HALF].rearrange("p (q t) -> p q t", q=PIECES),
                             full[:, :, ds(i * HALF, HALF)]).then_inc(g_loaded[n], 16)
                sp.dma_start(g[n][:, PIECES * HALF:], io["gates"][:, ds(i * REST + PIECES * P * HALF, REST)]).then_inc(g_loaded[n], 16)

            sp.dma_start(u_raw[0][:, :], io["u"][0, :, :]).then_inc(u_loaded[0], 16)
            sp.dma_start(v_raw[0][:, :], io["v"][:, 0, :]).then_inc(v_loaded[0], 16)
            sp.dma_start(v_raw[1][:, :], io["v"][:, 1, :]).then_inc(v_loaded[1], 16)
            load_gates(0, 0)
            sp.dma_start(yT[:, :, :], io["hT"][:, :, 0:NT].rearrange("k p t -> p k t")).then_inc(h_loaded, 16)

            def load(s, r):
                for j in range(BLK):
                    i, n = s * BLK + j, (j + 1) % BLK
                    if isinstance(s, int) and i == P - 1:
                        continue
                    since(sp, u_lo, i)
                    sp.dma_start(u_raw[n][:, :], io["u"][ds(i + 1, 1), :, :].rearrange("a p c -> (a p) c")).then_inc(u_loaded[n], 16)
                    since(sp, weighed, i)
                    load_gates(n, i + 1)

            def load_v(s, r):
                if isinstance(s, int) and s == SUPER - 1:
                    return
                for j in range(BLK):
                    sp.wait_ge(v_lo, s * BLK + (j + 1))
                    sp.dma_start(v_raw[j][:, :], io["v"][:, ds(s * BLK + (BLK + j), 1), :].rearrange("p a d -> p (a d)")).then_inc(v_loaded[j], 16)

            pipeline(sp, load, load_v)
            for k in range(KD):
                sp.wait_ge(y_added, SUPER * YN - (KD - 1 - k) * TC)
                sp.dma_start(io["yT"][k, :, :], yT[:, k, :]).then_inc(y_stored, 16)
            sp.wait_ge(y_stored, 16 * KD)

        @block.gpsimd
        def _(pool):
            move = (STATE - DQ) * SEG
            pool.wait_ge(h_loaded, 16)
            n = 0
            for state, out, new in (("state_k", "win_k_out", "kb"), ("state_v", "win_v_out", "vb")):
                src, dst = (io[x].rearrange("b s c -> b (s c)") for x in (state, out))
                pool.dma_start(dst[:, move:], io[new][SEQ:NT, :].rearrange("(b q) c -> b (q c)", q=DQ)).then_inc(window_moved, 16)
                for b in range(DB):
                    n += 1
                    pool.wait_ge(window_moved, 16 * n)
                    pool.dma_start(dst[b, 0:move].rearrange("(a c) -> a c", a=64),
                                   src[b, DQ * SEG:].rearrange("(a c) -> a c", a=64)).then_inc(window_moved, 16)
                n += 1
                pool.wait_ge(window_moved, 16 * n)

        @block.tensor
        def _(pe):
            def activations(s, r):
                for j in range(BLK):
                    pe.wait_ge(u_hi, s * BLK + (j + 1))
                    pe.wait_ge(u_lo, s * BLK + (j + 1))
                    for c in range(TC):
                        n = j * TC + c
                        since(pe, gelu_done, s * AN + (n - 3))
                        for k in range(KD):
                            for a, b in ((0, 0), (0, 1), (1, 0)):
                                ins = nc.tensor.matmul(bank[:, (AN * r + n) % 4, 0:CH], u[j][a][:, k * P:(k + 1) * P],
                                                       x2[b][:, k, c * CH:(c + 1) * CH], start=(k == 0 and a == b),
                                                       stop=(k == KD - 1 and a == 1))
                        ins.then_inc(a_in_psum, 1)

            def outputs(s, r):
                pe.wait_ge(coef_lo, s * BLK + BLK)
                pe.wait_ge(v_lo, s * BLK + BLK)
                for n in range(YN):
                    k, c = n // TC, n % TC
                    since(pe, y_added, s * YN + (n - 3))
                    for j in range(BLK):
                        for a, b in ((0, 0), (0, 1), (1, 0)):
                            ins = nc.tensor.matmul(bank[:, 4 + n % 4, 0:CH], v[j][a][:, k * P:(k + 1) * P],
                                                   coef[r][j][b][:, c * CH:(c + 1) * CH], start=(j == 0 and a == b),
                                                   stop=(j == BLK - 1 and a == 1))
                    ins.then_inc(y_in_psum, 1)

            pipeline(pe, activations, outputs)

        @block.scalar
        def _(act):
            def split_u(i, j):
                act.wait_ge(u_loaded[j], 8 * i + (16 - 8 * j))
                since(act, a_in_psum, (i - 1) * TC)
                nc.scalar.copy(u[j][0][:, :], u_raw[j][:, :]).then_inc(u_hi, 1)

            def split_v(s):
                for j in range(BLK):
                    act.wait_ge(v_loaded[j], s * 16 + 16)
                    since(act, y_in_psum, s * YN)
                    nc.scalar.copy(v[j][0][:, :], v_raw[j][:, :]).then_inc(v_hi, 1)

            def gelus(s, r):
                if not (isinstance(s, int) and s == 0):
                    split_v(s - 1)
                for j in range(BLK):
                    i = s * BLK + j
                    if not (isinstance(s, int) and i == P - 1):
                        split_u(i + 1, (j + 1) % BLK)
                    since(act, coef_lo, i - 1)
                    for c in range(TC):
                        n = j * TC + c
                        act.wait_ge(a_in_psum, s * AN + (n + 1))
                        nc.scalar.activation(w[j][:, c * CH:(c + 1) * CH], bank[:, (AN * r + n) % 4, 0:CH], ACT.Gelu).then_inc(gelu_done, 1)

            split_u(0, 0)
            pipeline(act, gelus, lambda s, r: None)
            split_v(SUPER - 1)

        @block.vector
        def _(dve):
            def rest(out, raw, hi, ready):
                nc.vector.tensor_tensor(out, raw, hi.bitcast(F32), ALU.subtract).then_inc(ready, 1)

            def split_u(i, j):
                dve.wait_ge(u_hi, i + 1)
                rest(u[j][1][:, :], u_raw[j][:, :], u[j][0][:, :], u_lo)

            def split_v(s):
                for j in range(BLK):
                    dve.wait_ge(v_hi, s * BLK + (j + 1))
                    rest(v[j][1][:, :], v_raw[j][:, :], v[j][0][:, :], v_lo)

            def coef_rest(i, r, j):
                dve.wait_ge(coef_hi, i + 1)
                rest(coef[r][j][1][:, :], w[j][:, :], coef[r][j][0][:, :], coef_lo)

            def weigh(s, r):
                if not (isinstance(s, int) and s == 0):
                    split_v(s - 1)
                for j in range(BLK):
                    i = s * BLK + j
                    if not (isinstance(s, int) and i == P - 1):
                        split_u(i + 1, (j + 1) % BLK)
                    dve.wait_ge(gelu_done, s * AN + (j + 1) * TC)
                    dve.wait_ge(g_loaded[j], s * 32 + 32)
                    nc.vector.tensor_tensor(w[j][:, :], w[j][:, :], g[j][:, :], ALU.mult).then_inc(weighed, 1)
                    dve.wait_ge(weighed, i + 1)
                    since(dve, y_in_psum, s * YN - YN)
                    nc.vector.tensor_copy(coef[r][j][0][:, :], w[j][:, :]).then_inc(coef_hi, 1)
                    if j < BLK - 1 or (isinstance(s, int) and s == 0):
                        coef_rest(i, r, j)

            def add(s, r):
                since(dve, y_added, s * YN)
                for n in range(YN):
                    k, c = n // TC, n % TC
                    dve.wait_ge(y_in_psum, s * YN + (n + 1))
                    out = yT[:, k, c * CH:(c + 1) * CH]
                    nc.vector.tensor_tensor(out, out, bank[:, 4 + n % 4, 0:CH], ALU.add).then_inc(y_added, 1)
                    if n == 2 and not (isinstance(s, int) and s == SUPER - 1):
                        coef_rest(s * BLK + (2 * BLK - 1), 1 - r, BLK - 1)

            def add_last(s, r):
                if isinstance(s, int) and s == SUPER - 1:
                    split_v(s)
                add(s, r)

            split_u(0, 0)
            dve.wait_ge(h_loaded, 16)
            pipeline(dve, weigh, add_last)


def build(nc, io, phases=9):
    with ExitStack() as ctx:
        bank = ctx.enter_context(nc.psum_tensor("banks", [P, 8, 512], F32))
        ident = ctx.enter_context(nc.sbuf_tensor("ident", [P, P], F32))[:, :]
        neg_lam = ctx.enter_context(nc.sbuf_tensor("neg_lambda", [P, 1], F32))[:, :]

        def phase(run, *args):
            own = []

            def sems(name):
                own.append(nc.alloc_semaphore(name=name))
                return own[-1]

            run(nc, io, sems, *args)
            nc.clear_and_free_semaphores(own)
            nc.all_engine_barrier()

        phase(load_constants, ident)
        phase(project, ident, bank)
        if phases >= 2:
            phase(lambda_column, neg_lam)
            phase(attend_prompt, ident, bank, neg_lam, "a")
            phase(attend_prompt, ident, bank, neg_lam, "b")
        if phases >= 3:
            phase(attend_sample, ident, bank, neg_lam, "a")
            phase(attend_sample, ident, bank, neg_lam, "b")
        if phases >= 4:
            phase(mix_and_route, ident, bank)
            with ExitStack() as later:
                x2 = [later.enter_context(nc.sbuf_tensor(f"x2_{part}", [P, KD, NT], F32R)) for part in ("hi", "lo")]
                phase(spread_gates, bank, x2)
                if phases >= 5:
                    phase(run_experts, bank, x2)


def slopes(n):
    return 2.0 ** (-8.0 * np.arange(1, n + 1) / n)


def log_branches(d):
    count = sum(((d >= 0) & (d <= w) & (d % dil == 0)).astype(np.int64) for w, dil in DILATIONS)
    return np.where(count > 0, np.log(np.maximum(count, 1).astype(np.float64)), NEG)


def shape_constants():
    d = np.arange(P)[:, None] + (SEQ - P) - np.arange(SEQ)[None, :]
    strips = [np.where(d >= 0, -s * d, NEG) for s in slopes(4)]
    strips += [np.where(log_branches(d) > NEG / 2, log_branches(d) - s * d, NEG) for s in slopes(8)]
    used = np.arange(P).reshape(4, PR)[:, 0:2 * DQ].ravel()
    row_q = np.tile(np.arange(DQ), 8)
    new = np.arange(DQ)
    bias_a, bias_b = np.zeros((P, PAST + DQ)), np.zeros((P, len(state_rows()) + DQ))
    pos_a = np.concatenate([np.arange(PAST), PAST + new])
    da = PAST + row_q[:, None] - pos_a[None, :]
    bias_a[used] = np.where(da >= 0, -np.repeat(slopes(4), 8)[:, None] * da, NEG)
    pos_b = np.concatenate([state_rows(), STATE + new])
    db = STATE + row_q[:, None] - pos_b[None, :]
    bias_b[used] = np.where(log_branches(db) > NEG / 2, log_branches(db) - np.repeat(slopes(8), DQ)[:, None] * db, NEG)
    sel_a = np.zeros((P, 4, DQ))
    sel_b = np.zeros((P, 8, DQ))
    second_map = np.zeros((P, 1))
    for i, r in enumerate(used):
        sel_a[r, i // 8, i % DQ] = 1
        sel_b[r, i // DQ, i % DQ] = 1
        second_map[r] = i // DQ % 2
    out = {"ident": np.eye(P), "strips": np.stack(strips), "bias_a": bias_a, "bias_b": bias_b,
           "sel_a": sel_a, "sel_b": sel_b, "second_map": second_map,
           "iota": np.broadcast_to(np.arange(P), (P, P))}
    return {k: np.ascontiguousarray(v, dtype=np.float32) for k, v in out.items()}


def state_rows():
    far = STATE - DILATIONS[1][0]
    step = DILATIONS[2][1]
    return np.concatenate([(np.arange(0, far, step)[:, None] + np.arange(DQ)[None, :]).ravel(),
                           np.arange(far, STATE)])


def lay_out(inp):
    a = {k: np.asarray(v) for k, v in inp.items()}
    c = np.ascontiguousarray
    n_phys = a["cache_a_k"].shape[1]
    x = np.zeros((TP, D), np.float32)
    x[0:SEQ] = a["x_prompt"].reshape(SEQ, D)
    x[SEQ:NT] = a["x_sample"].reshape(NS, D)
    rows = state_rows()
    tiles_b = len(rows) // P
    kb = a["state_b_k"][0][:, rows].reshape(DB, tiles_b, P, 4, P)
    vb = a["state_b_v"][0][:, rows].reshape(DB, tiles_b, P, SEG)
    m = {
        "x": x,
        "g1": c(a["norm1_g"].reshape(KD, P).T), "g2": c(a["norm2_g"].reshape(KD, P).T),
        "w_in": a["w_in"][0], "w_out": a["w_out"][0], "w_q": a["peer_wq"][0],
        "qk_gain": np.concatenate([a["qnorm_a"], a["knorm_a"], a["qnorm_b"], a["knorm_b"]]),
        "lams": np.concatenate([a["lambda_q1"], a["lambda_k1"], a["lambda_q2"], a["lambda_k2"]]),
        "subln": c(a["subln_g"].reshape(P, 1)),
        "cache_k": c(a["cache_a_k"][0].reshape(n_phys, P, 4, P).transpose(0, 3, 2, 1)).reshape(n_phys, P, SEG),
        "cache_v": a["cache_a_v"][0].reshape(n_phys, P, SEG),
        "page_table": a["page_table"].reshape(1, -1),
        "win_k": c(kb.transpose(0, 4, 1, 3, 2)).reshape(DB, P, tiles_b * SEG),
        "win_v": c(vb.transpose(0, 2, 1, 3)).reshape(DB, P, tiles_b * SEG),
        "state_k": a["state_b_k"].reshape(DB, STATE, SEG), "state_v": a["state_b_v"].reshape(DB, STATE, SEG),
        "sub_keys": c(a["peer_subkeys"][0].transpose(1, 3, 0, 2)).reshape(P, 8, P),
        "u": c(a["peer_u"][0].reshape(P, P, KD, P).transpose(1, 3, 2, 0)).reshape(P, P, KD * P),
        "v": a["peer_v"][0].reshape(P, P, D),
    }
    m.update(shape_constants())
    return m


OUTS = {"ka": (TP, SEG), "va": (TP, SEG), "kb": (TP, SEG), "vb": (TP, SEG),
        "win_k_out": (DB, STATE, SEG), "win_v_out": (DB, STATE, SEG), "yT": (KD, P, NT)}
SCRATCH = {"qkT": (16, P, TP), "mix": (TP, D), "picksT": (P, 3, TP), "gates": (P, P * NT), "hT": (KD, P, TP), "x2T": (KD, P, TP)}


def kernel(**inputs):
    import concourse.bacc as bacc
    from concourse.bass_utils import run_bass_kernel_spmd as run

    nc = bacc.Bacc("TRN2", target_bir_lowering=False, num_devices=1)
    arrays = lay_out(inputs)
    io = {}
    for name, arr in arrays.items():
        io[name] = nc.dram_tensor(f"in_{name}", arr.shape, mybir.dt.from_np(arr.dtype), kind="ExternalInput").ap()
    for name, shape in OUTS.items():
        io[name] = nc.dram_tensor(f"out_{name}", shape, F32, kind="ExternalOutput").ap()
    for name, shape in SCRATCH.items():
        io[name] = nc.dram_tensor(f"scratch_{name}", shape, F32).ap()
    build(nc, io)
    got = run(nc, [{f"in_{k}": v for k, v in arrays.items()}], core_ids=[0]).results[0]
    o = {name: np.asarray(got[f"out_{name}"]) for name in OUTS}
    y = o["yT"].reshape(D, NT).T
    new = lambda name, width: (o[name][:SEQ].reshape(1, 1, SEQ, -1, width),
                               o[name][SEQ:NT].reshape(1, DB, DQ, -1, width))
    (kap, kas), (vap, vas) = new("ka", P), new("va", P)
    (kbp, _), (vbp, _) = new("kb", HD), new("vb", HD)
    window = (1, DB, STATE, 8, HD)
    return (y[:SEQ].reshape(1, SEQ, D), y[SEQ:].reshape(DB, DQ, D), kap, vap, kas, vas,
            kbp, vbp, o["win_k_out"].reshape(window), o["win_v_out"].reshape(window))
```
